# Optimizing a Trainium2 kernel written in Bass

```python
import math
import jax, jax.numpy as jnp
from jax import lax
import numpy as np

D_MODEL = 2048
BATCH = 1
SEQ = 256
DEPTH = 1

MEM_LEN = 256
EPS = 1e-6
NEG_INF = -1e30
ROPE_THETA = 500000.0
Q_BLOCK = 128
DA_HEADS = 8
DA_DK = 64
DA_DV = 2 * DA_DK
NSA_HEADS = 16
NSA_GROUPS = 4
NSA_HPG = NSA_HEADS // NSA_GROUPS
NSA_DK = 64
CMP_LEN = 32
CMP_STRIDE = 16
CMP_HIDDEN = 128
SEL_LEN = 64
SEL_TOPK = 16
WINDOW = 512
FORCE_BONUS = 100.0
ROPE_DIM = DA_DK // 4
X_HEADS = 4
X_DH = 128
PEER_HEADS = 8
PEER_NKEYS = 128
PEER_EXPERTS = PEER_NKEYS * PEER_NKEYS
PEER_DQ = 256
PEER_TOPK = 16
PEER_CHUNK = 128
SPLIT_SIZES = (DA_HEADS * 2 * DA_DK, DA_HEADS * 2 * DA_DK, DA_HEADS * DA_DV,
               NSA_HEADS * NSA_DK, 6 * NSA_GROUPS * NSA_DK, NSA_HEADS * 3, 2 * D_MODEL)
IN_COLS = sum(SPLIT_SIZES)
SPLIT_POINTS = [int(o) for o in np.cumsum(SPLIT_SIZES)[:-1]]

kernel_name = 'hybrid_diffattn_nsa_peer_block'

def rms_norm(x, g):
    xf = x.astype(jnp.float32)
    y = xf * lax.rsqrt(jnp.mean(xf * xf, axis=-1, keepdims=True) + EPS)
    return (y * g.astype(jnp.float32)).astype(x.dtype)

def rope_tables(positions, dtype):
    inv = ROPE_THETA ** (-jnp.arange(0, ROPE_DIM, 2, dtype=jnp.float32) / ROPE_DIM)
    ang = positions.astype(jnp.float32)[..., None] * inv
    return jnp.cos(ang).astype(dtype), jnp.sin(ang).astype(dtype)

def partial_rope(x, cos, sin):
    half = ROPE_DIM // 2
    shp = cos.shape[:2] + (1,) * (x.ndim - 3) + (half,)
    c = cos.reshape(shp)
    s = sin.reshape(shp)
    x1 = x[..., :half]
    x2 = x[..., half:ROPE_DIM]
    return jnp.concatenate([x1 * c - x2 * s, x2 * c + x1 * s, x[..., ROPE_DIM:]], axis=-1)

def masked_softmax(s, mask):
    s32 = jnp.where(mask, s.astype(jnp.float32), NEG_INF)
    return jax.nn.softmax(s32, axis=-1) * mask

def diff_attention(q, k, v, lam, lambda_init, subln_g):
    B, S = q.shape[:2]
    scale = DA_DK ** -0.5
    kpos = jnp.arange(S)

    def block(c):
        q0 = c * Q_BLOCK
        qb = lax.dynamic_slice_in_dim(q, q0, Q_BLOCK, axis=1)
        t = q0 + jnp.arange(Q_BLOCK)
        s = jnp.einsum('bqhmd,bkhmd->bhmqk', qb, k) * scale
        mask = kpos[None, :] <= t[:, None]
        p = masked_softmax(s, mask)
        a = p[:, :, 0] - lam * p[:, :, 1]
        return jnp.einsum('bhqk,bkhd->bqhd', a.astype(v.dtype), v)

    o = lax.map(block, jnp.arange(S // Q_BLOCK))
    o = jnp.moveaxis(o, 0, 1).reshape(B, S, DA_HEADS, DA_DV)
    o = rms_norm(o, subln_g) * (1.0 - lambda_init)
    return o.reshape(B, S, DA_HEADS * DA_DV)

def compress(xs, pos_emb, w1, w2):
    S = xs.shape[1]
    n_cmp = (S - CMP_LEN) // CMP_STRIDE + 1
    idx = jnp.arange(n_cmp)[:, None] * CMP_STRIDE + jnp.arange(CMP_LEN)[None, :]
    blk = xs[:, idx] + pos_emb[None, None, :, None, :]
    hid = jax.nn.gelu(jnp.einsum('bnlgd,ldh->bngh', blk, w1.reshape(CMP_LEN, NSA_DK, CMP_HIDDEN)), approximate=False)
    return jnp.einsum('bngh,hd->bngd', hid, w2)

def nsa_attention(q, kv, gate_logits, cos, sin, cmp_pos, ck1, ck2, cv1, cv2):
    B, S = q.shape[:2]
    G = NSA_GROUPS
    q = partial_rope(q, cos, sin).reshape(B, S, G, NSA_HPG, NSA_DK)
    k_cmp = partial_rope(kv[:, :, 0], cos, sin)
    v_cmp = kv[:, :, 1]
    k_sel = partial_rope(kv[:, :, 2], cos, sin)
    v_sel = kv[:, :, 3]
    k_win = partial_rope(kv[:, :, 4], cos, sin)
    v_win = kv[:, :, 5]
    gates = jax.nn.sigmoid(gate_logits)

    n_cmp = (S - CMP_LEN) // CMP_STRIDE + 1
    n_sel = S // SEL_LEN
    topk = min(SEL_TOPK, n_sel)
    per_sel = SEL_LEN // CMP_STRIDE
    pad = n_sel * per_sel - n_cmp
    kc = compress(k_cmp, cmp_pos, ck1, ck2)
    vc = compress(v_cmp, cmp_pos, cv1, cv2)
    cmp_end = jnp.arange(n_cmp) * CMP_STRIDE + CMP_LEN - 1
    blk_ids = jnp.arange(n_sel)
    sel_start = blk_ids * SEL_LEN

    def to_blocks(a):
        return a.reshape(B, n_sel, SEL_LEN, G, NSA_DK).transpose(0, 3, 1, 2, 4)

    ks_blk = to_blocks(k_sel)
    vs_blk = to_blocks(v_sel)
    kw_pad = jnp.pad(k_win, ((0, 0), (WINDOW, 0), (0, 0), (0, 0)))
    vw_pad = jnp.pad(v_win, ((0, 0), (WINDOW, 0), (0, 0), (0, 0)))
    b_idx = jnp.arange(B)[:, None, None, None]
    g_idx = jnp.arange(G)[None, None, :, None]
    scale = NSA_DK ** -0.5

    def block(c):
        q0 = c * Q_BLOCK
        t = q0 + jnp.arange(Q_BLOCK)
        qb = lax.dynamic_slice_in_dim(q, q0, Q_BLOCK, axis=1)
        gb = lax.dynamic_slice_in_dim(gates, q0, Q_BLOCK, axis=1)
        s_c = jnp.einsum('bqghd,bngd->bqghn', qb, kc) * scale
        m_c = (cmp_end[None, :] <= t[:, None])[None, :, None, None, :]
        p_c = masked_softmax(s_c, m_c)
        o_c = jnp.einsum('bqghn,bngd->bqghd', p_c.astype(qb.dtype), vc)
        imp = jnp.pad(p_c.sum(axis=3), ((0, 0), (0, 0), (0, 0), (0, pad)))
        imp = imp.reshape(B, Q_BLOCK, G, n_sel, per_sel).sum(-1)
        elig = sel_start[None, :] <= t[:, None]
        cur = (t // SEL_LEN)[:, None]
        forced = (blk_ids[None, :] == 0) | (blk_ids[None, :] == cur) | (blk_ids[None, :] == cur - 1)
        bonus = jnp.where(forced, FORCE_BONUS, 0.0)
        score = jnp.where(elig[None, :, None, :], imp + bonus[None, :, None, :], -1.0)
        _, idx = lax.top_k(score, topk)
        valid = jnp.take_along_axis(jnp.broadcast_to(elig[None, :, None, :], score.shape), idx, axis=-1)
        k_g = ks_blk[b_idx, g_idx, idx].reshape(B, Q_BLOCK, G, topk * SEL_LEN, NSA_DK)
        v_g = vs_blk[b_idx, g_idx, idx].reshape(B, Q_BLOCK, G, topk * SEL_LEN, NSA_DK)
        tok = idx[..., None] * SEL_LEN + jnp.arange(SEL_LEN)
        m_s = ((tok <= t[None, :, None, None, None]) & valid[..., None]).reshape(B, Q_BLOCK, G, 1, topk * SEL_LEN)
        s_s = jnp.einsum('bqghd,bqgkd->bqghk', qb, k_g) * scale
        o_s = jnp.einsum('bqghk,bqgkd->bqghd', masked_softmax(s_s, m_s).astype(qb.dtype), v_g)
        kw = lax.dynamic_slice_in_dim(kw_pad, q0, Q_BLOCK + WINDOW, axis=1)
        vw = lax.dynamic_slice_in_dim(vw_pad, q0, Q_BLOCK + WINDOW, axis=1)
        kpos = q0 - WINDOW + jnp.arange(Q_BLOCK + WINDOW)
        dist = t[:, None] - kpos[None, :]
        m_w = ((dist >= 0) & (dist < WINDOW) & (kpos[None, :] >= 0))[None, :, None, None, :]
        s_w = jnp.einsum('bqghd,bkgd->bqghk', qb, kw) * scale
        o_w = jnp.einsum('bqghk,bkgd->bqghd', masked_softmax(s_w, m_w).astype(qb.dtype), vw)
        o = gb[..., 0:1] * o_c + gb[..., 1:2] * o_s + gb[..., 2:3] * o_w
        return o.reshape(B, Q_BLOCK, NSA_HEADS * NSA_DK)

    o = lax.map(block, jnp.arange(S // Q_BLOCK))
    return jnp.moveaxis(o, 0, 1).reshape(B, S, NSA_HEADS * NSA_DK)

def memory_cross_attention(hn, memn, wq, wkv, wo):
    B, S, _ = hn.shape
    M = memn.shape[1]
    q = (hn @ wq).reshape(B, S, X_HEADS, X_DH)
    kv = (memn @ wkv).reshape(B, M, 2, X_HEADS, X_DH)
    s = jnp.einsum('bshd,bmhd->bhsm', q, kv[:, :, 0]) * (X_DH ** -0.5)
    p = jax.nn.softmax(s.astype(jnp.float32), axis=-1).astype(hn.dtype)
    o = jnp.einsum('bhsm,bmhd->bshd', p, kv[:, :, 1])
    return o.reshape(B, S, X_HEADS * X_DH) @ wo

def peer_ffn(xn, wq, keys1, keys2, U, V):
    B, S, D = xn.shape
    C = PEER_CHUNK
    K = PEER_TOPK
    half = PEER_DQ // 2

    def chunk(c):
        xc = lax.dynamic_slice_in_dim(xn, c * C, C, axis=1)
        q = (xc @ wq).reshape(B, C, PEER_HEADS, PEER_DQ)
        s1 = jnp.einsum('bchd,nd->bchn', q[..., :half], keys1).astype(jnp.float32)
        s2 = jnp.einsum('bchd,nd->bchn', q[..., half:], keys2).astype(jnp.float32)
        v1, i1 = lax.top_k(s1, K)
        v2, i2 = lax.top_k(s2, K)
        cand = (v1[..., :, None] + v2[..., None, :]).reshape(B, C, PEER_HEADS, K * K)
        sc, ci = lax.top_k(cand, K)
        e = jnp.take_along_axis(i1, ci // K, axis=-1) * PEER_NKEYS + jnp.take_along_axis(i2, ci % K, axis=-1)
        g = jax.nn.softmax(sc, axis=-1).astype(xc.dtype)
        a = jax.nn.gelu(jnp.einsum('bchkd,bcd->bchk', U[e], xc), approximate=False)
        return jnp.einsum('bchk,bchkd->bcd', g * a, V[e])

    o = lax.map(chunk, jnp.arange(S // C))
    return jnp.moveaxis(o, 0, 1).reshape(B, S, D)

def setup_inputs(seed: int = 0) -> dict:
    key = jax.random.key(seed)
    ks = iter(jax.random.split(key, 40))

    def nrm(shape, scale):
        return jax.random.normal(next(ks), shape, jnp.float32) * scale

    def gain(shape):
        return 1.0 + nrm(shape, 0.02)

    L = DEPTH
    D = D_MODEL
    x = nrm((BATCH, SEQ, D), 1.0)
    mem = nrm((BATCH, MEM_LEN, D), 1.0)
    off = jax.random.randint(next(ks), (BATCH,), 0, 1024)
    positions = (jnp.arange(SEQ, dtype=jnp.int32)[None, :] + off[:, None]).astype(jnp.int32)
    return {
        'x': x,
        'mem': mem,
        'positions': positions,
        'norm_mix_g': gain((L, D)),
        'w_in': nrm((L, D, IN_COLS), D ** -0.5),
        'da_lambda_q1': nrm((L, DA_DK), 0.1),
        'da_lambda_k1': nrm((L, DA_DK), 0.1),
        'da_lambda_q2': nrm((L, DA_DK), 0.1),
        'da_lambda_k2': nrm((L, DA_DK), 0.1),
        'da_subln_g': gain((L, DA_DV)),
        'nsa_cmp_pos': nrm((L, CMP_LEN, NSA_DK), 0.02),
        'nsa_cmpk_w1': nrm((L, CMP_LEN * NSA_DK, CMP_HIDDEN), (CMP_LEN * NSA_DK) ** -0.5),
        'nsa_cmpk_w2': nrm((L, CMP_HIDDEN, NSA_DK), CMP_HIDDEN ** -0.5),
        'nsa_cmpv_w1': nrm((L, CMP_LEN * NSA_DK, CMP_HIDDEN), (CMP_LEN * NSA_DK) ** -0.5),
        'nsa_cmpv_w2': nrm((L, CMP_HIDDEN, NSA_DK), CMP_HIDDEN ** -0.5),
        'w_branch_da': nrm((L, DA_HEADS * DA_DV, D), (DA_HEADS * DA_DV) ** -0.5),
        'w_branch_nsa': nrm((L, NSA_HEADS * NSA_DK, D), (NSA_HEADS * NSA_DK) ** -0.5),
        'w_out': nrm((L, D, D), D ** -0.5),
        'norm_x_g': gain((L, D)),
        'norm_mem_g': gain((L, D)),
        'w_xq': nrm((L, D, X_HEADS * X_DH), D ** -0.5),
        'w_xkv': nrm((L, D, 2 * X_HEADS * X_DH), D ** -0.5),
        'w_xo': nrm((L, X_HEADS * X_DH, D), (X_HEADS * X_DH) ** -0.5),
        'norm_ffn_g': gain((L, D)),
        'peer_wq': nrm((L, D, PEER_HEADS * PEER_DQ), D ** -0.5),
        'peer_keys1': nrm((L, PEER_NKEYS, PEER_DQ // 2), (PEER_DQ // 2) ** -0.5),
        'peer_keys2': nrm((L, PEER_NKEYS, PEER_DQ // 2), (PEER_DQ // 2) ** -0.5),
        'peer_u': nrm((L, PEER_EXPERTS, D), D ** -0.5),
        'peer_v': nrm((L, PEER_EXPERTS, D), 0.5),
        'norm_final_g': gain((D,)),
    }

def reference(x, mem, positions, norm_mix_g, w_in, da_lambda_q1, da_lambda_k1, da_lambda_q2, da_lambda_k2,
              da_subln_g, nsa_cmp_pos, nsa_cmpk_w1, nsa_cmpk_w2, nsa_cmpv_w1, nsa_cmpv_w2, w_branch_da,
              w_branch_nsa, w_out, norm_x_g, norm_mem_g, w_xq, w_xkv, w_xo, norm_ffn_g, peer_wq, peer_keys1,
              peer_keys2, peer_u, peer_v, norm_final_g):
    B, S, _ = x.shape
    cos, sin = rope_tables(positions, x.dtype)
    h = x
    for l in range(DEPTH):
        xn = rms_norm(h, norm_mix_g[l])
        z = xn @ w_in[l]
        zq, zk, zv, nq, nkv, ng, bg = jnp.split(z, SPLIT_POINTS, axis=-1)
        dq = partial_rope(zq.reshape(B, S, DA_HEADS, 2, DA_DK), cos, sin)
        dk = partial_rope(zk.reshape(B, S, DA_HEADS, 2, DA_DK), cos, sin)
        dv = zv.reshape(B, S, DA_HEADS, DA_DV)
        lambda_init = 0.8 - 0.6 * math.exp(-0.3 * l)
        lam = (jnp.exp(jnp.sum((da_lambda_q1[l] * da_lambda_k1[l]).astype(jnp.float32)))
               - jnp.exp(jnp.sum((da_lambda_q2[l] * da_lambda_k2[l]).astype(jnp.float32))) + lambda_init)
        o_da = diff_attention(dq, dk, dv, lam, lambda_init, da_subln_g[l])
        o_nsa = nsa_attention(nq.reshape(B, S, NSA_HEADS, NSA_DK),
                              nkv.reshape(B, S, 6, NSA_GROUPS, NSA_DK),
                              ng.reshape(B, S, NSA_GROUPS, NSA_HPG, 3), cos, sin,
                              nsa_cmp_pos[l], nsa_cmpk_w1[l], nsa_cmpk_w2[l], nsa_cmpv_w1[l], nsa_cmpv_w2[l])
        gates = jax.nn.sigmoid(bg.reshape(B, S, 2, D_MODEL))
        mix = gates[:, :, 0] * (o_da @ w_branch_da[l]) + gates[:, :, 1] * (o_nsa @ w_branch_nsa[l])
        h = h + mix @ w_out[l]
        h = h + memory_cross_attention(rms_norm(h, norm_x_g[l]), rms_norm(mem, norm_mem_g[l]),
                                       w_xq[l], w_xkv[l], w_xo[l])
        h = h + peer_ffn(rms_norm(h, norm_ffn_g[l]), peer_wq[l], peer_keys1[l], peer_keys2[l],
                         peer_u[l], peer_v[l])
    return rms_norm(h, norm_final_g)


_drawn_inputs = setup_inputs


def setup_inputs(seed=0):
    import zlib

    import numpy as np

    out = dict(_drawn_inputs(seed))
    spreads = {}
    factors = {'da_lambda_q1': 44.679,
     'nsa_cmp_pos': 4.067,
     'norm_x_g': 4.752,
     'norm_mem_g': 4.063,
     'norm_final_g': 8.132,
     'norm_ffn_g': 6.017}
    for name, (base, spread) in spreads.items():
        noise = np.random.default_rng([zlib.crc32(name.encode()), seed]).standard_normal(out[name].shape)
        drawn = base * np.exp(spread * noise) if base else spread * noise
        out[name] = __import__('jax').numpy.asarray(drawn.astype(out[name].dtype))
    for name, factor in factors.items():
        out[name] = (out[name] * factor).astype(out[name].dtype)
    return out
```

```python
import math
from contextlib import ExitStack

import numpy as np
import concourse.bass as bass
from concourse import mybir

F32 = mybir.dt.float32
U32 = mybir.dt.uint32
I32 = mybir.dt.int32
ALU = mybir.AluOpType
ACT = mybir.ActivationFunctionType
AX = mybir.AxisListType

P = 128
D = 2048
S = 256
C = S // P
KT = D // P
NW = 512
SLOTS = 4
KS = KT // SLOTS
EPS = 1e-6
NEG = -1e30

DA_H, DA_DK, DA_DV = 8, 64, 128
N_H, N_G, N_DK = 16, 4, 64
ZQ, ZK, ZV, NQ, NKV = 0, 1024, 2048, 3072, 4096
QKV_COLS = NKV + 6 * N_G * N_DK
NG_COLS = N_H * 3
BG = QKV_COLS + NG_COLS
K_CMP, V_CMP, K_SEL, V_SEL, K_WIN, V_WIN = (NKV + 256 * n for n in range(6))
ATT_SCALE = DA_DK ** -0.5
LAMBDA_INIT = 0.8 - 0.6 * math.exp(-0.3 * 0)
ROPE_HALF = 8
ROPE_INV = [float(np.float32(500000.0) ** np.float32(-2 * i / 16)) for i in range(ROPE_HALF)]

CMP_LEN, CMP_STRIDE = 32, 16
N_CMP = (S - CMP_LEN) // CMP_STRIDE + 1
X_H, X_DH = 4, 128
X_SCALE = X_DH ** -0.5

PH, PK, NKEYS = 8, 16, 128
UNITS = PH * C

T_KV, T_QKV, T_BG, T_BR, T_WO, T_XQ, T_XO, T_PQ = 0, 2, 13, 21, 25, 29, 30, 31
N_QKV, N_BG, N_BR, N_WO, N_PQ = 11, 8, 4, 4, 4
A_PQ = T_PQ + 3

G_GAIN, G_POS, G_MEM, G_MK, G_X, G_CMP, G_ATT = 0, 1, 2, 10, 12, 20, 24
G_OT, G_MIX, G_X2, G_QX, G_OX, G_X3, G_PQ = 64, 72, 80, 88, 90, 92, 100
ATT_GROUPS = 10

ATT_STEPS, ROUTE_STEPS = 56, 21

LAG = 2
RING = 4

MAGIC = 12582912.0
TWO_PI_A = 6.28125
TWO_PI_B = float(np.float32(2 * math.pi - TWO_PI_A))
TWO_PI_C = float(2 * math.pi - TWO_PI_A - TWO_PI_B)
PI_IN = 3.1415925


class Chain:

    def __init__(self, eng, sem):
        self.eng, self.sem, self.n, self.var, self.per = eng, sem, 0, None, 0

    def __call__(self, ins):
        self.n += 1
        ins.then_inc(self.sem, 1)
        self.eng.wait_ge(self.sem, self.n if self.var is None else self.var * self.per + self.n)

    def loop(self, var, per):
        self.var, self.per, self.first = var, per, self.n

    def end(self, trips):
        assert self.n - self.first == self.per, (self.n - self.first, self.per)
        self.n += self.per * (trips - 1)
        self.var = None


def block_program(nc, x, mem, positions, norm_mix_g, w_in, lq1, lk1, lq2, lk2, subln_g, cmp_pos, ck1, ck2,
                  cv1, cv2, w_bda, w_bnsa, w_out, norm_x_g, norm_mem_g, w_xq, w_xkv, w_xo, norm_ffn_g,
                  peer_wq, keys1, keys2, peer_u, peer_v, norm_final_g, out):
    ctx = ExitStack()
    with ctx:
        def sb(name, shape, dt=F32):
            return ctx.enter_context(nc.sbuf_tensor(name, shape, dt))

        def sem(name):
            return ctx.enter_context(nc.semaphore(name))

        h = sb("h", [P, C, D])
        xT = sb("xT", [P, KT, S])
        oT = sb("oT", [P, KT, S])
        xn3 = oT[:, :, :].rearrange("p k s -> p (k s)").rearrange("p (c d) -> p c d", c=C)
        w = sb("w", [P, SLOTS, KS, NW])
        gfin = w[:, 0, :, :].rearrange("p k n -> p (k n)")
        big = sb("big", [P, C * QKV_COLS + C * 2 * D])
        z = big[:, 0:C * QKV_COLS].rearrange("p (c n) -> p c n", c=C)
        gates_flat = big[:, C * QKV_COLS:]
        gates = gates_flat.rearrange("p (c n) -> p c n", c=C)
        xn = gates_flat[:, 0:C * D].rearrange("p (c d) -> p c d", c=C)
        mn = gates_flat[:, C * D:].rearrange("p (c d) -> p c d", c=C)
        w1 = gates_flat[0:64, :].rearrange("p (t l h) -> p t l h", t=2, l=CMP_LEN)
        xn2 = big[:, 0:C * D].rearrange("p (c d) -> p c d", c=C)
        square_a = big[:, 0:D]
        square_b = big[:, C * D:C * D + D]
        u_ring = big[:, 0:RING * D].rearrange("p (r d) -> p r d", r=RING)
        v_ring = big[:, RING * D:2 * RING * D].rearrange("p (r d) -> p r d", r=RING)
        grow = big[:, 7 * D:8 * D]
        product = big[:, 8 * D:9 * D]
        arena = sb("arena", [P, 6144])
        xsT = arena[0:64, 0:2048].rearrange("p (t g s) -> p t g s", t=2, g=N_G)
        blk = arena[0:64, 2048:2048 + 2 * 1920].rearrange("p (t l g n) -> p t l g n", t=2, l=CMP_LEN, g=N_G)
        rot = arena[:, 0:1024].rearrange("p (k n) -> p k n", k=4)
        dT = arena[:, 0:512].rearrange("p (t s) -> p t s", t=2)
        nqT = arena[0:64, 512:1024].rearrange("p (t s) -> p t s", t=2)
        kT = arena[0:64, 1024:1536].rearrange("p (t s) -> p t s", t=2)
        Sc = arena[:, 1536:2560].rearrange("p (b n) -> p b n", b=2)
        Pr = arena[:, 2560:3584].rearrange("p (b n) -> p b n", b=2)
        at = arena[:, 3584:4608].rearrange("p (b n) -> p b n", b=2)
        dqk = arena[:, 4608:5120].rearrange("p (c t n) -> p c t n", c=C, t=2)
        nqs = arena[:, 5120:5376].rearrange("p (c n) -> p c n", c=C)
        kks = arena[:, 5376:5632].rearrange("p (t c n) -> p t c n", t=2, c=C)
        pcT = arena[0:N_CMP, 5632:6144].rearrange("p (t s) -> p t s", t=2)
        qxT = arena[:, 0:1024].rearrange("p (h s) -> p h s", h=X_H)
        oxT = qxT
        ox = arena[:, 4608:5632].rearrange("p (c n) -> p c n", c=C)
        scores = arena[:, 0:UNITS * 256]
        qpT = arena[:, 4096:5120].rearrange("p (j s) -> p j s", j=4)
        stage = sb("stage", [P, C, NW])
        half_mix = arena[:, 1536:2048]
        vmem = sb("vmem", [P, C, NW])
        kxT = sb("kxT", [P, X_H, S])
        keysT = sb("keysT", [P, 2, NKEYS])
        ident = sb("ident", [P, P])
        causal = sb("causal", [P, 2 * P])
        cm_add = sb("cm_add", [P, C, N_CMP])
        cm_mul = sb("cm_mul", [P, C, N_CMP])
        wng = sb("wng", [P, KT, NG_COLS])
        gn = sb("gn", [P, C, NG_COLS])
        raw = arena[:, 1024:1536].rearrange("p (t n) -> p t n", t=4)
        gT = sb("gT", [P, 48])
        posT = sb("posT", [64, CMP_LEN])
        w2 = sb("w2", [P, 2, N_DK])
        hid = sb("hid", [P, 2, N_G * N_CMP])
        kcT = sb("kcT", [64, N_G * N_CMP])
        vc = sb("vc", [N_CMP, N_G * N_DK])
        lam4 = arena[:, 1536:1792].rearrange("p (t n) -> p t n", t=4)
        lamb = sb("lamb", [P, 8])
        subg = sb("subg", [P, DA_DV])
        pos_i = sb("pos_i", [P, C], I32)
        rope = sb("rope", [P, 6, C, ROPE_HALF])
        inv = sb("inv", [P, ROPE_HALF])
        ssq = sb("ssq", [P, 12])
        msq = sb("msq", [P, 12])
        rstd = sb("rstd", [P, 12])
        nhalf = sb("nhalf", [P, 16])
        ms16 = sb("ms16", [P, 3, 16])
        mx = sb("mx", [P, 2, 2])
        nmx = sb("nmx", [P, 2, 2])
        sums = sb("sums", [P, 6, 4])
        rec = sb("rec", [P, 8])
        coef = sb("coef", [P, 4])
        tmp3 = sb("tmp3", [P, 3 * N_DK])
        cs = sb("cs", [P, C, 2, N_CMP])
        cmx = sb("cmx", [P, 4])
        csum = sb("csum", [P, 4])
        vmem_flat = vmem[:, :, :].rearrange("p c n -> p (c n)")
        kxT_flat = kxT[:, :, :].rearrange("p h s -> p (h s)")
        wk = vmem_flat[:, 0:256].rearrange("p (t n) -> p t n", t=2)
        wk2 = vmem_flat[:, 256:512]
        top = sb("top", [P, 2, PK])
        topi = sb("topi", [P, 2, PK], U32)
        topf = sb("topf", [P, 2, PK])
        cand = vmem_flat[:, 512:768].rearrange("p (a b) -> p a b", a=PK)
        sc16 = sb("sc16", [P, PK])
        ci = sb("ci", [P, PK], U32)
        ab = sb("ab", [P, 2, PK], U32)
        abf = sb("abf", [P, 2, PK])
        onehot = kxT_flat[:, 0:512].rearrange("p (t k a) -> p t k a", t=2, k=PK)
        e12 = sb("e12", [P, 2, PK])
        iota16 = sb("iota16", [P, PK])
        idx_u = [sb(f"idx_u{i}", [P, PK], U32) for i in range(2)]
        idx_v = [sb(f"idx_v{i}", [P, PK], U32) for i in range(2)]
        nsc = sb("nsc", [P, 1])
        ex = sb("ex", [P, PK])
        exs = sb("exs", [P, 2])
        gw = sb("gw", [P, 2, PK])
        dots = sb("dots", [P, 2, PK])
        act_u = sb("act_u", [P, PK])
        ga = sb("ga", [P, 2, PK])
        diag = kxT_flat[:, 512:1024].rearrange("p (r q) -> p r q", r=RING)

        psum = ctx.enter_context(nc.psum_tensor("banks", [P, 8 * NW], F32))
        B = [psum[:, n * NW:(n + 1) * NW] for n in range(8)]
        vacc = psum[:, 4 * NW:8 * NW]

        mem_landed, x_landed, small_landed, w1_landed = map(sem, ("mem_landed", "x_landed", "small_landed", "w1_landed"))
        grow_landed, gfin_landed, out_landed = map(sem, ("grow_landed", "gfin_landed", "out_landed"))
        w_landed = [sem(f"w_landed{s}") for s in range(SLOTS)]
        w_used = [sem(f"w_used{s}") for s in range(SLOTS)]
        acc0_ready = sem("acc0_ready")
        nacc0_ready = sem("nacc0_ready")
        acc_free = [sem(f"acc_free{c}") for c in range(C)]
        nacc_free = [sem(f"nacc_free{c}") for c in range(C)]
        tp_ready = [sem(f"tp_ready{b}") for b in range(2)]
        tp_free = [sem(f"tp_free{b}") for b in range(2)]
        consts_ready, sq_done, ms_done, rstd_done, xn_done = map(sem, ("consts_ready", "sq_done", "ms_done", "rstd_done", "xn_done"))
        dve_steps, act_steps, pool_steps = map(sem, ("dve_steps", "act_steps", "pool_steps"))
        angle_ready, sin_done, ng_ready, gn_tanh, gn_done, rope_done = map(sem, ("angle_ready", "sin_done", "ng_ready", "gn_tanh", "gn_done", "rope_done"))
        lam_in, lam_exp = sem("lam_in"), sem("lam_exp")
        blk_ready, hid_ready, hid_done, cmp_ready, cmp_done = map(sem, ("blk_ready", "hid_ready", "hid_done", "cmp_ready", "cmp_done"))
        staged, sc_ready, sc_free, nm_ready, exp_done = map(sem, ("staged", "sc_ready", "sc_free", "nm_ready", "exp_done"))
        da_ready, pt_ready, at_ready, pv_ready, ev_done = map(sem, ("da_ready", "pt_ready", "at_ready", "pv_ready", "ev_done"))
        map0_done = sem("map0_done")
        cm_ready, cexp_done, cp_ready = map(sem, ("cm_ready", "cexp_done", "cp_ready"))
        subln_ms, subln_rstd, subln_done, mix_ready, h_done = map(sem, ("subln_ms", "subln_rstd", "subln_done", "mix_ready", "h_done"))
        idx_ready, idx_v_ready = map(sem, ("idx_ready", "idx_v_ready"))
        pool_turns, pe_turns, dve_turns = map(sem, ("pool_turns", "pe_turns", "dve_turns"))
        u_landed = [sem(f"u_landed{r}") for r in range(RING)]
        v_landed = [sem(f"v_landed{r}") for r in range(RING)]
        dot_done, v_used, route_scores, route_exp, gelu_done, ga_ready, diag_ready, vacc_free, y_done = map(
            sem, ("dot_done", "v_used", "route_scores", "route_exp", "gelu_done", "ga_ready", "diag_ready", "vacc_free", "y_done"))

        x_v = x[0].rearrange("(c p) d -> p c d", p=P)
        mem_v = mem[0].rearrange("(c p) d -> p c d", p=P)
        out_v = out[0].rearrange("(c p) d -> p c d", p=P)
        N_SMALL = 16

        def slots_of(m):
            return m.rearrange("(s k p) n -> s p k n", k=KS, p=P)

        block = ctx.enter_context(nc.Block())

        @block.sync
        def _(sp):
            sp.dma_start(mn, mem_v).then_inc(mem_landed, 16)
            sp.dma_start(h[:, :, :], x_v).then_inc(x_landed, 16)

            def load(slot, tile, src):
                if not (isinstance(tile, int) and tile == 0):
                    sp.wait_ge(w_used[slot], tile)
                sp.dma_start(w[:, slot, :, :], src).then_inc(w_landed[slot], 16)

            kv, wi = slots_of(w_xkv[0]), slots_of(w_in[0])
            for n in range(2):
                for s in range(SLOTS):
                    load(s, T_KV + n, kv[s][:, :, n * NW:(n + 1) * NW])
            with sp.Fori(0, N_QKV) as i:
                for s in range(SLOTS):
                    load(s, i + T_QKV, wi[s][:, :, bass.ds(i * NW, NW)])
            for b in range(2):
                sp.wait_ge(tp_ready[b], (G_CMP - 2 + b) // 2 + 1)
            for t, m in enumerate((ck1, cv1)):
                sp.dma_start(w1[:, t, :, :], m[0].rearrange("(l d) h -> d l h", d=64)).then_inc(w1_landed, 16)
            with sp.Fori(0, N_BG) as i:
                for s in range(SLOTS):
                    load(s, i + T_BG, wi[s][:, :, bass.ds(i * NW + BG, NW)])
            br = (slots_of(w_bda[0]), slots_of(w_bnsa[0]))
            with sp.Fori(0, N_BR) as i:
                for s in range(SLOTS):
                    load(s, i + T_BR, br[s // 2][s % 2][:, :, bass.ds(i * NW, NW)])
            wo = slots_of(w_out[0])
            with sp.Fori(0, N_WO) as i:
                for s in range(SLOTS):
                    load(s, i + T_WO, wo[s][:, :, bass.ds(i * NW, NW)])
            for b in range(2):
                sp.wait_ge(tp_ready[b], (G_X2 - 2 + b) // 2 + 1)
            sp.dma_start(grow, norm_ffn_g[0].partition_broadcast(P)).then_inc(grow_landed, 16)
            xq, xo = slots_of(w_xq[0]), w_xo[0].rearrange("(k p) n -> p k n", p=P)
            for s in range(SLOTS):
                load(s, T_XQ, xq[s])
            for s in range(SLOTS):
                load(s, T_XO, xo[:, :, s * NW:(s + 1) * NW])
            pq = slots_of(peer_wq[0])
            with sp.Fori(0, N_PQ) as i:
                for s in range(SLOTS):
                    load(s, i + T_PQ, pq[s][:, :, bass.ds(i * NW, NW)])
            sp.wait_ge(w_used[0], T_PQ + N_PQ)
            sp.dma_start(gfin, norm_final_g.partition_broadcast(P)).then_inc(gfin_landed, 16)
            for c in range(C):
                sp.wait_ge(y_done, c + 1)
                sp.dma_start(out_v[:, c, :], xn3[:, c, :]).then_inc(out_landed, 16)
            sp.wait_ge(out_landed, 16 * C)

        @block.gpsimd
        def _(pool):
            link = Chain(pool, pool_steps)
            link(nc.gpsimd.memset(ident[:, :], 0.0))
            nc.gpsimd.affine_select(out=ident[:, :], in_=ident[:, :], compare_op=ALU.not_equal, fill=1.0, base=0,
                                    pattern=[[-1, P]], channel_multiplier=1).then_inc(consts_ready, 1)
            nc.gpsimd.memset(nhalf[:, :], -0.5).then_inc(consts_ready, 1)
            link(nc.gpsimd.memset(causal[:, :], 0.0))
            nc.gpsimd.affine_select(out=causal[:, :], in_=causal[:, :], compare_op=ALU.is_ge, fill=NEG, base=P,
                                    pattern=[[-1, 2 * P]], channel_multiplier=1).then_inc(consts_ready, 1)
            link(nc.gpsimd.memset(cm_add[:, :, :], 0.0))
            link(nc.gpsimd.memset(cm_mul[:, :, :], 1.0))
            for m, fill in ((cm_add, NEG), (cm_mul, 0.0)):
                nc.gpsimd.affine_select(out=m[:, :, :], in_=m[:, :, :], compare_op=ALU.is_ge, fill=fill,
                                        base=-(CMP_LEN - 1), pattern=[[P, C], [-CMP_STRIDE, N_CMP]],
                                        channel_multiplier=1).then_inc(consts_ready, 1)
            nc.gpsimd.iota(iota16[:, :], pattern=[[1, PK]], base=0, channel_multiplier=0,
                           allow_small_or_imprecise_dtypes=True).then_inc(consts_ready, 1)

            def rsqrt(n, cols=C):
                pool.wait_ge(ms_done, n + 1)
                nc.gpsimd.tensor_tensor(rstd[:, 2 * n:2 * n + cols], msq[:, 2 * n:2 * n + cols], nhalf[:, 0:cols],
                                        ALU.pow).then_inc(rstd_done, 1)

            pool.wait_ge(consts_ready, 6)
            rsqrt(0)
            rsqrt(1)
            pool.wait_ge(rope_done, 1)
            pool.wait_ge(cmp_done, 1)
            with pool.Fori(0, N_G) as g:
                for j in range(2):
                    last_q = (11, 14)[j]
                    pool.wait_ge(tp_ready[0], g * 5 + last_q - (1 if j else 0))
                    pool.sem_inc(pool_turns, 1)
                    nc.gpsimd.tensor_copy(dqk[:, :, 0, :], z[:, :, bass.ds(g * 256 + (ZQ + 128 * j), 128)])
                    nc.gpsimd.tensor_copy(dqk[:, :, 1, :], z[:, :, bass.ds(g * 256 + (ZK + 128 * j), 128)]).then_inc(staged, 1)
                    pool.wait_ge(tp_ready[1], g * 5 + last_q - (1 if j else 0))
                    pool.sem_inc(pool_turns, 1)
                    nc.gpsimd.tensor_copy(nqs[:, :, :], z[:, :, bass.ds(g * 256 + (NQ + 128 * j), 128)]).then_inc(staged, 1)
                    if j == 0:
                        nc.gpsimd.tensor_copy(kks[:, 0, :, :], z[:, :, bass.ds(g * 64 + K_SEL, 64)])
                        nc.gpsimd.tensor_copy(kks[:, 1, :, :], z[:, :, bass.ds(g * 64 + K_WIN, 64)]).then_inc(staged, 1)
            pool.wait_ge(subln_ms, 1)
            nc.gpsimd.tensor_tensor(ms16[:, 2, :], ms16[:, 1, :], nhalf[:, :], ALU.pow).then_inc(subln_rstd, 1)
            rsqrt(2)
            rsqrt(3)

            def step(par, has_u, has_v, u):
                if has_v:
                    if not (isinstance(u, int) and u == 1):
                        pool.wait_ge(v_used, u * 16 + (RING - 32))
                        pool.sem_inc(pool_turns, 1)
                    nc.gpsimd.tensor_copy(idx_v[1 - par][:, :], idx_u[1 - par][:, :]).then_inc(idx_v_ready, 1)
                    pool.wait_ge(idx_v_ready, u)
                    pool.sem_inc(pool_turns, 1)
                if has_u:
                    pool.wait_ge(idx_ready, u + 1)
                    pool.sem_inc(pool_turns, 1)
                for j in range(PK):
                    r = j % RING
                    if has_u:
                        pool.wait_ge(dot_done, u * 16 + (j + 1))
                        pool.sem_inc(pool_turns, 1)
                        nc.gpsimd.indirect_dma_start(u_ring[:, r, :], None, peer_u[0],
                                                     bass.IndirectOffsetOnAxis(ap=idx_u[par][:, j:j + 1], axis=0)).then_inc(u_landed[r], 16)
                    if has_v:
                        pool.wait_ge(v_used, u * 16 + (j + 1 - 16))
                        pool.sem_inc(pool_turns, 1)
                        nc.gpsimd.indirect_dma_start(v_ring[:, r, :], None, peer_v[0],
                                                     bass.IndirectOffsetOnAxis(ap=idx_v[1 - par][:, j:j + 1], axis=0)).then_inc(v_landed[r], 16)

            step(0, True, False, 0)
            step(1, True, True, 1)
            with pool.Fori(0, PH - 1) as i:
                step(0, True, True, i * 2 + 2)
                step(1, True, True, i * 2 + 3)
            step(0, False, True, UNITS)
            rsqrt(4, 1)
            rsqrt(5, 1)

        @block.tensor
        def _(pe):
            def tp_begin(n, g=None):
                if g is None:
                    pe.wait_ge(tp_free[n % 2], n // 2 + 1)
                else:
                    pe.wait_ge(tp_free[n % 2], g * (ATT_GROUPS // 2) + (G_ATT // 2 + n // 2 + 1))
                return B[2 + n % 2]

            def evacuated(n, g=None):
                if g is None:
                    pe.wait_ge(tp_free[n % 2], n // 2 + 2)
                else:
                    pe.wait_ge(tp_free[n % 2], g * (ATT_GROUPS // 2) + (G_ATT // 2 + n // 2 + 2))

            def transposes(n, tiles, g=None):
                bank = tp_begin(n, g)
                pe.sem_inc(pe_turns, 1)
                for src, col in tiles:
                    p, m = src.shape
                    last = nc.tensor.transpose(bank[0:m, col:col + p], src, ident[0:p, 0:p])
                last.then_inc(tp_ready[n % 2], 1)

            def part(tile, acc, s, c, lhsT, bank=None, first=0, final=SLOTS - 1, acc_sem=None):
                bank = B[c] if bank is None else bank
                if c == 0:
                    pe.wait_ge(w_landed[s], tile * 16 + 16)
                if s == first:
                    pe.wait_ge(acc_free[c] if acc_sem is None else nacc_free[c], acc + 1)
                for k in range(KS):
                    last = nc.tensor.matmul(bank, lhsT[:, (s - first) * KS + k, c * P:(c + 1) * P], w[:, s, k, :],
                                            start=(s == first and k == 0), stop=(s == final and k == KS - 1))
                if c == C - 1:
                    last.then_inc(w_used[s], 1)
                elif s == final:
                    last.then_inc(acc0_ready if acc_sem is None else acc_sem, 1)

            def whole(tile, lhsT, acc=None):
                for s in range(SLOTS):
                    for c in range(C):
                        part(tile, tile if acc is None else acc, s, c, lhsT)

            def norm_groups(base, src):
                for c in range(C):
                    for q in range(4):
                        transposes(base + 4 * c + q, [(src[:, c, (4 * q + t) * P:(4 * q + t + 1) * P], t * P) for t in range(4)])

            pe.wait_ge(consts_ready, 1)
            pe.wait_ge(small_landed, 16 * N_SMALL)
            transposes(G_GAIN, [(raw[0:48, 0, :], 0)])
            transposes(G_POS, [(raw[0:CMP_LEN, 1, 0:64], 0), (raw[:, 2, :], P), (raw[:, 3, :], 2 * P)])
            pe.wait_ge(xn_done, C)
            norm_groups(G_MEM, mn)
            for n in range(8):
                evacuated(G_MEM + n)
            for n in range(2):
                whole(T_KV + n, oT)
            pe.wait_ge(act_steps, 2)
            for c in range(C):
                transposes(G_MK + c, [(stage[:, c, t * P:(t + 1) * P], t * P) for t in range(X_H)])
            pe.wait_ge(xn_done, 2 * C)
            norm_groups(G_X, xn)
            for n in range(8):
                evacuated(G_X + n)
            with pe.Fori(0, N_QKV) as i:
                whole(i + T_QKV, xT)
            for c in range(C):
                for k in range(KT):
                    last = nc.tensor.matmul(B[4][:, c * NG_COLS:(c + 1) * NG_COLS], xT[:, k, c * P:(c + 1) * P],
                                            wng[:, k, :], start=(k == 0), stop=(k == KT - 1))
            last.then_inc(ng_ready, 1)
            pe.wait_ge(rope_done, 1)
            for t, base in enumerate((K_CMP, V_CMP)):
                for c in range(C):
                    transposes(G_CMP + 2 * t + c, [(z[:, c, base + g * 64:base + g * 64 + 64], g * P) for g in range(N_G)])
            pe.wait_ge(w1_landed, 32)
            pe.wait_ge(blk_ready, 2)
            for t in range(2):
                for l in range(CMP_LEN):
                    last = nc.tensor.matmul(B[5 + t][:, 0:60], w1[:, t, l, :], blk[:, t, l, :, :].rearrange("p g n -> p (g n)"),
                                            start=(l == 0), stop=(l == CMP_LEN - 1))
                last.then_inc(hid_ready, 1)
            pe.wait_ge(hid_done, 2)
            nc.tensor.matmul(B[7][0:64, 0:60], w2[:, 0, :], hid[:, 0, :], start=True, stop=True)
            for g in range(N_G):
                last = nc.tensor.matmul(B[7][0:N_CMP, 64 + g * 64:128 + g * 64], hid[:, 1, g * N_CMP:(g + 1) * N_CMP],
                                        w2[:, 1, :], start=True, stop=True)
            last.then_inc(cmp_ready, 1)

            pe.wait_ge(cmp_done, 2)
            pe.wait_ge(gn_done, 1)

            def score(U, u, c, pairs, apart=None):
                pe.wait_ge(sc_free, U + 1)
                nk = pairs[0][1].shape[-1]
                for m, (q, k) in enumerate(pairs):
                    last = nc.tensor.matmul(B[4 + u % 2][:, m * nk:(m + 1) * nk], q, k, start=True, stop=True)
                    if apart is not None and m == 0:
                        last.then_inc(map0_done, 1)
                        pe.wait_ge(map0_done, apart)
                last.then_inc(sc_ready, 1)

            def probs_T(U, u, nt, wait, value):
                pe.wait_ge(wait, value)
                pe.wait_ge(at_ready, U + 1)
                for t in range(nt):
                    last = nc.tensor.transpose(B[6][:, t * P:(t + 1) * P], Pr[:, u % 2, t * P:(t + 1) * P], ident[:, :])
                last.then_inc(pt_ready, 1)

            def values(U, products):
                pe.wait_ge(at_ready, U + 2)
                pe.wait_ge(ev_done, U + 1)
                pe.sem_inc(pe_turns, 1)
                for dst, terms in products:
                    for n, (a, v) in enumerate(terms):
                        last = nc.tensor.matmul(dst, a, v, start=(n == 0), stop=(n == len(terms) - 1))
                last.then_inc(pv_ready, 1)

            with pe.Fori(0, N_G) as g:
                for j in range(2):
                    T1, T2, CS, TC = ((0, 1, 4, 5), (6, 7, 8, 9))[j]
                    step = g * 2 + j
                    U = [g * 12 + (6 * j + u) for u in range(6)]

                    def fill(n):
                        part(step + T_BG, step + T_BG, n // 2, n % 2, xT)

                    def S_(u):
                        c = u % 2
                        nk = (c + 1) * P
                        if u < 2:
                            score(U[u], u, c, [(dT[64 * m:64 * m + 64, 0, c * P:(c + 1) * P], dT[64 * m:64 * m + 64, 1, 0:nk]) for m in range(2)],
                                  step * 2 + (c + 1))
                        else:
                            score(U[u], u, c, [(nqT[:, u // 2 - 1, c * P:(c + 1) * P], kT[:, m, 0:nk]) for m in range(2)])

                    def TP(u):
                        c = u % 2
                        if u < 2:
                            probs_T(U[u], u, c + 1, da_ready, step * 2 + (c + 1))
                        else:
                            probs_T(U[u], u, 2 * (c + 1), exp_done, U[u] + 1 + LAG)

                    def PV(u):
                        c = u % 2
                        a = at[:, u % 2, :]
                        kcs = range(c + 1)
                        if u < 2:
                            values(U[u], [(B[7][:, 0:P], [(a[:, kc * P:(kc + 1) * P], z[:, kc, bass.ds(g * 256 + (ZV + 128 * j), 128)]) for kc in kcs])])
                        else:
                            if u == 2:
                                evacuated(TC, g)
                            values(U[u], [
                                (B[7][:, 0:64], [(pcT[:, u // 2 - 1, c * P:(c + 1) * P], vc[:, bass.ds(g * 64, 64)])]),
                                (B[7][:, 64:128], [(a[:, kc * P:(kc + 1) * P], z[:, kc, bass.ds(g * 64 + V_SEL, 64)]) for kc in kcs]),
                                (B[7][:, 128:192], [(a[:, (c + 1 + kc) * P:(c + 2 + kc) * P], z[:, kc, bass.ds(g * 64 + V_WIN, 64)]) for kc in kcs])])

                    pe.wait_ge(staged, g * 5 + (1, 4)[j])
                    transposes(T1, [(dqk[:, c, t, :], (2 * t + c) * P) for t in range(2) for c in range(C)], g)
                    pe.wait_ge(staged, g * 5 + (2, 5)[j])
                    transposes(T2, [(nqs[:, c, t * 64:(t + 1) * 64], (2 * t + c) * P) for t in range(2) for c in range(C)], g)
                    if j == 0:
                        pe.wait_ge(staged, g * 5 + 3)
                        for t in range(2):
                            transposes(2 + t, [(kks[:, t, c, :], c * P) for c in range(C)], g)
                    fill(0)
                    evacuated(T1, g)
                    S_(0)
                    evacuated(T2, g)
                    if j == 0:
                        evacuated(2, g)
                        evacuated(3, g)
                    bank = tp_begin(CS, g)
                    pe.sem_inc(pe_turns, 1)
                    for c in range(C):
                        for t in range(2):
                            last = nc.tensor.matmul(bank[:, (2 * c + t) * N_CMP:(2 * c + t + 1) * N_CMP],
                                                    nqT[:, t, c * P:(c + 1) * P], kcT[:, bass.ds(g * N_CMP, N_CMP)],
                                                    start=True, stop=True)
                    last.then_inc(tp_ready[CS % 2], 1)
                    fill(1)
                    S_(1), TP(0)
                    fill(2)
                    S_(2), TP(1), PV(0)
                    fill(3)
                    S_(3), TP(2), PV(1)
                    pe.wait_ge(cp_ready, step + 1)
                    transposes(TC, [(cs[:, c, t, :], (2 * t + c) * P) for t in range(2) for c in range(C)], g)
                    fill(4)
                    S_(4), TP(3), PV(2)
                    fill(5)
                    S_(5), TP(4), PV(3)
                    fill(6)
                    TP(5), PV(4)
                    fill(7)
                    PV(5)

            pe.wait_ge(ev_done, 48 + 1)
            pe.wait_ge(sc_free, 48 + LAG)
            for n in range(4):
                c, hf = n // 2, n % 2
                transposes(G_OT + n, [(z[:, c, NQ + (4 * hf + t) * P:NQ + (4 * hf + t + 1) * P], t * P) for t in range(4)])
            for n in range(4):
                c, hf = n // 2, n % 2
                if hf == 0:
                    pe.wait_ge(subln_done, c + 1)
                transposes(G_OT + 4 + n, [(z[:, c, ZQ + (4 * hf + t) * P:ZQ + (4 * hf + t + 1) * P], t * P) for t in range(4)])
            for n in range(8):
                evacuated(G_OT + n)
            with pe.Fori(0, N_BR) as i:
                for s in range(SLOTS):
                    for c in range(C):
                        if s < 2:
                            part(i + T_BR, i + T_BR, s, c, oT[:, 0:8, :], first=0, final=1)
                        else:
                            part(i + T_BR, i, s, c, oT[:, 8:16, :], bank=B[4 + c], first=2, final=3, acc_sem=nacc0_ready)
                for c in range(C):
                    pe.wait_ge(mix_ready, i * 2 + (c + 1))
                    pe.wait_ge(tp_free[c], i + (G_MIX // 2 + 1))
                    for t in range(4):
                        last = nc.tensor.transpose(B[2 + c][:, t * P:(t + 1) * P], stage[:, c, t * P:(t + 1) * P], ident[:, :])
                    last.then_inc(tp_ready[c], 1)
            for n in range(2):
                evacuated(G_X2 - 2 + n)
            with pe.Fori(0, N_WO) as i:
                whole(i + T_WO, xT)

            pe.wait_ge(xn_done, 3 * C)
            norm_groups(G_X2, xn2)
            for n in range(8):
                evacuated(G_X2 + n)
            whole(T_XQ, xT)
            pe.wait_ge(act_steps, 6)
            for c in range(C):
                transposes(G_QX + c, [(stage[:, c, t * P:(t + 1) * P], t * P) for t in range(X_H)])
            for c in range(C):
                evacuated(G_QX + c)
                pe.wait_ge(nacc_free[c], 1 + N_BR)

            def XS(v):
                c, hp = v // 2, v % 2
                score(48 + v, v, c, [(qxT[:, 2 * hp + m, c * P:(c + 1) * P], kxT[:, 2 * hp + m, :]) for m in range(2)])

            def XT(v):
                probs_T(48 + v, v, 4, exp_done, 48 + v + 1 + LAG)

            def XV(v):
                hp, a = v % 2, at[:, v % 2, :]
                values(48 + v, [(B[7][:, m * P:(m + 1) * P],
                                 [(a[:, (2 * m + kc) * P:(2 * m + kc + 1) * P], vmem[:, kc, (2 * hp + m) * P:(2 * hp + m + 1) * P]) for kc in range(2)])
                                for m in range(2)])

            XS(0), XS(1), XT(0), XS(2), XT(1), XV(0), XS(3), XT(2), XV(1), XT(3), XV(2), XV(3)
            for c in range(C):
                pe.wait_ge(ev_done, 48 + 2 * c + 2 + 1)
                transposes(G_OX + c, [(ox[:, c, t * P:(t + 1) * P], t * P) for t in range(X_H)])
            for c in range(C):
                evacuated(G_OX + c)
            for s in range(SLOTS):
                for c in range(C):
                    part(T_XO, T_XO + s, s, c, oxT, first=s, final=s)

            pe.wait_ge(xn_done, 4 * C)
            norm_groups(G_X3, xn3)
            for n in range(8):
                evacuated(G_X3 + n)
            with pe.Fori(0, N_PQ) as i:
                whole(i + T_PQ, xT, i + A_PQ)
                for c in range(C):
                    pe.wait_ge(act_steps, i * 2 + (6 + c + 1))
                    pe.wait_ge(tp_free[c], i * 2 + (G_PQ // 2 + 1))
                    for t in range(4):
                        last = nc.tensor.transpose(B[2 + c][:, t * P:(t + 1) * P], stage[:, c, t * P:(t + 1) * P], ident[:, :])
                    last.then_inc(tp_ready[c], 1)
                for c in range(C):
                    pe.wait_ge(tp_free[c], i * 2 + (G_PQ // 2 + 2))
                for hh in range(2):
                    for c in range(C):
                        for half in range(2):
                            last = nc.tensor.matmul(B[2 + hh][:, (2 * c + half) * P:(2 * c + half + 1) * P],
                                                    qpT[:, 2 * hh + half, c * P:(c + 1) * P], keysT[:, half, :],
                                                    start=True, stop=True)
                    last.then_inc(tp_ready[hh], 1)

            def v_step(u):
                pe.wait_ge(vacc_free, u + 1)
                for j in range(PK):
                    r = j % RING
                    pe.wait_ge(v_landed[r], u * 64 + 16 * (j // RING + 1))
                    pe.wait_ge(diag_ready, u * 16 + (j + 1))
                    for n in range(4):
                        last = nc.tensor.matmul(B[4 + n], diag[:, r, :], v_ring[:, r, n * NW:(n + 1) * NW],
                                                start=(j == 0), stop=(j == PK - 1))
                    last.then_inc(v_used, 1)

            with pe.Fori(0, UNITS) as i:
                v_step(i)

        @block.scalar
        def _(act):
            A = nc.scalar.activation
            for q in (tp_free[0], tp_free[1], acc_free[0], acc_free[1], at_ready):
                act.sem_inc(q, 1)
            act.sem_inc(exp_done, LAG)

            smalls = [(raw[0:16, 0, :], norm_mix_g[0].rearrange("(k p) -> k p", p=P)),
                      (raw[16:32, 0, :], norm_mem_g[0].rearrange("(k p) -> k p", p=P)),
                      (raw[32:48, 0, :], norm_x_g[0].rearrange("(k p) -> k p", p=P)),
                      (raw[0:CMP_LEN, 1, 0:64], cmp_pos[0]),
                      (raw[:, 2, :], keys1[0]), (raw[:, 3, :], keys2[0]),
                      (w2[:, 0, :], ck2[0]), (w2[:, 1, :], cv2[0]),
                      (lam4[:, 0, :], lq1[0].partition_broadcast(P)), (lam4[:, 1, :], lk1[0].partition_broadcast(P)),
                      (lam4[:, 2, :], lq2[0].partition_broadcast(P)), (lam4[:, 3, :], lk2[0].partition_broadcast(P)),
                      (subg[:, :], subln_g[0].partition_broadcast(P)),
                      (pos_i[:, 0:1], positions[0, 0:P].rearrange("(p o) -> p o", o=1)),
                      (pos_i[:, 1:2], positions[0, P:S].rearrange("(p o) -> p o", o=1)),
                      (wng[:, :, :], w_in[0].rearrange("(k p) n -> p k n", p=P)[:, :, QKV_COLS:BG])]
            assert len(smalls) == N_SMALL
            for dst, src in smalls:
                act.dma_start(dst, src).then_inc(small_landed, 16)

            def squares(n, c, src, junk):
                done = min(2 * n, 8) + (n == 5) + c
                if done:
                    act.wait_ge(sq_done, done)
                A(junk, src, ACT.Square, accum_out=ssq[:, 2 * n + c:2 * n + c + 1]).then_inc(sq_done, 1)

            act.wait_ge(mem_landed, 16)
            for c in range(C):
                squares(0, c, mn[:, c, :], square_a)
            act.wait_ge(x_landed, 16)
            for c in range(C):
                squares(1, c, h[:, c, :], square_a)
            act.wait_ge(angle_ready, 1)
            A(rope[:, 4, :, :], rope[:, 2, :, :], ACT.Sin)
            A(rope[:, 5, :, :], rope[:, 3, :, :], ACT.Sin).then_inc(sin_done, 1)

            def evac_acc(c, tile, acc, dst, signal):
                if c == 0:
                    act.wait_ge(acc0_ready, acc + 1)
                else:
                    act.wait_ge(w_used[SLOTS - 1], tile + 1)

            def copy_acc(c, tile, acc, dst):
                evac_acc(c, tile, acc, dst, None)
                A(dst, B[c], ACT.Copy).then_inc(acc_free[c], 1)

            def evac(n, dst, src, g=None):
                act.wait_ge(tp_ready[n % 2], n // 2 + 1 if g is None else g * (ATT_GROUPS // 2) + (G_ATT // 2 + n // 2 + 1))
                A(dst, src, ACT.Copy).then_inc(tp_free[n % 2], 1)

            def four(n):
                return B[2 + n % 2].rearrange("p (t s) -> p t s", t=4)

            for n, dst in enumerate((stage, vmem)):
                for c in range(C):
                    copy_acc(c, T_KV + n, T_KV + n, dst[:, c, :])
                if n == 0:
                    for c in range(C):
                        act.wait_ge(acc_free[c], 2)
                        act.sem_inc(act_steps, 1)
            for c in range(C):
                evac(G_MK + c, kxT[:, :, c * P:(c + 1) * P], four(G_MK + c))
            with act.Fori(0, N_QKV) as i:
                for c in range(C):
                    copy_acc(c, i + T_QKV, i + T_QKV, z[:, c, bass.ds(i * NW, NW)])
            act.wait_ge(ng_ready, 1)
            A(gn[:, :, :].rearrange("p c n -> p (c n)"), B[4][:, 0:C * NG_COLS], ACT.Tanh, scale=0.5).then_inc(gn_tanh, 1)
            act.wait_ge(lam_in, 1)
            A(lamb[:, 2:4], lamb[:, 0:2], ACT.Exp).then_inc(lam_exp, 1)
            for t in range(2):
                for c in range(C):
                    n = G_CMP + 2 * t + c
                    evac(n, xsT[:, t, :, c * P:(c + 1) * P], four(n)[0:64])
            for t in range(2):
                act.wait_ge(hid_ready, t + 1)
                A(hid[:, t, :], B[5 + t][:, 0:60], ACT.Gelu).then_inc(hid_done, 1)
            act.wait_ge(cmp_ready, 1)
            A(kcT[:, :], B[7][0:64, 0:60], ACT.Copy).then_inc(cmp_done, 1)
            A(vc[:, :], B[7][0:N_CMP, 64:320], ACT.Copy).then_inc(cmp_done, 1)

            def exps(U, u, nk):
                act.wait_ge(nm_ready, U + 1)
                act.wait_ge(pt_ready, U + 1)
                for m in range(2):
                    last = A(Pr[:, u % 2, m * nk:(m + 1) * nk], Sc[:, u % 2, m * nk:(m + 1) * nk], ACT.Exp,
                             bias=nmx[:, u % 2, m:m + 1], accum_out=sums[:, u, 1 + m:2 + m])
                last.then_inc(exp_done, 1)

            def copy_pt(U, u, nt):
                act.wait_ge(pt_ready, U + 1 + LAG)
                act.wait_ge(pv_ready, U + 1)
                A(at[:, u % 2, 0:nt * P], B[6][:, 0:nt * P], ACT.Copy).then_inc(at_ready, 1)

            with act.Fori(0, N_G) as g:
                for j in range(2):
                    T1, T2, CS, TC = ((0, 1, 4, 5), (6, 7, 8, 9))[j]
                    step = g * 2 + j
                    U = [g * 12 + (6 * j + u) for u in range(6)]
                    act.wait_ge(sc_ready, U[0] + LAG)
                    evac(T1, dT, B[2 + T1 % 2].rearrange("p (t s) -> p t s", t=2), g)
                    evac(T2, nqT, B[2 + T2 % 2][0:64].rearrange("p (t s) -> p t s", t=2), g)
                    if j == 0:
                        for t in range(2):
                            evac(2 + t, kT[:, t, :], B[2 + t][0:64, 0:S], g)
                    nt = [1, 2, 2, 4, 2, 4]
                    nks = [P, 2 * P] * 3
                    exps(U[0], 0, nks[0])
                    act.wait_ge(cm_ready, step + 1)
                    A(cs[:, :, :, :].rearrange("p c t n -> p (c t n)"), cs[:, :, :, :].rearrange("p c t n -> p (c t n)"), ACT.Exp).then_inc(cexp_done, 1)
                    exps(U[1], 1, nks[1])
                    copy_pt(U[0], 0, nt[0])
                    exps(U[2], 2, nks[2])
                    copy_pt(U[1], 1, nt[1])
                    exps(U[3], 3, nks[3])
                    copy_pt(U[2], 2, nt[2])
                    evac(TC, pcT, B[2 + TC % 2][0:N_CMP].rearrange("p (t s) -> p t s", t=2), g)
                    exps(U[4], 4, nks[4])
                    copy_pt(U[3], 3, nt[3])
                    exps(U[5], 5, nks[5])
                    copy_pt(U[4], 4, nt[4])
                    copy_pt(U[5], 5, nt[5])
                    for c in range(C):
                        evac_acc(c, step + T_BG, step + T_BG, None, None)
                        A(gates[:, c, bass.ds(g * 1024 + 512 * j, NW)], B[c], ACT.Tanh, scale=0.5).then_inc(acc_free[c], 1)

            for n in range(8):
                c, hf, first = (n % 4) // 2, n % 2, 8 if n < 4 else 0
                evac(G_OT + n, oT[:, first + 4 * hf:first + 4 * hf + 4, c * P:(c + 1) * P], four(n))
            with act.Fori(0, N_BR) as i:
                for c in range(C):
                    act.wait_ge(tp_ready[c], i + (G_MIX // 2 + 1))
                    A(xT[:, bass.ds(i * 4, 4), c * P:(c + 1) * P], four(c), ACT.Copy).then_inc(tp_free[c], 1)
            act.wait_ge(h_done, 2 * N_WO)
            for c in range(C):
                squares(2, c, h[:, c, :], square_b)
            for c in range(C):
                copy_acc(c, T_XQ, T_XQ, stage[:, c, :])
            for c in range(C):
                act.wait_ge(acc_free[c], T_XQ + 2)
                act.sem_inc(act_steps, 2)
            for c in range(C):
                evac(G_QX + c, qxT[:, :, c * P:(c + 1) * P], four(c))
            for kind, v in (("e", 0), ("e", 1), ("t", 0), ("e", 2), ("t", 1), ("e", 3), ("t", 2), ("t", 3)):
                if kind == "e":
                    exps(48 + v, v, 2 * P)
                else:
                    copy_pt(48 + v, v, 4)
            for c in range(C):
                evac(G_OX + c, oxT[:, :, c * P:(c + 1) * P], four(c))
            act.wait_ge(h_done, 2 * N_WO + 2 * X_H)
            for c in range(C):
                squares(3, c, h[:, c, :], square_b)
            for c in range(C):
                for q in range(4):
                    evac(G_X3 + 4 * c + q, xT[:, 4 * q:4 * q + 4, c * P:(c + 1) * P], four(q))

            def query_tile(i):
                for c in range(C):
                    if c == 0:
                        act.wait_ge(acc0_ready, i + (A_PQ + 1))
                    else:
                        act.wait_ge(w_used[SLOTS - 1], i + (T_PQ + 1))
                    A(stage[:, c, :], B[c], ACT.Copy).then_inc(acc_free[c], 1)
                    act.wait_ge(acc_free[c], i + (A_PQ + 2))
                    act.sem_inc(act_steps, 1)
                for c in range(C):
                    act.wait_ge(tp_ready[c], i * 2 + (G_PQ // 2 + 1))
                    A(qpT[:, :, c * P:(c + 1) * P], four(c), ACT.Copy).then_inc(tp_free[c], 1)
                for hh in range(2):
                    act.wait_ge(tp_ready[hh], i * 2 + (G_PQ // 2 + 2))
                    A(scores[:, bass.ds(i * 1024 + 512 * hh, 512)] if not isinstance(i, int) else scores[:, i * 1024 + 512 * hh:i * 1024 + 512 * hh + 512],
                      B[2 + hh], ACT.Copy).then_inc(tp_free[hh], 1)

            def route_softmax(u):
                act.wait_ge(route_scores, u + 1)
                A(ex[:, :], sc16[:, :], ACT.Exp, bias=nsc[:, :], accum_out=exs[:, 0:1]).then_inc(route_exp, 1)

            query_tile(0)
            route_softmax(0)
            route_softmax(1)
            with act.Fori(1, N_PQ) as i:
                query_tile(i)

            def gelu(par, u):
                act.wait_ge(dot_done, u * 16 + (16 + RING))
                A(act_u[:, :], dots[:, par, :], ACT.Gelu).then_inc(gelu_done, 1)

            def diagonals(par, u, js):
                for j in js:
                    act.wait_ge(v_used, u * 16 + (j + 1))
                    A(diag[:, j % RING, :], ident[:, :], ACT.Copy, scale=ga[:, par, j:j + 1]).then_inc(diag_ready, 1)

            gelu(0, 0)
            with act.Fori(0, PH - 1) as i:
                for par, u in ((0, i * 2), (1, i * 2 + 1)):
                    act.wait_ge(ga_ready, u + 1)
                    diagonals(par, u, range(0, 5))
                    route_softmax(u + 2)
                    diagonals(par, u, range(5, PK))
                    gelu(1 - par, u + 1)
            act.wait_ge(ga_ready, UNITS - 1)
            diagonals(0, UNITS - 2, range(PK))
            gelu(1, UNITS - 1)
            act.wait_ge(ga_ready, UNITS)
            diagonals(1, UNITS - 1, range(0, 4))
            act.wait_ge(vacc_free, UNITS)
            squares(4, 0, h[:, 0, :], u_ring[:, 0, :])
            diagonals(1, UNITS - 1, range(4, PK))
            act.wait_ge(vacc_free, UNITS + 1)
            squares(5, 0, h[:, 1, :], u_ring[:, 0, :])

        @block.vector
        def _(dve):
            V = nc.vector
            link = Chain(dve, dve_steps)
            dve.sem_inc(sc_free, LAG)
            dve.sem_inc(sc_ready, LAG)
            dve.sem_inc(pt_ready, LAG)
            dve.sem_inc(pv_ready, LAG)
            dve.sem_inc(ev_done, 1)
            dve.sem_inc(vacc_free, 1)
            dve.sem_inc(nacc_free[0], 1)
            dve.sem_inc(nacc_free[1], 1)
            dve.sem_inc(dot_done, RING)
            dve.sem_inc(v_used, RING)

            for i in range(ROPE_HALF):
                V.memset(inv[:, i:i + 1], ROPE_INV[i])
            link(V.memset(lamb[:, :], 0.0))

            def mean_squares(n, cols=2, count=None):
                dve.wait_ge(sq_done, count)
                V.tensor_scalar(msq[:, 2 * n:2 * n + cols], ssq[:, 2 * n:2 * n + cols], 1.0 / D, EPS, ALU.mult, ALU.add).then_inc(ms_done, 1)

            def scale_rows(n, src, dst):
                dve.wait_ge(rstd_done, n + 1)
                for c in range(C):
                    V.tensor_scalar(dst[:, c, :], src[:, c, :], rstd[:, 2 * n + c:2 * n + c + 1], None, ALU.mult).then_inc(xn_done, 1)

            def evac_gain(base, col, dst):
                for c in range(C):
                    for q in range(4):
                        n = base + 4 * c + q
                        dve.wait_ge(tp_ready[n % 2], n // 2 + 1)
                        V.tensor_tensor(dst[:, 4 * q:4 * q + 4, c * P:(c + 1) * P], B[2 + n % 2].rearrange("p (t s) -> p t s", t=4),
                                        gT[:, col + 4 * q:col + 4 * q + 4].unsqueeze(2).broadcast_to([P, 4, P]), ALU.mult).then_inc(tp_free[n % 2], 1)

            dve.wait_ge(tp_ready[0], 1)
            V.tensor_copy(gT[:, :], B[2][:, 0:48]).then_inc(tp_free[0], 1)
            dve.wait_ge(tp_ready[1], 1)
            V.tensor_copy(posT[:, :], B[3][0:64, 0:CMP_LEN])
            V.tensor_copy(keysT[:, :, :].rearrange("p t n -> p (t n)"), B[3][:, P:3 * P]).then_inc(tp_free[1], 1)
            dve.wait_ge(tp_free[0], 2)
            mean_squares(0, count=2)
            scale_rows(0, mn, mn)
            evac_gain(G_MEM, 16, oT)
            mean_squares(1, count=4)
            scale_rows(1, h, xn)

            link(V.tensor_copy(rope[:, 0, :, 0], pos_i[:, :]))
            link(V.tensor_tensor(rope[:, 1, :, :], rope[:, 0, :, 0:1].broadcast_to([P, C, ROPE_HALF]),
                                 inv[:, :].unsqueeze(1).broadcast_to([P, C, ROPE_HALF]), ALU.mult))
            link(V.tensor_scalar(rope[:, 0, :, :], rope[:, 1, :, :], 1.0 / (2 * math.pi), MAGIC, ALU.mult, ALU.add))
            link(V.tensor_scalar(rope[:, 0, :, :], rope[:, 0, :, :], -MAGIC, None, ALU.add))
            for part_ in (TWO_PI_A, TWO_PI_B, TWO_PI_C):
                link(V.scalar_tensor_tensor(out=rope[:, 1, :, :], in0=rope[:, 0, :, :], scalar=-part_, in1=rope[:, 1, :, :],
                                            op0=ALU.mult, op1=ALU.add))
            link(V.tensor_scalar(rope[:, 2, :, :], rope[:, 1, :, :], PI_IN, -PI_IN, ALU.min, ALU.max))
            link(V.tensor_scalar(rope[:, 0, :, :], rope[:, 2, :, :], -1.0, None, ALU.mult))
            link(V.tensor_tensor(rope[:, 1, :, :], rope[:, 0, :, :], rope[:, 2, :, :], ALU.min))
            V.tensor_scalar(rope[:, 3, :, :], rope[:, 1, :, :], math.pi / 2, None, ALU.add).then_inc(angle_ready, 1)
            link(V.tensor_tensor(rot[:, 0, 0:64], lam4[:, 0, :], lam4[:, 1, :], ALU.mult))
            link(V.tensor_tensor(rot[:, 0, 64:128], lam4[:, 2, :], lam4[:, 3, :], ALU.mult))
            V.reduce_sum(lamb[:, 0:2], rot[:, 0, 0:128].rearrange("p (t d) -> p t d", t=2), axis=AX.X).then_inc(lam_in, 1)
            link(V.tensor_scalar(subg[:, :], subg[:, :], 1.0 - LAMBDA_INIT, None, ALU.mult))
            evac_gain(G_X, 0, xT)

            sin, cos = rope[:, 4, :, :], rope[:, 5, :, :]

            def rotate(c, first, n):
                v = z[:, c, first:first + 64 * n].rearrange("p (n d) -> p n d", d=64)
                x1, x2 = v[:, :, 0:ROPE_HALF], v[:, :, ROPE_HALF:2 * ROPE_HALF]
                t = [rot[:, k, 0:8 * n].rearrange("p (n d) -> p n d", d=8) for k in range(4)]
                cc = cos[:, c, :].unsqueeze(1).broadcast_to([P, n, ROPE_HALF])
                ss = sin[:, c, :].unsqueeze(1).broadcast_to([P, n, ROPE_HALF])
                V.tensor_tensor(t[0], x1, cc, ALU.mult)
                V.tensor_tensor(t[1], x2, ss, ALU.mult)
                V.tensor_tensor(t[2], x2, cc, ALU.mult)
                link(V.tensor_tensor(t[3], x1, ss, ALU.mult))
                V.tensor_tensor(x1, t[0], t[1], ALU.subtract)
                link(V.tensor_tensor(x2, t[2], t[3], ALU.add))

            dve.wait_ge(sin_done, 1)
            for tiles, parts in ((4, [(ZQ, 32)]), (8, [(NQ, 16)]), (11, [(K_CMP, 4), (K_SEL, 4), (K_WIN, 4)])):
                for c in range(C):
                    dve.wait_ge(acc_free[c], T_QKV + tiles + 1)
                for c in range(C):
                    for first, n in parts:
                        rotate(c, first, n)
            link(V.memset(csum[:, :], 0.0))
            V.tensor_copy(coef[:, 0:1], csum[:, 0:1]).then_inc(rope_done, 1)
            dve.wait_ge(gn_tanh, 1)
            V.tensor_scalar(gn[:, :, :], gn[:, :, :], 0.5, 0.5, ALU.mult, ALU.add).then_inc(gn_done, 1)
            dve.wait_ge(lam_exp, 1)
            link(V.tensor_tensor(lamb[:, 4:5], lamb[:, 3:4], lamb[:, 2:3], ALU.subtract))
            link(V.tensor_scalar(lamb[:, 5:6], lamb[:, 4:5], -LAMBDA_INIT, None, ALU.add))
            neg_lam = lamb[:, 5:6]
            for t in range(2):
                for c in range(C):
                    dve.wait_ge(tp_free[c], (G_CMP + 2 * t + c) // 2 + 2)
                for lh in range(2):
                    last = V.tensor_tensor(blk[:, t, 16 * lh:16 * lh + 16, :, :],
                                           xsT[:, t, :, 16 * lh:16 * lh + 240].rearrange("p g (n l) -> p l g n", l=16),
                                           posT[:, 16 * lh:16 * lh + 16].unsqueeze(2).unsqueeze(3).broadcast_to([64, 16, N_G, N_CMP]), ALU.add)
                last.then_inc(blk_ready, 1)

            def softmax_in(U, u, nk, mask):
                dve.wait_ge(sc_ready, U + 1 + LAG)
                dve.wait_ge(exp_done, U + 1)
                b = u % 2
                sv = Sc[:, b, 0:2 * nk].rearrange("p (m n) -> p m n", m=2)
                pv = B[4 + b][:, 0:2 * nk].rearrange("p (m n) -> p m n", m=2)
                if mask is None:
                    V.tensor_scalar(sv, pv, X_SCALE, None, ALU.mult).then_inc(sc_free, 1)
                else:
                    V.scalar_tensor_tensor(out=sv, in0=pv, scalar=ATT_SCALE, in1=mask.unsqueeze(1).broadcast_to([P, 2, nk]),
                                           op0=ALU.mult, op1=ALU.add).then_inc(sc_free, 1)
                dve.wait_ge(sc_free, U + 1 + LAG)
                link(V.reduce_max(mx[:, b, :], sv, axis=AX.X))
                V.tensor_scalar(nmx[:, b, :], mx[:, b, :], -1.0, None, ALU.mult).then_inc(nm_ready, 1)

            with dve.Fori(0, N_G) as g:
                link.loop(g, ATT_STEPS)
                for j in range(2):
                    CS, TC = ((4, 5), (8, 9))[j]
                    step = g * 2 + j
                    U = [g * 12 + (6 * j + u) for u in range(6)]

                    def SM(u):
                        c = u % 2
                        softmax_in(U[u], u, (c + 1) * P, causal[:, P:2 * P] if c == 0 else causal[:, :])

                    def difference(u):
                        dve.wait_ge(exp_done, U[u] + 1 + LAG)
                        nk = (u + 1) * P
                        p0, p1 = Pr[:, u, 0:nk], Pr[:, u, nk:2 * nk]
                        link(V.reciprocal(rec[:, 0:2], sums[:, u, 1:3]))
                        V.tensor_scalar(coef[:, 0:1], rec[:, 1:2], neg_lam, None, ALU.mult)
                        link(V.tensor_scalar(p0, p0, rec[:, 0:1], None, ALU.mult))
                        V.scalar_tensor_tensor(out=p0, in0=p1, scalar=coef[:, 0:1], in1=p0, op0=ALU.mult, op1=ALU.add).then_inc(da_ready, 1)

                    def EV(u):
                        c = u % 2
                        dve.wait_ge(pv_ready, U[u] + 1 + LAG)
                        if u < 2:
                            V.tensor_copy(z[:, c, bass.ds(g * 256 + (ZQ + 128 * j), 128)], B[7][:, 0:P]).then_inc(ev_done, 1)
                            return
                        t = u // 2 - 1
                        link(V.tensor_copy(sums[:, u, 0:1], csum[:, 2 * c + t:2 * c + t + 1]))
                        link(V.reciprocal(rec[:, 2:5], sums[:, u, 0:3]))
                        link(V.tensor_tensor(coef[:, 1:4], rec[:, 2:5], gn[:, c, bass.ds(g * 12 + (6 * j + 3 * t), 3)], ALU.mult))
                        tv = tmp3[:, :].rearrange("p (b d) -> p b d", b=3)
                        link(V.tensor_tensor(tv, B[7][:, 0:3 * N_DK].rearrange("p (b d) -> p b d", b=3),
                                             coef[:, 1:4].unsqueeze(2).broadcast_to([P, 3, N_DK]), ALU.mult))
                        V.reduce_sum(z[:, c, bass.ds(g * 256 + (NQ + 128 * j + 64 * t), 64)],
                                     tmp3[:, :].rearrange("p (b d) -> p d b", b=3), axis=AX.X).then_inc(ev_done, 1)

                    def compressed_in():
                        dve.wait_ge(tp_ready[CS % 2], g * 5 + (G_ATT // 2 + CS // 2 + 1))
                        dve.wait_ge(tp_ready[1], g * 5 + (12, 15)[j])
                        for c in range(C):
                            last = V.scalar_tensor_tensor(out=cs[:, c, :, :], in0=B[2 + CS % 2][:, 30 * c:30 * c + 30].rearrange("p (t n) -> p t n", t=2),
                                                          scalar=ATT_SCALE, in1=cm_add[:, c, :].unsqueeze(1).broadcast_to([P, 2, N_CMP]),
                                                          op0=ALU.mult, op1=ALU.add)
                        last.then_inc(tp_free[CS % 2], 1)
                        dve.wait_ge(tp_free[CS % 2], g * 5 + (G_ATT // 2 + CS // 2 + 2))
                        flat = cs[:, :, :, :].rearrange("p c t n -> p (c t) n")
                        link(V.reduce_max(cmx[:, :], flat, axis=AX.X))
                        V.tensor_tensor(flat, flat, cmx[:, :].unsqueeze(2).broadcast_to([P, 4, N_CMP]), ALU.subtract).then_inc(cm_ready, 1)

                    def compressed_out():
                        dve.wait_ge(cexp_done, step + 1)
                        flat = cs[:, :, :, :].rearrange("p c t n -> p (c t) n")
                        link(V.reduce_sum(csum[:, :], flat, axis=AX.X))
                        for c in range(C):
                            last = V.tensor_tensor(cs[:, c, :, :], cs[:, c, :, :], cm_mul[:, c, :].unsqueeze(1).broadcast_to([P, 2, N_CMP]), ALU.mult)
                        last.then_inc(cp_ready, 1)

                    SM(0), compressed_in(), SM(1), difference(0), SM(2), difference(1), compressed_out(), EV(0)
                    SM(3), EV(1), SM(4), EV(2), SM(5), EV(3), EV(4), EV(5)
                link.end(N_G)

            dve.wait_ge(ev_done, 48 + 1)
            sq = stage[:, :, :].rearrange("p c n -> p (c n)")
            for c in range(C):
                link(V.tensor_tensor(sq, z[:, c, 0:1024], z[:, c, 0:1024], ALU.mult))
                link(V.reduce_sum(ms16[:, 0, 8 * c:8 * c + 8], sq.rearrange("p (h d) -> p h d", h=DA_H), axis=AX.X))
            V.tensor_scalar(ms16[:, 1, :], ms16[:, 0, :], 1.0 / DA_DV, EPS, ALU.mult, ALU.add).then_inc(subln_ms, 1)
            dve.wait_ge(subln_rstd, 1)
            for c in range(C):
                o = z[:, c, 0:1024].rearrange("p (h d) -> p h d", h=DA_H)
                link(V.tensor_tensor(o, o, ms16[:, 2, 8 * c:8 * c + 8].unsqueeze(2).broadcast_to([P, DA_H, DA_DV]), ALU.mult))
                V.tensor_tensor(o, o, subg[:, :].unsqueeze(1).broadcast_to([P, DA_H, DA_DV]), ALU.mult).then_inc(subln_done, 1)

            with dve.Fori(0, N_BR) as i:
                for c in range(C):
                    if c == 0:
                        dve.wait_ge(acc0_ready, i + (T_BR + 1))
                    else:
                        dve.wait_ge(w_used[1], i + (T_BR + 1))
                    dve.wait_ge(tp_ready[c], i + G_MIX // 2)
                    V.scalar_tensor_tensor(out=stage[:, c, :], in0=gates[:, c, bass.ds(i * NW, NW)], scalar=1.0, in1=B[c],
                                           op0=ALU.add, op1=ALU.mult).then_inc(acc_free[c], 1)
                for c in range(C):
                    if c == 0:
                        dve.wait_ge(nacc0_ready, i + 1)
                    else:
                        dve.wait_ge(w_used[3], i + (T_BR + 1))
                        dve.wait_ge(mix_ready, i * 2 + 1)
                    V.scalar_tensor_tensor(out=half_mix[:, :], in0=gates[:, c, bass.ds(i * NW + D, NW)], scalar=1.0, in1=B[4 + c],
                                           op0=ALU.add, op1=ALU.mult).then_inc(nacc_free[c], 1)
                    dve.wait_ge(nacc_free[c], i + 2)
                    dve.wait_ge(acc_free[c], i + (T_BR + 2))
                    V.tensor_tensor(stage[:, c, :], stage[:, c, :], half_mix[:, :], ALU.add).then_inc(mix_ready, 1)
            with dve.Fori(0, N_WO) as i:
                for c in range(C):
                    if c == 0:
                        dve.wait_ge(acc0_ready, i + (T_WO + 1))
                    else:
                        dve.wait_ge(w_used[3], i + (T_WO + 1))
                    hv = h[:, c, bass.ds(i * NW, NW)]
                    V.scalar_tensor_tensor(out=hv, in0=B[c], scalar=0.5, in1=hv, op0=ALU.mult, op1=ALU.add).then_inc(acc_free[c], 1)
                    dve.wait_ge(acc_free[c], i + (T_WO + 2))
                    dve.sem_inc(h_done, 1)
            mean_squares(2, count=6)
            scale_rows(2, h, xn2)
            evac_gain(G_X2, 32, xT)

            def XEV(v):
                c, hp = v // 2, v % 2
                dve.wait_ge(pv_ready, 48 + v + 1 + LAG)
                link(V.reciprocal(rec[:, 0:2], sums[:, v, 1:3]))
                V.tensor_tensor(ox[:, c, 256 * hp:256 * hp + 256].rearrange("p (m d) -> p m d", m=2), B[7][:, 0:256].rearrange("p (m d) -> p m d", m=2),
                                rec[:, 0:2].unsqueeze(2).broadcast_to([P, 2, P]), ALU.mult).then_inc(ev_done, 1)

            for kind, v in (("s", 0), ("s", 1), ("s", 2), ("e", 0), ("s", 3), ("e", 1), ("e", 2), ("e", 3)):
                if kind == "s":
                    softmax_in(48 + v, v, 2 * P, None)
                else:
                    XEV(v)
            for n in range(X_H):
                for c in range(C):
                    if c == 0:
                        dve.wait_ge(acc0_ready, T_XO + n + 1)
                    else:
                        dve.wait_ge(w_used[n], T_XO + 1)
                    hv = h[:, c, n * NW:(n + 1) * NW]
                    V.tensor_tensor(hv, B[c], hv, ALU.add).then_inc(acc_free[c], 1)
                    dve.wait_ge(acc_free[c], T_XO + n + 2)
                    dve.sem_inc(h_done, 1)
            mean_squares(3, count=8)
            dve.wait_ge(grow_landed, 16)
            dve.wait_ge(rstd_done, 4)
            for c in range(C):
                V.scalar_tensor_tensor(out=xn3[:, c, :], in0=h[:, c, :], scalar=rstd[:, 6 + c:7 + c], in1=grow,
                                       op0=ALU.mult, op1=ALU.mult).then_inc(xn_done, 1)

            def top16(src, scratch, vals, ids):
                dve.sem_inc(dve_turns, 1)
                link(V.max(vals[:, 0:8], src))
                dve.sem_inc(dve_turns, 1)
                V.max_index(ids[:, 0:8], vals[:, 0:8], src)
                link(V.match_replace(scratch, vals[:, 0:8], src, -3.0e38))
                dve.sem_inc(dve_turns, 1)
                link(V.max(vals[:, 8:16], scratch))
                dve.sem_inc(dve_turns, 1)
                link(V.max_index(ids[:, 8:16], vals[:, 8:16], scratch))

            def route(u, src, par):
                link(V.tensor_copy(wk[:, :, :].rearrange("p t n -> p (t n)"), src))
                for t in range(2):
                    top16(wk[:, t, :], wk2[:, t * P:(t + 1) * P], top[:, t, :], topi[:, t, :])
                V.tensor_copy(topf[:, :, :], topi[:, :, :])
                link(V.tensor_tensor(cand[:, :, :], top[:, 0, :].unsqueeze(2).broadcast_to([P, PK, PK]),
                                     top[:, 1, :].unsqueeze(1).broadcast_to([P, PK, PK]), ALU.add))
                if not (isinstance(u, int) and u == 0):
                    dve.wait_ge(route_exp, u)
                top16(cand[:, :, :].rearrange("p a b -> p (a b)"), wk2[:, :], sc16, ci)
                V.tensor_scalar(nsc[:, :], sc16[:, 0:1], -1.0, None, ALU.mult).then_inc(route_scores, 1)
                V.tensor_scalar(ab[:, 0, :], ci[:, :], 4, None, ALU.logical_shift_right)
                link(V.tensor_scalar(ab[:, 1, :], ci[:, :], PK - 1, None, ALU.bitwise_and))
                link(V.tensor_copy(abf[:, :, :], ab[:, :, :]))
                for t in range(2):
                    last = V.tensor_tensor(onehot[:, t, :, :], abf[:, t, :].unsqueeze(2).broadcast_to([P, PK, PK]),
                                           iota16[:, :].unsqueeze(1).broadcast_to([P, PK, PK]), ALU.is_equal)
                link(last)
                for t in range(2):
                    last = V.tensor_tensor(onehot[:, t, :, :], onehot[:, t, :, :],
                                           topf[:, t, :].unsqueeze(1).broadcast_to([P, PK, PK]), ALU.mult)
                link(last)
                link(V.reduce_sum(e12[:, :, :].rearrange("p t k -> p (t k)"), onehot[:, :, :, :].rearrange("p t k a -> p (t k) a"), axis=AX.X))
                if not (isinstance(u, int) and u < 2):
                    dve.wait_ge(idx_v_ready, u - 1)
                V.scalar_tensor_tensor(out=idx_u[par][:, :], in0=e12[:, 0, :], scalar=float(NKEYS), in1=e12[:, 1, :],
                                       op0=ALU.mult, op1=ALU.add).then_inc(idx_ready, 1)

            def route_weights(u, par):
                dve.wait_ge(route_exp, u + 1)
                link(V.reciprocal(exs[:, 1:2], exs[:, 0:1]))
                link(V.tensor_scalar(gw[:, par, :], ex[:, :], exs[:, 1:2], None, ALU.mult))

            def dot(u, par, j):
                r = j % RING
                dve.wait_ge(u_landed[r], u * 64 + 16 * (j // RING + 1))
                dve.wait_ge(dot_done, u * 16 + (j + RING))
                V.scalar_tensor_tensor(out=product, in0=u_ring[:, r, :], scalar=1.0, in1=xn3[:, par, :], op0=ALU.mult, op1=ALU.mult,
                                       accum_out=dots[:, par, j:j + 1]).then_inc(dot_done, 1)

            def weigh(u, par):
                dve.wait_ge(gelu_done, u + 1)
                V.tensor_tensor(ga[:, par, :], act_u[:, :], gw[:, par, :], ALU.mult).then_inc(ga_ready, 1)

            def add_out(u, par):
                dve.wait_ge(v_used, u * 16 + (16 + RING))
                V.tensor_tensor(h[:, par, :], vacc, h[:, par, :], ALU.add).then_inc(vacc_free, 1)

            for hh in range(2):
                dve.wait_ge(tp_free[hh], (G_PQ + 2) // 2 + 2)
            route(0, scores[:, 0:256], 0)
            route_weights(0, 0)
            route(1, scores[:, 256:512], 1)
            route_weights(1, 1)
            for j in range(PK):
                dot(0, 0, j)
            weigh(0, 0)
            for hh in range(2):
                dve.wait_ge(tp_free[hh], (G_PQ + 14) // 2 + 2)

            def step(u, par, add, route_next):
                if add:
                    add_out(u - 2, par)
                for j in range(PK):
                    dot(u, par, j)
                    if route_next and j == 3:
                        route(u + 1, scores[:, bass.ds(u * 256 + 256, 256)], 1 - par)
                    if route_next and j == 8:
                        route_weights(u + 1, 1 - par)
                weigh(u, par)

            for par, u in ((1, 1),):
                for j in range(PK):
                    dot(u, par, j)
                    if j == 3:
                        route(2, scores[:, 512:768], 0)
                    if j == 8:
                        route_weights(2, 0)
                weigh(u, par)
            with dve.Fori(0, PH - 2) as i:
                link.loop(i, 2 * ROUTE_STEPS)
                step(i * 2 + 2, 0, True, True)
                step(i * 2 + 3, 1, True, True)
                link.end(PH - 2)
            add_out(UNITS - 4, 0)
            for j in range(PK):
                dot(UNITS - 2, 0, j)
                if j == 3:
                    route(UNITS - 1, scores[:, (UNITS - 1) * 256:UNITS * 256], 1)
                if j == 8:
                    route_weights(UNITS - 1, 1)
            weigh(UNITS - 2, 0)
            add_out(UNITS - 3, 1)
            for j in range(PK):
                dot(UNITS - 1, 1, j)
            weigh(UNITS - 1, 1)

            dve.wait_ge(gfin_landed, 16)
            for c in range(C):
                add_out(UNITS - 2 + c, c)
                n = 4 + c
                mean_squares(n, cols=1, count=9 + c)
                dve.wait_ge(rstd_done, n + 1)
                V.scalar_tensor_tensor(out=xn3[:, c, :], in0=h[:, c, :], scalar=rstd[:, 2 * n:2 * n + 1], in1=gfin,
                                       op0=ALU.mult, op1=ALU.mult).then_inc(y_done, 1)


_INS = ['x', 'mem', 'positions', 'norm_mix_g', 'w_in', 'da_lambda_q1', 'da_lambda_k1', 'da_lambda_q2', 'da_lambda_k2',
        'da_subln_g', 'nsa_cmp_pos', 'nsa_cmpk_w1', 'nsa_cmpk_w2', 'nsa_cmpv_w1', 'nsa_cmpv_w2', 'w_branch_da',
        'w_branch_nsa', 'w_out', 'norm_x_g', 'norm_mem_g', 'w_xq', 'w_xkv', 'w_xo', 'norm_ffn_g', 'peer_wq',
        'peer_keys1', 'peer_keys2', 'peer_u', 'peer_v', 'norm_final_g']


def kernel(**inputs):
    import numpy as _np
    import concourse.bacc as _bacc
    from concourse import mybir as _mybir
    from concourse.bass_utils import run_bass_kernel_spmd as _run

    nc = _bacc.Bacc("TRN2", target_bir_lowering=False, num_devices=1)
    arrays, args = {}, []
    for name in _INS:
        a = _np.ascontiguousarray(inputs[name])
        arrays[f"in_{name}_dram"] = a
        args.append(nc.dram_tensor(f"in_{name}_dram", a.shape, _mybir.dt.from_np(a.dtype), kind="ExternalInput").ap())
    args.append(nc.dram_tensor("out_dram", (1, S, D), _mybir.dt.float32, kind="ExternalOutput").ap())
    block_program(nc, *args)
    r = _run(nc, [arrays], core_ids=[0])
    return r.results[0]["out_dram"]
```

```python
import math
from contextlib import ExitStack

import numpy as np
import concourse.bass as bass
from concourse import mybir

F32 = mybir.dt.float32
U32 = mybir.dt.uint32
I32 = mybir.dt.int32
F32R = mybir.dt.float32r
ALU = mybir.AluOpType
ACT = mybir.ActivationFunctionType
AX = mybir.AxisListType

P = 128
D = 2048
S = 256
C = S // P
KT = D // P
NW = 512
PIECES = 8
KS = KT // PIECES
WR = 4
AHEAD = 3
MIX_AFTER = 2
EPS = 1e-6
NEG = -1e30

DA_H, DA_DK, DA_DV = 8, 64, 128
N_H, N_G, N_DK = 16, 4, 64
ZQ, ZK, ZV, NQ, NKV = 0, 1024, 2048, 3072, 4096
QKV_COLS = NKV + 6 * N_G * N_DK
NG_COLS = N_H * 3
BG = QKV_COLS + NG_COLS
K_CMP, V_CMP, K_SEL, V_SEL, K_WIN, V_WIN = (NKV + 256 * n for n in range(6))
ATT_SCALE = DA_DK ** -0.5
LAMBDA_INIT = 0.8 - 0.6 * math.exp(-0.3 * 0)
ROPE_HALF = 8
ROPE_INV = [float(np.float32(500000.0) ** np.float32(-2 * i / 16)) for i in range(ROPE_HALF)]

CMP_LEN, CMP_STRIDE = 32, 16
N_CMP = (S - CMP_LEN) // CMP_STRIDE + 1
X_H, X_DH = 4, 128
X_SCALE = X_DH ** -0.5

PH, PK, NKEYS = 8, 16, 128
UNITS = PH * C

T_KV, T_QKV, T_NG, T_BG, T_BR, T_WO, T_XQ, T_XO, T_PQ = 0, 2, 13, 14, 22, 26, 30, 31, 32
N_TILES = 36
N_QKV, N_BG, N_BR, N_WO, N_PQ = 11, 8, 4, 4, 4
A_PQ = T_PQ + 3

H_MEM, H_X, H_OT, H_MIX, H_X2, H_OX, H_X3 = 0, 8, 16, 24, 32, 40, 42

G_MEM, G_POS, G_KEYS, G_MK, G_X, G_CMP, G_ATT = 0, 8, 9, 10, 12, 20, 24
G_OT, G_MIX, G_X2, G_QX, G_OX, G_X3, G_PQ = 64, 72, 80, 88, 90, 92, 100
ATT_GROUPS = 10

ATT_STEPS, ROUTE_STEPS = 56, 21

LAG = 2
RING = 4

BIG = C * QKV_COLS + C * 2 * D
RES_KB = 157
MAIN_KB = RES_KB + 32

MAGIC = 12582912.0
TWO_PI_A = 6.28125
TWO_PI_B = float(np.float32(2 * math.pi - TWO_PI_A))
TWO_PI_C = float(2 * math.pi - TWO_PI_A - TWO_PI_B)
PI_IN = 3.1415925


class Chain:

    def __init__(self, eng, sem):
        self.eng, self.sem, self.n, self.var, self.per = eng, sem, 0, None, 0

    def __call__(self, ins):
        self.n += 1
        ins.then_inc(self.sem, 1)
        self.eng.wait_ge(self.sem, self.n if self.var is None else self.var * self.per + self.n)

    def loop(self, var, per):
        self.var, self.per, self.first = var, per, self.n

    def end(self, trips):
        assert self.n - self.first == self.per, (self.n - self.first, self.per)
        self.n += self.per * (trips - 1)
        self.var = None


def block_program(nc, x, mem, positions, norm_mix_g, w_in, lq1, lk1, lq2, lk2, subln_g, cmp_pos, ck1, ck2,
                  cv1, cv2, w_bda, w_bnsa, w_out, norm_x_g, norm_mem_g, w_xq, w_xkv, w_xo, norm_ffn_g,
                  peer_wq, keys1, keys2, peer_u, peer_v, norm_final_g, out):
    ctx = ExitStack()
    with ctx:
        def sb(name, shape, dt=F32):
            return ctx.enter_context(nc.sbuf_tensor(name, shape, dt))

        def sem(name):
            return ctx.enter_context(nc.semaphore(name))

        KB = 1024
        whole_map = sb("whole_map", [P, MAIN_KB * KB // 4])
        origin = nc.sbuf_base - MAIN_KB * KB

        def at_kb(name, kb, shape, dt=F32):
            return nc.alloc_sbuf_tensor_at(name, shape, dt, offset=origin + int(kb * KB))

        wraw = at_kb("wraw", 0, [P, WR, KS, NW])
        gfin = at_kb("gfin", 0, [P, D])
        ws = at_kb("ws", 16, [P, WR, 2, KS, NW], F32R)
        xr = at_kb("xr", 48, [P, 2, KT, S], F32R)
        v_ring_t = at_kb("v_ring", 48, [P, RING, D])
        v_ring = v_ring_t[:, :, :]
        big = at_kb("big", 80, [P, BIG])
        orr = at_kb("orr", RES_KB, [P, 2, KT, S], F32R)
        att = at_kb("att", RES_KB, [P, 6144])
        h = at_kb("h", RES_KB, [P, C, D])
        xn3_t = at_kb("xn3", RES_KB + 16, [P, C, D])
        xn3 = xn3_t[:, :, :]
        z = big[:, 0:C * QKV_COLS].rearrange("p (c n) -> p c n", c=C)
        gates_flat = big[:, C * QKV_COLS:]
        gates = gates_flat.rearrange("p (c n) -> p c n", c=C)
        xn = gates_flat[:, 0:C * D].rearrange("p (c d) -> p c d", c=C)
        mn = gates_flat[:, C * D:].rearrange("p (c d) -> p c d", c=C)
        w1 = gates_flat[0:64, :].rearrange("p (t l h) -> p t l h", t=2, l=CMP_LEN)
        stage_a = big[:, 1024:2048].rearrange("p (c n) -> p c n", c=C)
        gmem, gmix, square_a = (big[:, n * D:(n + 1) * D] for n in (1, 2, 3))
        raw = big[:, 4 * D:4 * D + 512].rearrange("p (t n) -> p t n", t=4)
        lam4 = big[:, 4 * D + 512:4 * D + 768].rearrange("p (t n) -> p t n", t=4)
        lamp = big[:, 4 * D + 768:4 * D + 896]
        xn2 = big[:, 0:C * D].rearrange("p (c d) -> p c d", c=C)
        square_b = big[:, 2 * D:3 * D]
        gx = big[:, 3 * D:4 * D]
        later = big[:, 4 * D:4 * D + 6144]
        product = big[:, 7 * D:8 * D]
        grow = big[:, 8 * D:9 * D]
        stage_b = big[:, 9 * D:9 * D + 1024].rearrange("p (c n) -> p c n", c=C)
        u_ring = big[:, 0:RING * D].rearrange("p (r d) -> p r d", r=RING)
        arena = att[:, :]
        rot = arena[:, 0:1024].rearrange("p (k n) -> p k n", k=4)
        xsT = arena[0:64, 0:2048].rearrange("p (t g s) -> p t g s", t=2, g=N_G)
        blk = arena[0:64, 2048:2048 + 2 * 1920].rearrange("p (t l g n) -> p t l g n", t=2, l=CMP_LEN, g=N_G)
        dT = arena[:, 0:512].rearrange("p (t s) -> p t s", t=2)
        nqT = arena[0:64, 512:1024].rearrange("p (t s) -> p t s", t=2)
        kT = arena[0:64, 1024:1536].rearrange("p (t s) -> p t s", t=2)
        Sc, Pr, at = ([m[:, f:f + 1024].rearrange("p (b n) -> p b n", b=2) for m in (arena, later)] for f in (1536, 2560, 3584))
        dqk = arena[:, 4608:5120].rearrange("p (c t n) -> p c t n", c=C, t=2)
        nqs = arena[:, 5120:5376].rearrange("p (c n) -> p c n", c=C)
        kks = arena[:, 5376:5632].rearrange("p (t c n) -> p t c n", t=2, c=C)
        pcT = arena[0:N_CMP, 5632:6144].rearrange("p (t s) -> p t s", t=2)
        qxT = later[:, 0:1024].rearrange("p (h s) -> p h s", h=X_H)
        oxr = xr[:, :, 0:X_H, :]
        ox = later[:, 4608:5632].rearrange("p (c n) -> p c n", c=C)
        scores = later[:, 0:UNITS * 256]
        qpT = later[:, 4096:5120].rearrange("p (j s) -> p j s", j=4)
        half_mix = big[:, 2048:2560]
        vmem = sb("vmem", [P, C, NW])
        kxT = sb("kxT", [P, X_H, S])
        keysT = sb("keysT", [P, 2, NKEYS])
        ident = sb("ident", [P, P])
        causal = sb("causal", [P, 2 * P])
        cm_add = sb("cm_add", [P, C, N_CMP])
        cm_mul = sb("cm_mul", [P, C, N_CMP])
        gn = sb("gn", [P, C, NG_COLS])
        posT = sb("posT", [64, CMP_LEN])
        w2 = sb("w2", [P, 2, N_DK])
        hid = sb("hid", [P, 2, N_G * N_CMP])
        kcT = sb("kcT", [64, N_G * N_CMP])
        vc = sb("vc", [N_CMP, N_G * N_DK])
        lamb = sb("lamb", [P, 8])
        subg = sb("subg", [P, DA_DV])
        pos_i = sb("pos_i", [P, C], I32)
        rope = sb("rope", [P, 6, C, ROPE_HALF])
        inv = sb("inv", [P, ROPE_HALF])
        ssq = sb("ssq", [P, 12])
        msq = sb("msq", [P, 12])
        rstd = sb("rstd", [P, 12])
        nhalf = sb("nhalf", [P, 16])
        ms2 = sb("ms2", [P, 3, 2])
        mx = sb("mx", [P, 2, 2])
        nmx = sb("nmx", [P, 2, 2])
        sums = sb("sums", [P, 6, 4])
        rec = sb("rec", [P, 8])
        coef = sb("coef", [P, 4])
        tmp3 = sb("tmp3", [P, 3 * N_DK])
        cs = sb("cs", [P, C, 2, N_CMP])
        cmx = sb("cmx", [P, 4])
        csum = sb("csum", [P, 4])
        vmem_flat = vmem[:, :, :].rearrange("p c n -> p (c n)")
        kxT_flat = kxT[:, :, :].rearrange("p h s -> p (h s)")
        wk = vmem_flat[:, 0:256].rearrange("p (t n) -> p t n", t=2)
        wk2 = vmem_flat[:, 256:512]
        top = sb("top", [P, 2, PK])
        topi = sb("topi", [P, 2, PK], U32)
        topf = sb("topf", [P, 2, PK])
        cand = vmem_flat[:, 512:768].rearrange("p (a b) -> p a b", a=PK)
        sc16 = sb("sc16", [P, PK])
        ci = sb("ci", [P, PK], U32)
        ab = sb("ab", [P, 2, PK], U32)
        abf = sb("abf", [P, 2, PK])
        onehot = kxT_flat[:, 0:512].rearrange("p (t k a) -> p t k a", t=2, k=PK)
        e12 = sb("e12", [P, 2, PK])
        iota16 = sb("iota16", [P, PK])
        idx_u = [sb(f"idx_u{i}", [P, PK], U32) for i in range(2)]
        idx_v = [sb(f"idx_v{i}", [P, PK], U32) for i in range(2)]
        nsc = sb("nsc", [P, 1])
        ex = sb("ex", [P, PK])
        exs = sb("exs", [P, 2])
        gw = sb("gw", [P, 2, PK])
        dots = sb("dots", [P, 2, PK])
        act_u = sb("act_u", [P, PK])
        ga = sb("ga", [P, 2, PK])
        diag = kxT_flat[:, 512:1024].rearrange("p (r q) -> p r q", r=RING)

        psum = ctx.enter_context(nc.psum_tensor("banks", [P, 8 * NW], F32))
        B = [psum[:, n * NW:(n + 1) * NW] for n in range(8)]
        vacc = psum[:, 4 * NW:8 * NW]

        mem_landed = [sem(f"mem_landed{c}") for c in range(C)]
        x_landed, small_landed, w1_landed, gmem_landed, gmix_landed, gx_landed, h_landed = map(sem, (
            "x_landed", "small_landed", "w1_landed", "gmem_landed", "gmix_landed", "gx_landed", "h_landed"))
        grow_landed, gfin_landed, out_landed = map(sem, ("grow_landed", "gfin_landed", "out_landed"))
        w_landed = [sem(f"w_landed{r}") for r in range(WR)]
        w_hi, w_split, w_used = sem("w_hi"), sem("w_split"), sem("w_used")
        hi_done = sem("hi_done")
        acc0_ready = sem("acc0_ready")
        nacc0_ready = sem("nacc0_ready")
        acc_free = [sem(f"acc_free{c}") for c in range(C)]
        nacc_free = [sem(f"nacc_free{c}") for c in range(C)]
        tp_ready = [sem(f"tp_ready{b}") for b in range(2)]
        tp_free = [sem(f"tp_free{b}") for b in range(2)]
        consts_ready, sq_done, ms_done, rstd_done, xn_done = map(sem, ("consts_ready", "sq_done", "ms_done", "rstd_done", "xn_done"))
        dve_steps, act_steps, pool_steps = map(sem, ("dve_steps", "act_steps", "pool_steps"))
        angle_ready, sin_done, ng_ready, gn_tanh, gn_done, rope_done = map(sem, ("angle_ready", "sin_done", "ng_ready", "gn_tanh", "gn_done", "rope_done"))
        lam_in, lam_exp = sem("lam_in"), sem("lam_exp")
        blk_ready, hid_ready, hid_done, cmp_ready, cmp_done = map(sem, ("blk_ready", "hid_ready", "hid_done", "cmp_ready", "cmp_done"))
        staged, sc_ready, sc_free, nm_ready, exp_done = map(sem, ("staged", "sc_ready", "sc_free", "nm_ready", "exp_done"))
        da_ready, pt_ready, at_ready, pv_ready, ev_done = map(sem, ("da_ready", "pt_ready", "at_ready", "pv_ready", "ev_done"))
        map0_done = sem("map0_done")
        cm_ready, cexp_done, cp_ready = map(sem, ("cm_ready", "cexp_done", "cp_ready"))
        subln_sq, subln_ms, subln_rstd, subln_done, mix_ready, h_done = map(sem, ("subln_sq", "subln_ms", "subln_rstd", "subln_done", "mix_ready", "h_done"))
        idx_ready, idx_v_ready = map(sem, ("idx_ready", "idx_v_ready"))
        pool_turns, pe_turns, dve_turns = map(sem, ("pool_turns", "pe_turns", "dve_turns"))
        u_landed = [sem(f"u_landed{r}") for r in range(RING)]
        v_landed = [sem(f"v_landed{r}") for r in range(RING)]
        dot_done, v_used, route_scores, route_exp, gelu_done, ga_ready, diag_ready, vacc_free, y_done = map(
            sem, ("dot_done", "v_used", "route_scores", "route_exp", "gelu_done", "ga_ready", "diag_ready", "vacc_free", "y_done"))

        x_v = x[0].rearrange("(c p) d -> p c d", p=P)
        mem_v = mem[0].rearrange("(c p) d -> p c d", p=P)
        out_v = out[0].rearrange("(c p) d -> p c d", p=P)
        N_SMALL = 12

        def pieces_of(m):
            return m.rearrange("(s k p) n -> s p k n", k=KS, p=P)

        block = ctx.enter_context(nc.Block())

        @block.sync
        def _(sp):
            for c in range(C):
                sp.dma_start(mn[:, c, :], mem_v[:, c, :]).then_inc(mem_landed[c], 16)
            sp.dma_start(gmem, norm_mem_g[0].partition_broadcast(P)).then_inc(gmem_landed, 16)

            def load(n, tile, src, cols=NW):
                sp.wait_ge(w_split, tile * PIECES + (n + 1))
                sp.dma_start(wraw[:, n % WR, :, 0:cols], src).then_inc(w_landed[n % WR], 16)

            kv, wi = pieces_of(w_xkv[0]), pieces_of(w_in[0])
            for t in range(2):
                for n in range(PIECES):
                    load(n, T_KV + t, kv[n][:, :, t * NW:(t + 1) * NW])
                    if t == 0 and n == WR - 1:
                        sp.dma_start(xn, x_v).then_inc(x_landed, 16)
                        sp.dma_start(gmix, norm_mix_g[0].partition_broadcast(P)).then_inc(gmix_landed, 16)
            with sp.Fori(0, N_QKV) as i:
                for n in range(PIECES):
                    load(n, i + T_QKV, wi[n][:, :, bass.ds(i * NW, NW)])
            for n in range(PIECES):
                load(n, T_NG, wi[n][:, :, QKV_COLS:BG], NG_COLS)
            for b in range(2):
                sp.wait_ge(tp_ready[b], (G_CMP - 2 + b) // 2 + 1)
            for t, m in enumerate((ck1, cv1)):
                sp.dma_start(w1[:, t, :, :], m[0].rearrange("(l d) h -> d l h", d=64)).then_inc(w1_landed, 16)
            with sp.Fori(0, N_BG) as i:
                for n in range(PIECES):
                    load(n, i + T_BG, wi[n][:, :, bass.ds(i * NW + BG, NW)])
            br = (pieces_of(w_bda[0]), pieces_of(w_bnsa[0]))
            with sp.Fori(0, N_BR) as i:
                for n in range(PIECES):
                    load(n, i + T_BR, br[n // 4][n % 4][:, :, bass.ds(i * NW, NW)])
            wo = pieces_of(w_out[0])
            for n in range(WR):
                load(n, T_WO, wo[n][:, :, 0:NW])
            sp.wait_ge(w_used, T_WO * PIECES + WR)
            sp.dma_start(h[:, :, :], x_v).then_inc(h_landed, 16)
            for n in range(WR, PIECES):
                load(n, T_WO, wo[n][:, :, 0:NW])
            with sp.Fori(1, N_WO) as i:
                for n in range(PIECES):
                    load(n, i + T_WO, wo[n][:, :, bass.ds(i * NW, NW)])
            for b in range(2):
                sp.wait_ge(tp_ready[b], (G_X2 - 2 + b) // 2 + 1)
            sp.dma_start(gx, norm_x_g[0].partition_broadcast(P)).then_inc(gx_landed, 16)
            sp.dma_start(grow, norm_ffn_g[0].partition_broadcast(P)).then_inc(grow_landed, 16)
            xq, xo = pieces_of(w_xq[0]), pieces_of(w_xo[0])
            for n in range(PIECES):
                load(n, T_XQ, xq[n])
            for n in range(PIECES):
                load(n, T_XO, xo[n % 2][:, :, n // 2 * NW:(n // 2 + 1) * NW])
            pq = pieces_of(peer_wq[0])
            with sp.Fori(0, N_PQ) as i:
                for n in range(PIECES):
                    load(n, i + T_PQ, pq[n][:, :, bass.ds(i * NW, NW)])
            sp.wait_ge(w_split, N_TILES * PIECES + WR)
            sp.dma_start(gfin[:, :], norm_final_g.partition_broadcast(P)).then_inc(gfin_landed, 16)
            for c in range(C):
                sp.wait_ge(y_done, c + 1)
                sp.dma_start(out_v[:, c, :], xn3[:, c, :]).then_inc(out_landed, 16)
            sp.wait_ge(out_landed, 16 * C)

        @block.gpsimd
        def _(pool):
            link = Chain(pool, pool_steps)
            link(nc.gpsimd.memset(ident[:, :], 0.0))
            nc.gpsimd.affine_select(out=ident[:, :], in_=ident[:, :], compare_op=ALU.not_equal, fill=1.0, base=0,
                                    pattern=[[-1, P]], channel_multiplier=1).then_inc(consts_ready, 1)
            nc.gpsimd.memset(nhalf[:, :], -0.5).then_inc(consts_ready, 1)
            link(nc.gpsimd.memset(causal[:, :], 0.0))
            nc.gpsimd.affine_select(out=causal[:, :], in_=causal[:, :], compare_op=ALU.is_ge, fill=NEG, base=P,
                                    pattern=[[-1, 2 * P]], channel_multiplier=1).then_inc(consts_ready, 1)
            link(nc.gpsimd.memset(cm_add[:, :, :], 0.0))
            link(nc.gpsimd.memset(cm_mul[:, :, :], 1.0))
            for m, fill in ((cm_add, NEG), (cm_mul, 0.0)):
                nc.gpsimd.affine_select(out=m[:, :, :], in_=m[:, :, :], compare_op=ALU.is_ge, fill=fill,
                                        base=-(CMP_LEN - 1), pattern=[[P, C], [-CMP_STRIDE, N_CMP]],
                                        channel_multiplier=1).then_inc(consts_ready, 1)
            nc.gpsimd.iota(iota16[:, :], pattern=[[1, PK]], base=0, channel_multiplier=0,
                           allow_small_or_imprecise_dtypes=True).then_inc(consts_ready, 1)

            def rsqrt(n, cols=C):
                pool.wait_ge(ms_done, n + 1)
                nc.gpsimd.tensor_tensor(rstd[:, 2 * n:2 * n + cols], msq[:, 2 * n:2 * n + cols], nhalf[:, 0:cols],
                                        ALU.pow).then_inc(rstd_done, 1)

            pool.wait_ge(consts_ready, 6)
            rsqrt(0)
            rsqrt(1)
            pool.wait_ge(rope_done, 1)
            pool.wait_ge(cmp_done, 1)
            with pool.Fori(0, N_G) as g:
                for j in range(2):
                    last_q = (11, 14)[j]
                    pool.wait_ge(tp_ready[0], g * 5 + last_q - (1 if j else 0))
                    pool.sem_inc(pool_turns, 1)
                    nc.gpsimd.tensor_copy(dqk[:, :, 0, :], z[:, :, bass.ds(g * 256 + (ZQ + 128 * j), 128)])
                    nc.gpsimd.tensor_copy(dqk[:, :, 1, :], z[:, :, bass.ds(g * 256 + (ZK + 128 * j), 128)]).then_inc(staged, 1)
                    pool.wait_ge(tp_ready[1], g * 5 + last_q - (1 if j else 0))
                    pool.sem_inc(pool_turns, 1)
                    nc.gpsimd.tensor_copy(nqs[:, :, :], z[:, :, bass.ds(g * 256 + (NQ + 128 * j), 128)]).then_inc(staged, 1)
                    if j == 0:
                        nc.gpsimd.tensor_copy(kks[:, 0, :, :], z[:, :, bass.ds(g * 64 + K_SEL, 64)])
                        nc.gpsimd.tensor_copy(kks[:, 1, :, :], z[:, :, bass.ds(g * 64 + K_WIN, 64)]).then_inc(staged, 1)
                    pool.wait_ge(subln_ms, g * 2 + j + 1)
                    nc.gpsimd.tensor_tensor(ms2[:, 2, :], ms2[:, 1, :], nhalf[:, 0:C], ALU.pow).then_inc(subln_rstd, 1)
            rsqrt(2)
            rsqrt(3)

            def step(par, has_u, has_v, u):
                if has_v:
                    if not (isinstance(u, int) and u == 1):
                        pool.wait_ge(v_used, u * 16 + (RING - 32))
                        pool.sem_inc(pool_turns, 1)
                    nc.gpsimd.tensor_copy(idx_v[1 - par][:, :], idx_u[1 - par][:, :]).then_inc(idx_v_ready, 1)
                    pool.wait_ge(idx_v_ready, u)
                    pool.sem_inc(pool_turns, 1)
                if has_u:
                    pool.wait_ge(idx_ready, u + 1)
                    pool.sem_inc(pool_turns, 1)
                for j in range(PK):
                    r = j % RING
                    if has_u:
                        pool.wait_ge(dot_done, u * 16 + (j + 1))
                        pool.sem_inc(pool_turns, 1)
                        nc.gpsimd.indirect_dma_start(u_ring[:, r, :], None, peer_u[0],
                                                     bass.IndirectOffsetOnAxis(ap=idx_u[par][:, j:j + 1], axis=0)).then_inc(u_landed[r], 16)
                    if has_v:
                        pool.wait_ge(v_used, u * 16 + (j + 1 - 16))
                        pool.sem_inc(pool_turns, 1)
                        nc.gpsimd.indirect_dma_start(v_ring[:, r, :], None, peer_v[0],
                                                     bass.IndirectOffsetOnAxis(ap=idx_v[1 - par][:, j:j + 1], axis=0)).then_inc(v_landed[r], 16)

            step(0, True, False, 0)
            pool.wait_ge(w_used, N_TILES * PIECES + WR)
            step(1, True, True, 1)
            with pool.Fori(0, PH - 1) as i:
                step(0, True, True, i * 2 + 2)
                step(1, True, True, i * 2 + 3)
            step(0, False, True, UNITS)
            rsqrt(4, 1)
            rsqrt(5, 1)

        @block.tensor
        def _(pe):
            def tp_begin(n, g=None):
                if g is None:
                    pe.wait_ge(tp_free[n % 2], n // 2 + 1)
                else:
                    pe.wait_ge(tp_free[n % 2], g * (ATT_GROUPS // 2) + (G_ATT // 2 + n // 2 + 1))
                return B[2 + n % 2]

            def evacuated(n, g=None):
                if g is None:
                    pe.wait_ge(tp_free[n % 2], n // 2 + 2)
                else:
                    pe.wait_ge(tp_free[n % 2], g * (ATT_GROUPS // 2) + (G_ATT // 2 + n // 2 + 2))

            def transposes(n, tiles, g=None):
                bank = tp_begin(n, g)
                pe.sem_inc(pe_turns, 1)
                for src, col in tiles:
                    p, m = src.shape
                    last = nc.tensor.transpose(bank[0:m, col:col + p], src, ident[0:p, 0:p])
                last.then_inc(tp_ready[n % 2], 1)

            def part(tile, acc, n, lhs, bank=0, first=0, final=PIECES - 1, cols=NW):
                pe.wait_ge(w_split, tile * PIECES + (n + 1 + WR))
                for c in range(C):
                    if n == first:
                        pe.wait_ge((acc_free if bank == 0 else nacc_free)[c], acc + 1)
                    for k in range(KS):
                        hi, lo = (lhs[:, t, (n - first) * KS + k, c * P:(c + 1) * P] for t in range(2))
                        w_h, w_l = (ws[:, n % WR, t, k, 0:cols] for t in range(2))
                        dst = B[bank + c][:, 0:cols]
                        nc.tensor.matmul(dst, hi, w_h, start=(n == first and k == 0), stop=False)
                        nc.tensor.matmul(dst, hi, w_l, start=False, stop=False)
                        last = nc.tensor.matmul(dst, lo, w_h, start=False, stop=(n == final and k == KS - 1))
                    if c == C - 1:
                        last.then_inc(w_used, 1)
                    elif n == final:
                        last.then_inc(acc0_ready if bank == 0 else nacc0_ready, 1)

            def whole(tile, lhs, acc=None, cols=NW):
                for n in range(PIECES):
                    part(tile, tile if acc is None else acc, n, lhs, cols=cols)

            def norm_groups(base, src, norm):
                for c in range(C):
                    pe.wait_ge(xn_done, C * norm + c + 1)
                    for q in range(4):
                        transposes(base + 4 * c + q, [(src[:, c, (4 * q + t) * P:(4 * q + t + 1) * P], t * P) for t in range(4)])

            pe.wait_ge(consts_ready, 1)
            norm_groups(G_MEM, mn, 0)
            pe.wait_ge(small_landed, 16 * N_SMALL)
            transposes(G_POS, [(raw[0:CMP_LEN, 1, 0:64], 0)])
            transposes(G_KEYS, [(raw[:, 2, :], 0), (raw[:, 3, :], P)])
            for n in range(8):
                evacuated(G_MEM + n)
            for n in range(2):
                whole(T_KV + n, orr)
            pe.wait_ge(act_steps, 2)
            for c in range(C):
                transposes(G_MK + c, [(stage_a[:, c, t * P:(t + 1) * P], t * P) for t in range(X_H)])
            norm_groups(G_X, xn, 1)
            for n in range(8):
                evacuated(G_X + n)
            with pe.Fori(0, N_QKV) as i:
                whole(i + T_QKV, xr)
            whole(T_NG, xr, cols=NG_COLS)
            pe.wait_ge(rope_done, 1)
            for t, base in enumerate((K_CMP, V_CMP)):
                for c in range(C):
                    transposes(G_CMP + 2 * t + c, [(z[:, c, base + g * 64:base + g * 64 + 64], g * P) for g in range(N_G)])
            pe.wait_ge(w1_landed, 32)
            pe.wait_ge(blk_ready, 2)
            for t in range(2):
                for l in range(CMP_LEN):
                    last = nc.tensor.matmul(B[5 + t][:, 0:60], w1[:, t, l, :], blk[:, t, l, :, :].rearrange("p g n -> p (g n)"),
                                            start=(l == 0), stop=(l == CMP_LEN - 1))
                last.then_inc(hid_ready, 1)
            pe.wait_ge(hid_done, 2)
            nc.tensor.matmul(B[7][0:64, 0:60], w2[:, 0, :], hid[:, 0, :], start=True, stop=True)
            for g in range(N_G):
                last = nc.tensor.matmul(B[7][0:N_CMP, 64 + g * 64:128 + g * 64], hid[:, 1, g * N_CMP:(g + 1) * N_CMP],
                                        w2[:, 1, :], start=True, stop=True)
            last.then_inc(cmp_ready, 1)

            pe.wait_ge(cmp_done, 2)
            pe.wait_ge(gn_done, 1)

            def score(U, u, c, pairs, apart=None):
                pe.wait_ge(sc_free, U + 1)
                nk = pairs[0][1].shape[-1]
                for m, (q, k) in enumerate(pairs):
                    last = nc.tensor.matmul(B[4 + u % 2][:, m * nk:(m + 1) * nk], q, k, start=True, stop=True)
                    if apart is not None and m == 0:
                        last.then_inc(map0_done, 1)
                        pe.wait_ge(map0_done, apart)
                last.then_inc(sc_ready, 1)

            def probs_T(U, u, nt, wait, value, x=0):
                pe.wait_ge(wait, value)
                pe.wait_ge(at_ready, U + 1)
                for t in range(nt):
                    last = nc.tensor.transpose(B[6][:, t * P:(t + 1) * P], Pr[x][:, u % 2, t * P:(t + 1) * P], ident[:, :])
                last.then_inc(pt_ready, 1)

            def values(U, products):
                pe.wait_ge(at_ready, U + 2)
                pe.wait_ge(ev_done, U + 1)
                pe.sem_inc(pe_turns, 1)
                for dst, terms in products:
                    for n, (a, v) in enumerate(terms):
                        last = nc.tensor.matmul(dst, a, v, start=(n == 0), stop=(n == len(terms) - 1))
                last.then_inc(pv_ready, 1)

            with pe.Fori(0, N_G) as g:
                for j in range(2):
                    T1, T2, CS, TC = ((0, 1, 4, 5), (6, 7, 8, 9))[j]
                    step = g * 2 + j
                    U = [g * 12 + (6 * j + u) for u in range(6)]

                    def fill(n):
                        part(step + T_BG, step + T_BG, n, xr)

                    def S_(u):
                        c = u % 2
                        nk = (c + 1) * P
                        if u < 2:
                            score(U[u], u, c, [(dT[64 * m:64 * m + 64, 0, c * P:(c + 1) * P], dT[64 * m:64 * m + 64, 1, 0:nk]) for m in range(2)],
                                  step * 2 + (c + 1))
                        else:
                            score(U[u], u, c, [(nqT[:, u // 2 - 1, c * P:(c + 1) * P], kT[:, m, 0:nk]) for m in range(2)])

                    def TP(u):
                        c = u % 2
                        if u < 2:
                            probs_T(U[u], u, c + 1, da_ready, step * 2 + (c + 1))
                        else:
                            probs_T(U[u], u, 2 * (c + 1), exp_done, U[u] + 1 + LAG)

                    def PV(u):
                        c = u % 2
                        a = at[0][:, u % 2, :]
                        kcs = range(c + 1)
                        if u < 2:
                            values(U[u], [(B[7][:, 0:P], [(a[:, kc * P:(kc + 1) * P], z[:, kc, bass.ds(g * 256 + (ZV + 128 * j), 128)]) for kc in kcs])])
                        else:
                            if u == 2:
                                evacuated(TC, g)
                            values(U[u], [
                                (B[7][:, 0:64], [(pcT[:, u // 2 - 1, c * P:(c + 1) * P], vc[:, bass.ds(g * 64, 64)])]),
                                (B[7][:, 64:128], [(a[:, kc * P:(kc + 1) * P], z[:, kc, bass.ds(g * 64 + V_SEL, 64)]) for kc in kcs]),
                                (B[7][:, 128:192], [(a[:, (c + 1 + kc) * P:(c + 2 + kc) * P], z[:, kc, bass.ds(g * 64 + V_WIN, 64)]) for kc in kcs])])

                    pe.wait_ge(staged, g * 5 + (1, 4)[j])
                    transposes(T1, [(dqk[:, c, t, :], (2 * t + c) * P) for t in range(2) for c in range(C)], g)
                    pe.wait_ge(staged, g * 5 + (2, 5)[j])
                    transposes(T2, [(nqs[:, c, t * 64:(t + 1) * 64], (2 * t + c) * P) for t in range(2) for c in range(C)], g)
                    if j == 0:
                        pe.wait_ge(staged, g * 5 + 3)
                        for t in range(2):
                            transposes(2 + t, [(kks[:, t, c, :], c * P) for c in range(C)], g)
                    fill(0)
                    evacuated(T1, g)
                    S_(0), S_(1)
                    evacuated(T2, g)
                    if j == 0:
                        evacuated(2, g)
                        evacuated(3, g)
                    bank = tp_begin(CS, g)
                    pe.sem_inc(pe_turns, 1)
                    for c in range(C):
                        for t in range(2):
                            last = nc.tensor.matmul(bank[:, (2 * c + t) * N_CMP:(2 * c + t + 1) * N_CMP],
                                                    nqT[:, t, c * P:(c + 1) * P], kcT[:, bass.ds(g * N_CMP, N_CMP)],
                                                    start=True, stop=True)
                    last.then_inc(tp_ready[CS % 2], 1)
                    fill(1)
                    TP(0), S_(2)
                    fill(2)
                    PV(0), TP(1), S_(3)
                    fill(3)
                    PV(1), TP(2), S_(4)
                    fill(4)
                    pe.wait_ge(cp_ready, step + 1)
                    transposes(TC, [(cs[:, c, t, :], (2 * t + c) * P) for t in range(2) for c in range(C)], g)
                    TP(3), S_(5), PV(2)
                    fill(5)
                    PV(3), TP(4)
                    fill(6)
                    PV(4), TP(5)
                    fill(7)
                    PV(5)

            pe.wait_ge(ev_done, 48 + 1)
            pe.wait_ge(sc_free, 48 + LAG)
            for n in range(4):
                c, hf = n // 2, n % 2
                transposes(G_OT + n, [(z[:, c, NQ + (4 * hf + t) * P:NQ + (4 * hf + t + 1) * P], t * P) for t in range(4)])
            for n in range(4):
                c, hf = n // 2, n % 2
                if n == 0:
                    pe.wait_ge(subln_done, C * DA_H)
                transposes(G_OT + 4 + n, [(z[:, c, ZQ + (4 * hf + t) * P:ZQ + (4 * hf + t + 1) * P], t * P) for t in range(4)])
            for n in range(8):
                evacuated(G_OT + n)

            def branch_part(i, n):
                if n < 4:
                    part(i + T_BR, i + T_BR, n, orr[:, :, 0:8, :], final=3)
                else:
                    part(i + T_BR, i, n, orr[:, :, 8:16, :], bank=4, first=4)

            def mix_transposes(i):
                for c in range(C):
                    pe.wait_ge(mix_ready, i * 2 + (c + 1))
                    pe.wait_ge(tp_free[c], i + (G_MIX // 2 + 1))
                    for t in range(4):
                        last = nc.tensor.transpose(B[2 + c][:, t * P:(t + 1) * P], stage_a[:, c, t * P:(t + 1) * P], ident[:, :])
                    last.then_inc(tp_ready[c], 1)

            for n in range(PIECES):
                branch_part(0, n)
            with pe.Fori(1, N_BR) as i:
                for n in range(PIECES):
                    if n == MIX_AFTER:
                        mix_transposes(i - 1)
                    branch_part(i, n)
            for n in range(PIECES):
                if n == MIX_AFTER:
                    mix_transposes(N_BR - 1)
                if n == PIECES - KS:
                    for b in range(2):
                        evacuated(G_X2 - 2 + b)
                part(T_WO, T_WO, n, xr)
            with pe.Fori(1, N_WO) as i:
                whole(i + T_WO, xr)

            norm_groups(G_X2, xn2, 2)
            for n in range(8):
                evacuated(G_X2 + n)
            whole(T_XQ, xr)
            pe.wait_ge(act_steps, 6)
            for c in range(C):
                transposes(G_QX + c, [(stage_b[:, c, t * P:(t + 1) * P], t * P) for t in range(X_H)])
            for c in range(C):
                evacuated(G_QX + c)
                pe.wait_ge(nacc_free[c], 1 + N_BR)

            def XS(v):
                c, hp = v // 2, v % 2
                score(48 + v, v, c, [(qxT[:, 2 * hp + m, c * P:(c + 1) * P], kxT[:, 2 * hp + m, :]) for m in range(2)])

            def XT(v):
                probs_T(48 + v, v, 4, exp_done, 48 + v + 1 + LAG, 1)

            def XV(v):
                hp, a = v % 2, at[1][:, v % 2, :]
                values(48 + v, [(B[7][:, m * P:(m + 1) * P],
                                 [(a[:, (2 * m + kc) * P:(2 * m + kc + 1) * P], vmem[:, kc, (2 * hp + m) * P:(2 * hp + m + 1) * P]) for kc in range(2)])
                                for m in range(2)])

            XS(0), XS(1), XT(0), XS(2), XT(1), XV(0), XS(3), XT(2), XV(1), XT(3), XV(2), XV(3)
            for c in range(C):
                pe.wait_ge(ev_done, 48 + 2 * c + 2 + 1)
                transposes(G_OX + c, [(ox[:, c, t * P:(t + 1) * P], t * P) for t in range(X_H)])
            for c in range(C):
                evacuated(G_OX + c)
            for n in range(PIECES):
                part(T_XO, T_XO + n // 2, n, oxr, first=n // 2 * 2, final=n // 2 * 2 + 1)

            norm_groups(G_X3, xn3, 3)
            for n in range(8):
                evacuated(G_X3 + n)
            with pe.Fori(0, N_PQ) as i:
                whole(i + T_PQ, xr, i + A_PQ)
                for c in range(C):
                    pe.wait_ge(act_steps, i * 2 + (6 + c + 1))
                    pe.wait_ge(tp_free[c], i * 2 + (G_PQ // 2 + 1))
                    for t in range(4):
                        last = nc.tensor.transpose(B[2 + c][:, t * P:(t + 1) * P], stage_b[:, c, t * P:(t + 1) * P], ident[:, :])
                    last.then_inc(tp_ready[c], 1)
                for c in range(C):
                    pe.wait_ge(tp_free[c], i * 2 + (G_PQ // 2 + 2))
                for hh in range(2):
                    for c in range(C):
                        for half in range(2):
                            last = nc.tensor.matmul(B[2 + hh][:, (2 * c + half) * P:(2 * c + half + 1) * P],
                                                    qpT[:, 2 * hh + half, c * P:(c + 1) * P], keysT[:, half, :],
                                                    start=True, stop=True)
                    last.then_inc(tp_ready[hh], 1)

            def v_step(u):
                pe.wait_ge(vacc_free, u + 1)
                for j in range(PK):
                    r = j % RING
                    pe.wait_ge(v_landed[r], u * 64 + 16 * (j // RING + 1))
                    pe.wait_ge(diag_ready, u * 16 + (j + 1))
                    for n in range(4):
                        last = nc.tensor.matmul(B[4 + n], diag[:, r, :], v_ring[:, r, n * NW:(n + 1) * NW],
                                                start=(j == 0), stop=(j == PK - 1))
                    last.then_inc(v_used, 1)

            with pe.Fori(0, UNITS) as i:
                v_step(i)

        @block.scalar
        def _(act):
            A = nc.scalar.activation
            for q in (tp_free[0], tp_free[1], acc_free[0], acc_free[1], at_ready):
                act.sem_inc(q, 1)
            act.sem_inc(exp_done, LAG)
            act.sem_inc(w_split, WR)
            act.sem_inc(w_used, WR)

            smalls = [(raw[0:CMP_LEN, 1, 0:64], cmp_pos[0]),
                      (raw[:, 2, :], keys1[0]), (raw[:, 3, :], keys2[0]),
                      (w2[:, 0, :], ck2[0]), (w2[:, 1, :], cv2[0]),
                      (lam4[:, 0, :], lq1[0].partition_broadcast(P)), (lam4[:, 1, :], lk1[0].partition_broadcast(P)),
                      (lam4[:, 2, :], lq2[0].partition_broadcast(P)), (lam4[:, 3, :], lk2[0].partition_broadcast(P)),
                      (subg[:, :], subln_g[0].partition_broadcast(P)),
                      (pos_i[:, 0:1], positions[0, 0:P].rearrange("(p o) -> p o", o=1)),
                      (pos_i[:, 1:2], positions[0, P:S].rearrange("(p o) -> p o", o=1))]
            assert len(smalls) == N_SMALL
            for dst, src in smalls:
                act.dma_start(dst, src).then_inc(small_landed, 16)

            def squares(n, c, src, junk):
                done = min(2 * n, 8) + (n == 5) + c
                if done:
                    act.wait_ge(sq_done, done)
                A(junk, src, ACT.Square, accum_out=ssq[:, 2 * n + c:2 * n + c + 1]).then_inc(sq_done, 1)

            def hi(n, tile, cols=NW):
                q = n + AHEAD
                act.wait_ge(w_landed[q % WR], tile * (16 * PIECES // WR) + 16 * (q // WR + 1))
                act.wait_ge(w_used, tile * PIECES + (q + 1))
                A(ws[:, q % WR, 0, :, 0:cols], wraw[:, q % WR, :, 0:cols], ACT.Copy).then_inc(w_hi, 1)

            def next_cols(n, cols, following):
                return cols if n + AHEAD < PIECES else following

            for c in range(C):
                act.wait_ge(mem_landed[c], 16)
                squares(0, c, mn[:, c, :], square_a)
            for n in range(-AHEAD, 0):
                hi(n, 0)

            def evac_hi(n, number, dst):
                act.wait_ge(tp_ready[n % 2], n // 2 + 1)
                A(dst, four(n), ACT.Copy).then_inc(hi_done, 1)

            def four(n):
                return B[2 + n % 2].rearrange("p (t s) -> p t s", t=4)

            for c in range(C):
                for q in range(4):
                    evac_hi(G_MEM + 4 * c + q, H_MEM + 4 * c + q, orr[:, 0, 4 * q:4 * q + 4, c * P:(c + 1) * P])
            act.wait_ge(x_landed, 16)
            for c in range(C):
                squares(1, c, xn[:, c, :], square_a)
            act.wait_ge(angle_ready, 1)
            A(rope[:, 4, :, :], rope[:, 2, :, :], ACT.Sin)
            A(rope[:, 5, :, :], rope[:, 3, :, :], ACT.Sin).then_inc(sin_done, 1)

            def evac_acc(c, tile, acc, dst, signal):
                if c == 0:
                    act.wait_ge(acc0_ready, acc + 1)
                else:
                    act.wait_ge(w_used, tile * PIECES + (PIECES + WR))

            def copy_acc(c, tile, acc, dst):
                evac_acc(c, tile, acc, dst, None)
                A(dst, B[c], ACT.Copy).then_inc(acc_free[c], 1)

            def evac(n, dst, src, g=None):
                act.wait_ge(tp_ready[n % 2], n // 2 + 1 if g is None else g * (ATT_GROUPS // 2) + (G_ATT // 2 + n // 2 + 1))
                A(dst, src, ACT.Copy).then_inc(tp_free[n % 2], 1)

            for n, dst in enumerate((stage_a, vmem)):
                for k in range(PIECES):
                    hi(k, T_KV + n)
                for c in range(C):
                    copy_acc(c, T_KV + n, T_KV + n, dst[:, c, :])
                if n == 0:
                    for c in range(C):
                        act.wait_ge(acc_free[c], 2)
                        act.sem_inc(act_steps, 1)
            for c in range(C):
                evac(G_MK + c, kxT[:, :, c * P:(c + 1) * P], four(G_MK + c))
            for c in range(C):
                for q in range(4):
                    evac_hi(G_X + 4 * c + q, H_X + 4 * c + q, xr[:, 0, 4 * q:4 * q + 4, c * P:(c + 1) * P])
            with act.Fori(0, N_QKV - 1) as i:
                for n in range(PIECES):
                    hi(n, i + T_QKV)
                for c in range(C):
                    copy_acc(c, i + T_QKV, i + T_QKV, z[:, c, bass.ds(i * NW, NW)])
            last = N_QKV - 1
            for n in range(PIECES):
                hi(n, T_QKV + last, next_cols(n, NW, NG_COLS))
            for c in range(C):
                copy_acc(c, T_QKV + last, T_QKV + last, z[:, c, last * NW:(last + 1) * NW])
            for n in range(PIECES):
                hi(n, T_NG, next_cols(n, NG_COLS, NW))
            for c in range(C):
                evac_acc(c, T_NG, T_NG, None, None)
                A(gn[:, c, :], B[c][:, 0:NG_COLS], ACT.Tanh, scale=0.5).then_inc(acc_free[c], 1)
            act.wait_ge(lam_in, 1)
            A(lamb[:, 2:4], lamb[:, 0:2], ACT.Exp).then_inc(lam_exp, 1)
            for t in range(2):
                for c in range(C):
                    n = G_CMP + 2 * t + c
                    evac(n, xsT[:, t, :, c * P:(c + 1) * P], four(n)[0:64])
            for t in range(2):
                act.wait_ge(hid_ready, t + 1)
                A(hid[:, t, :], B[5 + t][:, 0:60], ACT.Gelu).then_inc(hid_done, 1)
            act.wait_ge(cmp_ready, 1)
            A(kcT[:, :], B[7][0:64, 0:60], ACT.Copy).then_inc(cmp_done, 1)
            A(vc[:, :], B[7][0:N_CMP, 64:320], ACT.Copy).then_inc(cmp_done, 1)

            def exps(U, u, nk, x=0):
                act.wait_ge(nm_ready, U + 1)
                act.wait_ge(pt_ready, U + 1)
                for m in range(2):
                    last = A(Pr[x][:, u % 2, m * nk:(m + 1) * nk], Sc[x][:, u % 2, m * nk:(m + 1) * nk], ACT.Exp,
                             bias=nmx[:, u % 2, m:m + 1], accum_out=sums[:, u, 1 + m:2 + m])
                last.then_inc(exp_done, 1)

            def copy_pt(U, u, nt, x=0):
                act.wait_ge(pt_ready, U + 1 + LAG)
                act.wait_ge(pv_ready, U + 1)
                A(at[x][:, u % 2, 0:nt * P], B[6][:, 0:nt * P], ACT.Copy).then_inc(at_ready, 1)

            with act.Fori(0, N_G) as g:
                for j in range(2):
                    T1, T2, CS, TC = ((0, 1, 4, 5), (6, 7, 8, 9))[j]
                    step = g * 2 + j
                    U = [g * 12 + (6 * j + u) for u in range(6)]
                    act.wait_ge(sc_ready, U[0] + LAG)
                    evac(T1, dT, B[2 + T1 % 2].rearrange("p (t s) -> p t s", t=2), g)
                    evac(T2, nqT, B[2 + T2 % 2][0:64].rearrange("p (t s) -> p t s", t=2), g)
                    if j == 0:
                        for t in range(2):
                            evac(2 + t, kT[:, t, :], B[2 + t][0:64, 0:S], g)
                    nt = [1, 2, 2, 4, 2, 4]
                    nks = [P, 2 * P] * 3
                    tile = step + T_BG
                    exps(U[0], 0, nks[0])
                    exps(U[1], 1, nks[1])
                    hi(0, tile)
                    copy_pt(U[0], 0, nt[0])
                    hi(1, tile)
                    exps(U[2], 2, nks[2])
                    act.wait_ge(cm_ready, step + 1)
                    A(cs[:, :, :, :].rearrange("p c t n -> p (c t n)"), cs[:, :, :, :].rearrange("p c t n -> p (c t n)"), ACT.Exp).then_inc(cexp_done, 1)
                    copy_pt(U[1], 1, nt[1])
                    exps(U[3], 3, nks[3])
                    hi(2, tile)
                    copy_pt(U[2], 2, nt[2])
                    exps(U[4], 4, nks[4])
                    hi(3, tile)
                    evac(TC, pcT, B[2 + TC % 2][0:N_CMP].rearrange("p (t s) -> p t s", t=2), g)
                    copy_pt(U[3], 3, nt[3])
                    exps(U[5], 5, nks[5])
                    hi(4, tile)
                    copy_pt(U[4], 4, nt[4])
                    hi(5, tile)
                    copy_pt(U[5], 5, nt[5])
                    hi(6, tile)
                    hi(7, tile)
                    for c in range(C):
                        evac_acc(c, step + T_BG, step + T_BG, None, None)
                        A(gates[:, c, bass.ds(g * 1024 + 512 * j, NW)], B[c], ACT.Tanh, scale=0.5).then_inc(acc_free[c], 1)

            for n in range(8):
                c, hf, first = (n % 4) // 2, n % 2, 8 if n < 4 else 0
                evac_hi(G_OT + n, H_OT + n, orr[:, 0, first + 4 * hf:first + 4 * hf + 4, c * P:(c + 1) * P])

            def mix_hi(i):
                for c in range(C):
                    act.wait_ge(tp_ready[c], i + (G_MIX // 2 + 1))
                    A(xr[:, 0, bass.ds(i * 4, 4), c * P:(c + 1) * P], four(c), ACT.Copy).then_inc(hi_done, 1)

            for n in range(PIECES):
                hi(n, T_BR)
            with act.Fori(1, N_BR) as i:
                for n in range(PIECES):
                    if n == MIX_AFTER:
                        mix_hi(i - 1)
                    hi(n, i + T_BR)
            for n in range(PIECES):
                if n == MIX_AFTER:
                    mix_hi(N_BR - 1)
                hi(n, T_WO)
            with act.Fori(1, N_WO) as i:
                for n in range(PIECES):
                    hi(n, i + T_WO)
            act.wait_ge(h_done, 2 * N_WO)
            for c in range(C):
                squares(2, c, h[:, c, :], square_b)
            for c in range(C):
                for q in range(4):
                    evac_hi(G_X2 + 4 * c + q, H_X2 + 4 * c + q, xr[:, 0, 4 * q:4 * q + 4, c * P:(c + 1) * P])
            for n in range(PIECES):
                hi(n, T_XQ)
            for c in range(C):
                copy_acc(c, T_XQ, T_XQ, stage_b[:, c, :])
            for c in range(C):
                act.wait_ge(acc_free[c], T_XQ + 2)
                act.sem_inc(act_steps, 2)
            for c in range(C):
                evac(G_QX + c, qxT[:, :, c * P:(c + 1) * P], four(c))
            for kind, v in (("e", 0), ("e", 1), ("t", 0), ("e", 2), ("t", 1), ("e", 3), ("t", 2), ("t", 3)):
                if kind == "e":
                    exps(48 + v, v, 2 * P, 1)
                else:
                    copy_pt(48 + v, v, 4, 1)
            for c in range(C):
                evac_hi(G_OX + c, H_OX + c, oxr[:, 0, :, c * P:(c + 1) * P])
            for n in range(PIECES):
                hi(n, T_XO)
            act.wait_ge(h_done, 2 * N_WO + 2 * X_H)
            for c in range(C):
                squares(3, c, h[:, c, :], square_b)
            for c in range(C):
                for q in range(4):
                    evac_hi(G_X3 + 4 * c + q, H_X3 + 4 * c + q, xr[:, 0, 4 * q:4 * q + 4, c * P:(c + 1) * P])

            def query_tile(i, pieces=PIECES):
                for n in range(pieces):
                    hi(n, i + T_PQ)
                for c in range(C):
                    if c == 0:
                        act.wait_ge(acc0_ready, i + (A_PQ + 1))
                    else:
                        act.wait_ge(w_used, i * PIECES + ((T_PQ + 1) * PIECES + WR))
                    A(stage_b[:, c, :], B[c], ACT.Copy).then_inc(acc_free[c], 1)
                    act.wait_ge(acc_free[c], i + (A_PQ + 2))
                    act.sem_inc(act_steps, 1)
                for c in range(C):
                    act.wait_ge(tp_ready[c], i * 2 + (G_PQ // 2 + 1))
                    A(qpT[:, :, c * P:(c + 1) * P], four(c), ACT.Copy).then_inc(tp_free[c], 1)
                for hh in range(2):
                    act.wait_ge(tp_ready[hh], i * 2 + (G_PQ // 2 + 2))
                    A(scores[:, bass.ds(i * 1024 + 512 * hh, 512)] if not isinstance(i, int) else scores[:, i * 1024 + 512 * hh:i * 1024 + 512 * hh + 512],
                      B[2 + hh], ACT.Copy).then_inc(tp_free[hh], 1)

            def route_softmax(u):
                act.wait_ge(route_scores, u + 1)
                A(ex[:, :], sc16[:, :], ACT.Exp, bias=nsc[:, :], accum_out=exs[:, 0:1]).then_inc(route_exp, 1)

            query_tile(0)
            route_softmax(0)
            route_softmax(1)
            with act.Fori(1, N_PQ - 1) as i:
                query_tile(i)
            query_tile(N_PQ - 1, PIECES - AHEAD)

            def gelu(par, u):
                act.wait_ge(dot_done, u * 16 + (16 + RING))
                A(act_u[:, :], dots[:, par, :], ACT.Gelu).then_inc(gelu_done, 1)

            def diagonals(par, u, js):
                for j in js:
                    act.wait_ge(v_used, u * 16 + (j + 1))
                    A(diag[:, j % RING, :], ident[:, :], ACT.Copy, scale=ga[:, par, j:j + 1]).then_inc(diag_ready, 1)

            gelu(0, 0)
            with act.Fori(0, PH - 1) as i:
                for par, u in ((0, i * 2), (1, i * 2 + 1)):
                    act.wait_ge(ga_ready, u + 1)
                    diagonals(par, u, range(0, 5))
                    route_softmax(u + 2)
                    diagonals(par, u, range(5, PK))
                    gelu(1 - par, u + 1)
            act.wait_ge(ga_ready, UNITS - 1)
            diagonals(0, UNITS - 2, range(PK))
            gelu(1, UNITS - 1)
            act.wait_ge(ga_ready, UNITS)
            diagonals(1, UNITS - 1, range(0, 4))
            act.wait_ge(vacc_free, UNITS)
            squares(4, 0, h[:, 0, :], u_ring[:, 0, :])
            diagonals(1, UNITS - 1, range(4, PK))
            act.wait_ge(vacc_free, UNITS + 1)
            squares(5, 0, h[:, 1, :], u_ring[:, 0, :])

        @block.vector
        def _(dve):
            V = nc.vector
            link = Chain(dve, dve_steps)
            dve.sem_inc(sc_free, LAG)
            dve.sem_inc(sc_ready, LAG)
            dve.sem_inc(pt_ready, LAG)
            dve.sem_inc(pv_ready, LAG)
            dve.sem_inc(ev_done, 1)
            dve.sem_inc(vacc_free, 1)
            dve.sem_inc(nacc_free[0], 1)
            dve.sem_inc(nacc_free[1], 1)
            dve.sem_inc(dot_done, RING)
            dve.sem_inc(v_used, RING)

            for i in range(ROPE_HALF):
                V.memset(inv[:, i:i + 1], ROPE_INV[i])
            link(V.memset(lamb[:, :], 0.0))

            def mean_squares(n, cols=2, count=None):
                dve.wait_ge(sq_done, count)
                V.tensor_scalar(msq[:, 2 * n:2 * n + cols], ssq[:, 2 * n:2 * n + cols], 1.0 / D, EPS, ALU.mult, ALU.add).then_inc(ms_done, 1)

            def scale_rows(n, src, dst, gain):
                dve.wait_ge(rstd_done, n + 1)
                for c in range(C):
                    V.scalar_tensor_tensor(out=dst[:, c, :], in0=src[:, c, :], scalar=rstd[:, 2 * n + c:2 * n + c + 1], in1=gain,
                                           op0=ALU.mult, op1=ALU.mult).then_inc(xn_done, 1)

            def lo(n, tile, cols=NW):
                q = n + AHEAD
                dve.wait_ge(w_hi, tile * PIECES + (q + 1))
                V.tensor_tensor(ws[:, q % WR, 1, :, 0:cols], wraw[:, q % WR, :, 0:cols], ws[:, q % WR, 0, :, 0:cols].bitcast(F32),
                                ALU.subtract).then_inc(w_split, 1)

            def next_cols(n, cols, following):
                return cols if n + AHEAD < PIECES else following

            def evac_lo(n, number, pair):
                dve.wait_ge(hi_done, number + 1)
                V.tensor_tensor(pair[1], B[2 + n % 2].rearrange("p (t s) -> p t s", t=4), pair[0].bitcast(F32),
                                ALU.subtract).then_inc(tp_free[n % 2], 1)

            def norm_lo(base, number, dst):
                for c in range(C):
                    for q in range(4):
                        evac_lo(base + 4 * c + q, number + 4 * c + q, [dst[:, t, 4 * q:4 * q + 4, c * P:(c + 1) * P] for t in range(2)])

            mean_squares(0, count=2)
            dve.wait_ge(gmem_landed, 16)
            scale_rows(0, mn, mn, gmem)
            for n in range(-AHEAD, 0):
                lo(n, 0)
            norm_lo(G_MEM, H_MEM, orr)
            dve.wait_ge(tp_ready[0], G_POS // 2 + 1)
            V.tensor_copy(posT[:, :], B[2][0:64, 0:CMP_LEN]).then_inc(tp_free[0], 1)
            dve.wait_ge(tp_ready[1], G_KEYS // 2 + 1)
            V.tensor_copy(keysT[:, :, :].rearrange("p t n -> p (t n)"), B[3][:, 0:2 * P]).then_inc(tp_free[1], 1)
            mean_squares(1, count=4)
            dve.wait_ge(gmix_landed, 16)
            scale_rows(1, xn, xn, gmix)

            dve.wait_ge(small_landed, 16 * N_SMALL)
            link(V.tensor_copy(rope[:, 0, :, 0], pos_i[:, :]))
            link(V.tensor_tensor(rope[:, 1, :, :], rope[:, 0, :, 0:1].broadcast_to([P, C, ROPE_HALF]),
                                 inv[:, :].unsqueeze(1).broadcast_to([P, C, ROPE_HALF]), ALU.mult))
            link(V.tensor_scalar(rope[:, 0, :, :], rope[:, 1, :, :], 1.0 / (2 * math.pi), MAGIC, ALU.mult, ALU.add))
            link(V.tensor_scalar(rope[:, 0, :, :], rope[:, 0, :, :], -MAGIC, None, ALU.add))
            for part_ in (TWO_PI_A, TWO_PI_B, TWO_PI_C):
                link(V.scalar_tensor_tensor(out=rope[:, 1, :, :], in0=rope[:, 0, :, :], scalar=-part_, in1=rope[:, 1, :, :],
                                            op0=ALU.mult, op1=ALU.add))
            link(V.tensor_scalar(rope[:, 2, :, :], rope[:, 1, :, :], PI_IN, -PI_IN, ALU.min, ALU.max))
            link(V.tensor_scalar(rope[:, 0, :, :], rope[:, 2, :, :], -1.0, None, ALU.mult))
            link(V.tensor_tensor(rope[:, 1, :, :], rope[:, 0, :, :], rope[:, 2, :, :], ALU.min))
            V.tensor_scalar(rope[:, 3, :, :], rope[:, 1, :, :], math.pi / 2, None, ALU.add).then_inc(angle_ready, 1)
            link(V.tensor_tensor(lamp[:, 0:64], lam4[:, 0, :], lam4[:, 1, :], ALU.mult))
            link(V.tensor_tensor(lamp[:, 64:128], lam4[:, 2, :], lam4[:, 3, :], ALU.mult))
            V.reduce_sum(lamb[:, 0:2], lamp.rearrange("p (t d) -> p t d", t=2), axis=AX.X).then_inc(lam_in, 1)
            link(V.tensor_scalar(subg[:, :], subg[:, :], 1.0 - LAMBDA_INIT, None, ALU.mult))
            for t in range(2):
                for n in range(PIECES):
                    lo(n, T_KV + t)
            norm_lo(G_X, H_X, xr)

            sin, cos = rope[:, 4, :, :], rope[:, 5, :, :]

            def rotate(c, first, n):
                v = z[:, c, first:first + 64 * n].rearrange("p (n d) -> p n d", d=64)
                x1, x2 = v[:, :, 0:ROPE_HALF], v[:, :, ROPE_HALF:2 * ROPE_HALF]
                t = [rot[:, k, 0:8 * n].rearrange("p (n d) -> p n d", d=8) for k in range(4)]
                cc = cos[:, c, :].unsqueeze(1).broadcast_to([P, n, ROPE_HALF])
                ss = sin[:, c, :].unsqueeze(1).broadcast_to([P, n, ROPE_HALF])
                V.tensor_tensor(t[0], x1, cc, ALU.mult)
                V.tensor_tensor(t[1], x2, ss, ALU.mult)
                V.tensor_tensor(t[2], x2, cc, ALU.mult)
                link(V.tensor_tensor(t[3], x1, ss, ALU.mult))
                V.tensor_tensor(x1, t[0], t[1], ALU.subtract)
                link(V.tensor_tensor(x2, t[2], t[3], ALU.add))

            dve.wait_ge(sin_done, 1)
            done = 0
            for tiles, parts in ((4, [(ZQ, 32)]), (8, [(NQ, 16)]), (11, [(K_CMP, 4), (K_SEL, 4), (K_WIN, 4)])):
                plain = tiles - done - (tiles == N_QKV)
                with dve.Fori(0, plain) as i:
                    for n in range(PIECES):
                        lo(n, i + (T_QKV + done))
                if tiles == N_QKV:
                    for n in range(PIECES):
                        lo(n, T_QKV + N_QKV - 1, next_cols(n, NW, NG_COLS))
                    for n in range(PIECES):
                        lo(n, T_NG, next_cols(n, NG_COLS, NW))
                done = tiles
                for c in range(C):
                    dve.wait_ge(acc_free[c], T_QKV + tiles + 1)
                for c in range(C):
                    for first, n in parts:
                        rotate(c, first, n)
            link(V.memset(csum[:, :], 0.0))
            V.tensor_copy(coef[:, 0:1], csum[:, 0:1]).then_inc(rope_done, 1)
            for c in range(C):
                dve.wait_ge(acc_free[c], T_NG + 2)
            V.tensor_scalar(gn[:, :, :], gn[:, :, :], 0.5, 0.5, ALU.mult, ALU.add).then_inc(gn_done, 1)
            dve.wait_ge(lam_exp, 1)
            link(V.tensor_tensor(lamb[:, 4:5], lamb[:, 3:4], lamb[:, 2:3], ALU.subtract))
            link(V.tensor_scalar(lamb[:, 5:6], lamb[:, 4:5], -LAMBDA_INIT, None, ALU.add))
            neg_lam = lamb[:, 5:6]
            for t in range(2):
                for c in range(C):
                    dve.wait_ge(tp_free[c], (G_CMP + 2 * t + c) // 2 + 2)
                for lh in range(2):
                    last = V.tensor_tensor(blk[:, t, 16 * lh:16 * lh + 16, :, :],
                                           xsT[:, t, :, 16 * lh:16 * lh + 240].rearrange("p g (n l) -> p l g n", l=16),
                                           posT[:, 16 * lh:16 * lh + 16].unsqueeze(2).unsqueeze(3).broadcast_to([64, 16, N_G, N_CMP]), ALU.add)
                last.then_inc(blk_ready, 1)

            def softmax_in(U, u, nk, mask, x=0):
                dve.wait_ge(sc_ready, U + 1 + LAG)
                dve.wait_ge(exp_done, U + 1)
                b = u % 2
                sv = Sc[x][:, b, 0:2 * nk].rearrange("p (m n) -> p m n", m=2)
                pv = B[4 + b][:, 0:2 * nk].rearrange("p (m n) -> p m n", m=2)
                if mask is None:
                    V.tensor_scalar(sv, pv, X_SCALE, None, ALU.mult).then_inc(sc_free, 1)
                else:
                    V.scalar_tensor_tensor(out=sv, in0=pv, scalar=ATT_SCALE, in1=mask.unsqueeze(1).broadcast_to([P, 2, nk]),
                                           op0=ALU.mult, op1=ALU.add).then_inc(sc_free, 1)
                dve.wait_ge(sc_free, U + 1 + LAG)
                link(V.reduce_max(mx[:, b, :], sv, axis=AX.X))
                V.tensor_scalar(nmx[:, b, :], mx[:, b, :], -1.0, None, ALU.mult).then_inc(nm_ready, 1)

            with dve.Fori(0, N_G) as g:
                link.loop(g, ATT_STEPS)
                for j in range(2):
                    CS, TC = ((4, 5), (8, 9))[j]
                    step = g * 2 + j
                    U = [g * 12 + (6 * j + u) for u in range(6)]

                    def SM(u):
                        c = u % 2
                        softmax_in(U[u], u, (c + 1) * P, causal[:, P:2 * P] if c == 0 else causal[:, :])

                    def difference(u):
                        dve.wait_ge(exp_done, U[u] + 1 + LAG)
                        nk = (u + 1) * P
                        p0, p1 = Pr[0][:, u, 0:nk], Pr[0][:, u, nk:2 * nk]
                        link(V.reciprocal(rec[:, 0:2], sums[:, u, 1:3]))
                        V.tensor_scalar(coef[:, 0:1], rec[:, 1:2], neg_lam, None, ALU.mult)
                        link(V.tensor_scalar(p0, p0, rec[:, 0:1], None, ALU.mult))
                        V.scalar_tensor_tensor(out=p0, in0=p1, scalar=coef[:, 0:1], in1=p0, op0=ALU.mult, op1=ALU.add).then_inc(da_ready, 1)

                    def EV(u):
                        c = u % 2
                        dve.wait_ge(pv_ready, U[u] + 1 + LAG)
                        if u < 2:
                            out_u = z[:, c, bass.ds(g * 256 + (ZQ + 128 * j), 128)]
                            V.tensor_copy(out_u, B[7][:, 0:P]).then_inc(ev_done, 1)
                            dve.wait_ge(ev_done, U[u] + 2)
                            V.scalar_tensor_tensor(out=tmp3[:, 0:P], in0=out_u, scalar=1.0, in1=out_u, op0=ALU.mult, op1=ALU.mult,
                                                   accum_out=ms2[:, 0, c:c + 1]).then_inc(subln_sq, 1)
                            if c == 1:
                                dve.wait_ge(subln_sq, step * 2 + 2)
                                V.tensor_scalar(ms2[:, 1, :], ms2[:, 0, :], 1.0 / DA_DV, EPS, ALU.mult, ALU.add).then_inc(subln_ms, 1)
                            return
                        t = u // 2 - 1
                        link(V.tensor_copy(sums[:, u, 0:1], csum[:, 2 * c + t:2 * c + t + 1]))
                        link(V.reciprocal(rec[:, 2:5], sums[:, u, 0:3]))
                        link(V.tensor_tensor(coef[:, 1:4], rec[:, 2:5], gn[:, c, bass.ds(g * 12 + (6 * j + 3 * t), 3)], ALU.mult))
                        tv = tmp3[:, :].rearrange("p (b d) -> p b d", b=3)
                        link(V.tensor_tensor(tv, B[7][:, 0:3 * N_DK].rearrange("p (b d) -> p b d", b=3),
                                             coef[:, 1:4].unsqueeze(2).broadcast_to([P, 3, N_DK]), ALU.mult))
                        V.reduce_sum(z[:, c, bass.ds(g * 256 + (NQ + 128 * j + 64 * t), 64)],
                                     tmp3[:, :].rearrange("p (b d) -> p d b", b=3), axis=AX.X).then_inc(ev_done, 1)

                    def head_norm():
                        dve.wait_ge(subln_rstd, step + 1)
                        for c in range(C):
                            out_u = z[:, c, bass.ds(g * 256 + (ZQ + 128 * j), 128)]
                            V.scalar_tensor_tensor(out=out_u, in0=out_u, scalar=ms2[:, 2, c:c + 1], in1=subg[:, :],
                                                   op0=ALU.mult, op1=ALU.mult).then_inc(subln_done, 1)

                    def compressed_in():
                        dve.wait_ge(tp_ready[CS % 2], g * 5 + (G_ATT // 2 + CS // 2 + 1))
                        dve.wait_ge(tp_ready[1], g * 5 + (12, 15)[j])
                        for c in range(C):
                            last = V.scalar_tensor_tensor(out=cs[:, c, :, :], in0=B[2 + CS % 2][:, 30 * c:30 * c + 30].rearrange("p (t n) -> p t n", t=2),
                                                          scalar=ATT_SCALE, in1=cm_add[:, c, :].unsqueeze(1).broadcast_to([P, 2, N_CMP]),
                                                          op0=ALU.mult, op1=ALU.add)
                        last.then_inc(tp_free[CS % 2], 1)
                        dve.wait_ge(tp_free[CS % 2], g * 5 + (G_ATT // 2 + CS // 2 + 2))
                        flat = cs[:, :, :, :].rearrange("p c t n -> p (c t) n")
                        link(V.reduce_max(cmx[:, :], flat, axis=AX.X))
                        V.tensor_tensor(flat, flat, cmx[:, :].unsqueeze(2).broadcast_to([P, 4, N_CMP]), ALU.subtract).then_inc(cm_ready, 1)

                    def compressed_out():
                        dve.wait_ge(cexp_done, step + 1)
                        flat = cs[:, :, :, :].rearrange("p c t n -> p (c t) n")
                        link(V.reduce_sum(csum[:, :], flat, axis=AX.X))
                        for c in range(C):
                            last = V.tensor_tensor(cs[:, c, :, :], cs[:, c, :, :], cm_mul[:, c, :].unsqueeze(1).broadcast_to([P, 2, N_CMP]), ALU.mult)
                        last.then_inc(cp_ready, 1)

                    tile = step + T_BG
                    SM(0), SM(1), difference(0), difference(1), lo(0, tile), SM(2), lo(1, tile)
                    compressed_in(), EV(0), SM(3), lo(2, tile), compressed_out(), EV(1), SM(4), lo(3, tile)
                    SM(5), EV(2), lo(4, tile), EV(3), lo(5, tile), head_norm(), EV(4), lo(6, tile), EV(5), lo(7, tile)
                link.end(N_G)

            for n in range(8):
                c, hf, first = (n % 4) // 2, n % 2, 8 if n < 4 else 0
                evac_lo(G_OT + n, H_OT + n, [orr[:, t, first + 4 * hf:first + 4 * hf + 4, c * P:(c + 1) * P] for t in range(2)])

            def branch_tile(i):
                for c in range(C):
                    for n in range(2 * c, 2 * c + 2):
                        if n == MIX_AFTER and not isinstance(i, int):
                            mix_lo(i - 1)
                        lo(n, i + T_BR)
                for c in range(C):
                    if c == 0:
                        dve.wait_ge(acc0_ready, i + (T_BR + 1))
                    else:
                        dve.wait_ge(w_used, i * PIECES + (T_BR * PIECES + 4 + WR))
                    dve.wait_ge(tp_ready[c], i + G_MIX // 2)
                    V.scalar_tensor_tensor(out=stage_a[:, c, :], in0=gates[:, c, bass.ds(i * NW, NW)], scalar=1.0, in1=B[c],
                                           op0=ALU.add, op1=ALU.mult).then_inc(acc_free[c], 1)
                    lo(4 + c, i + T_BR)
                for n in range(6, PIECES):
                    lo(n, i + T_BR)
                for c in range(C):
                    if c == 0:
                        dve.wait_ge(nacc0_ready, i + 1)
                    else:
                        dve.wait_ge(w_used, i * PIECES + ((T_BR + 1) * PIECES + WR))
                        dve.wait_ge(mix_ready, i * 2 + 1)
                    V.scalar_tensor_tensor(out=half_mix, in0=gates[:, c, bass.ds(i * NW + D, NW)], scalar=1.0, in1=B[4 + c],
                                           op0=ALU.add, op1=ALU.mult).then_inc(nacc_free[c], 1)
                    dve.wait_ge(nacc_free[c], i + 2)
                    dve.wait_ge(acc_free[c], i + (T_BR + 2))
                    V.tensor_tensor(stage_a[:, c, :], stage_a[:, c, :], half_mix, ALU.add).then_inc(mix_ready, 1)

            def mix_lo(i):
                for c in range(C):
                    dve.wait_ge(hi_done, i * 2 + (H_MIX + c + 1))
                    V.tensor_tensor(xr[:, 1, bass.ds(i * 4, 4), c * P:(c + 1) * P], B[2 + c].rearrange("p (t s) -> p t s", t=4),
                                    xr[:, 0, bass.ds(i * 4, 4), c * P:(c + 1) * P].bitcast(F32), ALU.subtract).then_inc(tp_free[c], 1)

            def residual(i):
                for c in range(C):
                    if c == 0:
                        dve.wait_ge(acc0_ready, i + (T_WO + 1))
                    else:
                        dve.wait_ge(w_used, i * PIECES + ((T_WO + 1) * PIECES + WR))
                    hv = h[:, c, bass.ds(i * NW, NW)]
                    V.scalar_tensor_tensor(out=hv, in0=B[c], scalar=0.5, in1=hv, op0=ALU.mult, op1=ALU.add).then_inc(acc_free[c], 1)
                    dve.wait_ge(acc_free[c], i + (T_WO + 2))
                    dve.sem_inc(h_done, 1)

            branch_tile(0)
            with dve.Fori(1, N_BR) as i:
                branch_tile(i)
            for n in range(PIECES):
                if n == MIX_AFTER:
                    mix_lo(N_BR - 1)
                lo(n, T_WO)
            dve.wait_ge(h_landed, 16)
            residual(0)
            with dve.Fori(1, N_WO) as i:
                for n in range(PIECES):
                    lo(n, i + T_WO)
                residual(i)
            mean_squares(2, count=6)
            dve.wait_ge(gx_landed, 16)
            scale_rows(2, h, xn2, gx)
            norm_lo(G_X2, H_X2, xr)
            for n in range(PIECES):
                lo(n, T_XQ)

            def XEV(v):
                c, hp = v // 2, v % 2
                dve.wait_ge(pv_ready, 48 + v + 1 + LAG)
                link(V.reciprocal(rec[:, 0:2], sums[:, v, 1:3]))
                V.tensor_tensor(ox[:, c, 256 * hp:256 * hp + 256].rearrange("p (m d) -> p m d", m=2), B[7][:, 0:256].rearrange("p (m d) -> p m d", m=2),
                                rec[:, 0:2].unsqueeze(2).broadcast_to([P, 2, P]), ALU.mult).then_inc(ev_done, 1)

            for kind, v in (("s", 0), ("s", 1), ("s", 2), ("e", 0), ("s", 3), ("e", 1), ("e", 2), ("e", 3)):
                if kind == "s":
                    softmax_in(48 + v, v, 2 * P, None, 1)
                else:
                    XEV(v)
            for c in range(C):
                evac_lo(G_OX + c, H_OX + c, [oxr[:, t, :, c * P:(c + 1) * P] for t in range(2)])
            for n in range(X_H):
                lo(2 * n, T_XO)
                lo(2 * n + 1, T_XO)
                for c in range(C):
                    if c == 0:
                        dve.wait_ge(acc0_ready, T_XO + n + 1)
                    else:
                        dve.wait_ge(w_used, T_XO * PIECES + 2 * n + 2 + WR)
                    hv = h[:, c, n * NW:(n + 1) * NW]
                    V.tensor_tensor(hv, B[c], hv, ALU.add).then_inc(acc_free[c], 1)
                    dve.wait_ge(acc_free[c], T_XO + n + 2)
                    dve.sem_inc(h_done, 1)
            mean_squares(3, count=8)
            dve.wait_ge(grow_landed, 16)
            scale_rows(3, h, xn3, grow)
            norm_lo(G_X3, H_X3, xr)
            for n in range(PIECES):
                lo(n, T_PQ)

            def top16(src, scratch, vals, ids):
                dve.sem_inc(dve_turns, 1)
                link(V.max(vals[:, 0:8], src))
                dve.sem_inc(dve_turns, 1)
                V.max_index(ids[:, 0:8], vals[:, 0:8], src)
                link(V.match_replace(scratch, vals[:, 0:8], src, -3.0e38))
                dve.sem_inc(dve_turns, 1)
                link(V.max(vals[:, 8:16], scratch))
                dve.sem_inc(dve_turns, 1)
                link(V.max_index(ids[:, 8:16], vals[:, 8:16], scratch))

            def route(u, src, par):
                link(V.tensor_copy(wk[:, :, :].rearrange("p t n -> p (t n)"), src))
                for t in range(2):
                    top16(wk[:, t, :], wk2[:, t * P:(t + 1) * P], top[:, t, :], topi[:, t, :])
                V.tensor_copy(topf[:, :, :], topi[:, :, :])
                link(V.tensor_tensor(cand[:, :, :], top[:, 0, :].unsqueeze(2).broadcast_to([P, PK, PK]),
                                     top[:, 1, :].unsqueeze(1).broadcast_to([P, PK, PK]), ALU.add))
                if not (isinstance(u, int) and u == 0):
                    dve.wait_ge(route_exp, u)
                top16(cand[:, :, :].rearrange("p a b -> p (a b)"), wk2[:, :], sc16, ci)
                V.tensor_scalar(nsc[:, :], sc16[:, 0:1], -1.0, None, ALU.mult).then_inc(route_scores, 1)
                V.tensor_scalar(ab[:, 0, :], ci[:, :], 4, None, ALU.logical_shift_right)
                link(V.tensor_scalar(ab[:, 1, :], ci[:, :], PK - 1, None, ALU.bitwise_and))
                link(V.tensor_copy(abf[:, :, :], ab[:, :, :]))
                for t in range(2):
                    last = V.tensor_tensor(onehot[:, t, :, :], abf[:, t, :].unsqueeze(2).broadcast_to([P, PK, PK]),
                                           iota16[:, :].unsqueeze(1).broadcast_to([P, PK, PK]), ALU.is_equal)
                link(last)
                for t in range(2):
                    last = V.tensor_tensor(onehot[:, t, :, :], onehot[:, t, :, :],
                                           topf[:, t, :].unsqueeze(1).broadcast_to([P, PK, PK]), ALU.mult)
                link(last)
                link(V.reduce_sum(e12[:, :, :].rearrange("p t k -> p (t k)"), onehot[:, :, :, :].rearrange("p t k a -> p (t k) a"), axis=AX.X))
                if not (isinstance(u, int) and u < 2):
                    dve.wait_ge(idx_v_ready, u - 1)
                V.scalar_tensor_tensor(out=idx_u[par][:, :], in0=e12[:, 0, :], scalar=float(NKEYS), in1=e12[:, 1, :],
                                       op0=ALU.mult, op1=ALU.add).then_inc(idx_ready, 1)

            def route_weights(u, par):
                dve.wait_ge(route_exp, u + 1)
                link(V.reciprocal(exs[:, 1:2], exs[:, 0:1]))
                link(V.tensor_scalar(gw[:, par, :], ex[:, :], exs[:, 1:2], None, ALU.mult))

            def dot(u, par, j):
                r = j % RING
                dve.wait_ge(u_landed[r], u * 64 + 16 * (j // RING + 1))
                dve.wait_ge(dot_done, u * 16 + (j + RING))
                V.scalar_tensor_tensor(out=product, in0=u_ring[:, r, :], scalar=1.0, in1=xn3[:, par, :], op0=ALU.mult, op1=ALU.mult,
                                       accum_out=dots[:, par, j:j + 1]).then_inc(dot_done, 1)

            def weigh(u, par):
                dve.wait_ge(gelu_done, u + 1)
                V.tensor_tensor(ga[:, par, :], act_u[:, :], gw[:, par, :], ALU.mult).then_inc(ga_ready, 1)

            def add_out(u, par):
                dve.wait_ge(v_used, u * 16 + (16 + RING))
                V.tensor_tensor(h[:, par, :], vacc, h[:, par, :], ALU.add).then_inc(vacc_free, 1)

            for hh in range(2):
                dve.wait_ge(tp_free[hh], (G_PQ + 2) // 2 + 2)
            route(0, scores[:, 0:256], 0)
            route_weights(0, 0)
            route(1, scores[:, 256:512], 1)
            route_weights(1, 1)
            for n in range(3):
                lo(n, T_PQ + 1)
            pieces = [(T_PQ + 1 + n // PIECES, n % PIECES) for n in range(3, 3 * PIECES - AHEAD)]
            for j in range(PK):
                dot(0, 0, j)
                for tile, n in pieces[2 * j:2 * j + 2]:
                    lo(n, tile)
            weigh(0, 0)
            for hh in range(2):
                dve.wait_ge(tp_free[hh], (G_PQ + 14) // 2 + 2)

            def step(u, par, add, route_next):
                if add:
                    add_out(u - 2, par)
                for j in range(PK):
                    dot(u, par, j)
                    if route_next and j == 3:
                        route(u + 1, scores[:, bass.ds(u * 256 + 256, 256)], 1 - par)
                    if route_next and j == 8:
                        route_weights(u + 1, 1 - par)
                weigh(u, par)

            for par, u in ((1, 1),):
                for j in range(PK):
                    dot(u, par, j)
                    if j == 3:
                        route(2, scores[:, 512:768], 0)
                    if j == 8:
                        route_weights(2, 0)
                weigh(u, par)
            with dve.Fori(0, PH - 2) as i:
                link.loop(i, 2 * ROUTE_STEPS)
                step(i * 2 + 2, 0, True, True)
                step(i * 2 + 3, 1, True, True)
                link.end(PH - 2)
            add_out(UNITS - 4, 0)
            for j in range(PK):
                dot(UNITS - 2, 0, j)
                if j == 3:
                    route(UNITS - 1, scores[:, (UNITS - 1) * 256:UNITS * 256], 1)
                if j == 8:
                    route_weights(UNITS - 1, 1)
            weigh(UNITS - 2, 0)
            add_out(UNITS - 3, 1)
            for j in range(PK):
                dot(UNITS - 1, 1, j)
            weigh(UNITS - 1, 1)

            dve.wait_ge(gfin_landed, 16)
            for c in range(C):
                add_out(UNITS - 2 + c, c)
                n = 4 + c
                mean_squares(n, cols=1, count=9 + c)
                dve.wait_ge(rstd_done, n + 1)
                V.scalar_tensor_tensor(out=xn3[:, c, :], in0=h[:, c, :], scalar=rstd[:, 2 * n:2 * n + 1], in1=gfin[:, :],
                                       op0=ALU.mult, op1=ALU.mult).then_inc(y_done, 1)


_INS = ['x', 'mem', 'positions', 'norm_mix_g', 'w_in', 'da_lambda_q1', 'da_lambda_k1', 'da_lambda_q2', 'da_lambda_k2',
        'da_subln_g', 'nsa_cmp_pos', 'nsa_cmpk_w1', 'nsa_cmpk_w2', 'nsa_cmpv_w1', 'nsa_cmpv_w2', 'w_branch_da',
        'w_branch_nsa', 'w_out', 'norm_x_g', 'norm_mem_g', 'w_xq', 'w_xkv', 'w_xo', 'norm_ffn_g', 'peer_wq',
        'peer_keys1', 'peer_keys2', 'peer_u', 'peer_v', 'norm_final_g']


def kernel(**inputs):
    import numpy as _np
    import concourse.bacc as _bacc
    from concourse import mybir as _mybir
    from concourse.bass_utils import run_bass_kernel_spmd as _run

    nc = _bacc.Bacc("TRN2", target_bir_lowering=False, num_devices=1)
    arrays, args = {}, []
    for name in _INS:
        a = _np.ascontiguousarray(inputs[name])
        arrays[f"in_{name}_dram"] = a
        args.append(nc.dram_tensor(f"in_{name}_dram", a.shape, _mybir.dt.from_np(a.dtype), kind="ExternalInput").ap())
    args.append(nc.dram_tensor("out_dram", (1, S, D), _mybir.dt.float32, kind="ExternalOutput").ap())
    block_program(nc, *args)
    r = _run(nc, [arrays], core_ids=[0])
    return r.results[0]["out_dram"]
```

```python
import math
from contextlib import ExitStack

import numpy as np
import concourse.bass as bass
from concourse import mybir

F32 = mybir.dt.float32
U32 = mybir.dt.uint32
I32 = mybir.dt.int32
F32R = mybir.dt.float32r
ALU = mybir.AluOpType
ACT = mybir.ActivationFunctionType
AX = mybir.AxisListType

P = 128
D = 2048
S = 256
C = S // P
KT = D // P
NW = 512
PIECES = 8
KS = KT // PIECES
WR = 4
AHEAD = 3
MIX_AFTER = 2
EPS = 1e-6
NEG = -1e30

DA_H, DA_DK, DA_DV = 8, 64, 128
N_H, N_G, N_DK = 16, 4, 64
ZQ, ZK, ZV, NQ, NKV = 0, 1024, 2048, 3072, 4096
QKV_COLS = NKV + 6 * N_G * N_DK
NG_COLS = N_H * 3
BG = QKV_COLS + NG_COLS
K_CMP, V_CMP, K_SEL, V_SEL, K_WIN, V_WIN = (NKV + 256 * n for n in range(6))
ATT_SCALE = DA_DK ** -0.5
LAMBDA_INIT = 0.8 - 0.6 * math.exp(-0.3 * 0)
ROPE_HALF = 8
ROPE_INV = [float(np.float32(500000.0) ** np.float32(-2 * i / 16)) for i in range(ROPE_HALF)]

CMP_LEN, CMP_STRIDE = 32, 16
N_CMP = (S - CMP_LEN) // CMP_STRIDE + 1
X_H, X_DH = 4, 128
X_SCALE = X_DH ** -0.5

PH, PK, NKEYS = 8, 16, 128
UNITS = PH * C
HW = 2 * NKEYS
HK = KS * NW // HW
HP = PIECES // 2

T_KV, T_QKV, T_NG, T_BG, T_BR, T_WO, T_XQ, T_XO, T_PQ = 0, 2, 13, 14, 22, 26, 30, 31, 32
N_TILES = 36
N_QKV, N_BG, N_BR, N_WO, N_PQ = 11, 8, 4, 4, 4
A_PQ = T_PQ + 3

H_MEM, H_X, H_OT, H_MIX, H_X2, H_OX, H_X3 = 0, 8, 16, 24, 32, 40, 42

ATT_GROUPS = 10
G_MEM, G_POS, G_KEYS, G_MK, G_X, G_CMP, G_NG, G_ATT = 0, 8, 9, 10, 12, 20, 24, 26
G_OT = G_ATT + N_G * ATT_GROUPS
G_MIX, G_X2, G_QX, G_OX, G_X3, G_PQ = (G_OT + n for n in (8, 16, 24, 26, 28, 36))
T_CMP = T_QKV + K_CMP // NW

ATT_STEPS, ROUTE_STEPS = 56, 21

LAG = 2
RING = 4

BIG = C * QKV_COLS + C * 2 * D
RES_KB = 157
MAIN_KB = RES_KB + 32

MAGIC = 12582912.0
TWO_PI_A = 6.28125
TWO_PI_B = float(np.float32(2 * math.pi - TWO_PI_A))
TWO_PI_C = float(2 * math.pi - TWO_PI_A - TWO_PI_B)
PI_IN = 3.1415925


class Chain:

    def __init__(self, eng, sem):
        self.eng, self.sem, self.n, self.var, self.per = eng, sem, 0, None, 0

    def __call__(self, ins):
        self.n += 1
        ins.then_inc(self.sem, 1)
        self.eng.wait_ge(self.sem, self.n if self.var is None else self.var * self.per + self.n)

    def loop(self, var, per):
        self.var, self.per, self.first = var, per, self.n

    def end(self, trips):
        assert self.n - self.first == self.per, (self.n - self.first, self.per)
        self.n += self.per * (trips - 1)
        self.var = None


def block_program(nc, x, mem, positions, norm_mix_g, w_in, lq1, lk1, lq2, lk2, subln_g, cmp_pos, ck1, ck2,
                  cv1, cv2, w_bda, w_bnsa, w_out, norm_x_g, norm_mem_g, w_xq, w_xkv, w_xo, norm_ffn_g,
                  peer_wq, keys1, keys2, peer_u, peer_v, norm_final_g, out):
    ctx = ExitStack()
    with ctx:
        def sb(name, shape, dt=F32):
            return ctx.enter_context(nc.sbuf_tensor(name, shape, dt))

        def sem(name):
            return ctx.enter_context(nc.semaphore(name))

        KB = 1024
        whole_map = sb("whole_map", [P, MAIN_KB * KB // 4])
        origin = nc.sbuf_base - MAIN_KB * KB

        def at_kb(name, kb, shape, dt=F32):
            return nc.alloc_sbuf_tensor_at(name, shape, dt, offset=origin + int(kb * KB))

        wraw = at_kb("wraw", 0, [P, WR, KS, NW])
        gfin = at_kb("gfin", 0, [P, D])
        ws = at_kb("ws", 16, [P, WR, 2, KS, NW], F32R)
        xr = at_kb("xr", 48, [P, 2, KT, S], F32R)
        v_ring_t = at_kb("v_ring", 48, [P, RING, D])
        v_ring = v_ring_t[:, :, :]
        big = at_kb("big", 80, [P, BIG])
        orr = at_kb("orr", RES_KB, [P, 2, KT, S], F32R)
        att = at_kb("att", RES_KB, [P, 6144])
        h = at_kb("h", RES_KB, [P, C, D])
        xn3_t = at_kb("xn3", RES_KB + 16, [P, C, D])
        xn3 = xn3_t[:, :, :]
        z = big[:, 0:C * QKV_COLS].rearrange("p (c n) -> p c n", c=C)
        gates_flat = big[:, C * QKV_COLS:]
        gates = gates_flat.rearrange("p (c n) -> p c n", c=C)
        xn = gates_flat[:, 0:C * D].rearrange("p (c d) -> p c d", c=C)
        mn = gates_flat[:, C * D:].rearrange("p (c d) -> p c d", c=C)
        w1 = gates_flat[:, 0:CMP_LEN * P].rearrange("p (t l h) -> p t l h", t=2, l=CMP_LEN // 2)
        stage_a = big[:, 1024:2048].rearrange("p (c n) -> p c n", c=C)
        gmem, gmix, square_a = (big[:, n * D:(n + 1) * D] for n in (1, 2, 3))
        raw = big[:, 4 * D:4 * D + 512].rearrange("p (t n) -> p t n", t=4)
        lam4 = big[:, 4 * D + 512:4 * D + 768].rearrange("p (t n) -> p t n", t=4)
        lamp = big[:, 4 * D + 768:4 * D + 896]
        xn2 = big[:, 0:C * D].rearrange("p (c d) -> p c d", c=C)
        square_b = big[:, 2 * D:3 * D]
        gx = big[:, 3 * D:4 * D]
        later = big[:, 4 * D:4 * D + 6144]
        product = big[:, 7 * D:8 * D]
        grow = big[:, 8 * D:9 * D]
        stage_b = big[:, 9 * D:9 * D + 1024].rearrange("p (c n) -> p c n", c=C)
        u_ring = big[:, 0:RING * D].rearrange("p (r d) -> p r d", r=RING)
        arena = att[:, :]
        rot = arena[:, 0:1024].rearrange("p (k n) -> p k n", k=4)
        twice = arena[:, 3968:6016].rearrange("p (t c g h d) -> p t c g h d", t=2, c=C, g=N_G, h=2)
        rot_b = arena[:, 6016:6144].rearrange("p (k n) -> p k n", k=4)
        xsT = arena[:, 0:2048].rearrange("p (t g s) -> p t g s", t=2, g=N_G)
        blk = arena[:, 2048:2048 + 2 * 960].rearrange("p (t l g n) -> p t l g n", t=2, l=CMP_LEN // 2, g=N_G)
        dT = arena[:, 0:512].rearrange("p (t s) -> p t s", t=2)
        nqT = arena[0:64, 512:1024].rearrange("p (t s) -> p t s", t=2)
        kT = arena[0:64, 1024:1536].rearrange("p (t s) -> p t s", t=2)
        Sc, Pr, at = ([m[:, f:f + 1024].rearrange("p (b n) -> p b n", b=2) for m in (arena, later)] for f in (1536, 2560, 3584))
        dqk = arena[:, 4608:5120].rearrange("p (c t n) -> p c t n", c=C, t=2)
        nqs = arena[:, 5120:5376].rearrange("p (c n) -> p c n", c=C)
        kks = arena[:, 5376:5632].rearrange("p (t c n) -> p t c n", t=2, c=C)
        pcT = arena[0:N_CMP, 5632:6144].rearrange("p (t s) -> p t s", t=2)
        qxT = later[:, 0:1024].rearrange("p (h s) -> p h s", h=X_H)
        oxr = xr[:, :, 0:X_H, :]
        ox = later[:, 4608:5632].rearrange("p (c n) -> p c n", c=C)
        scores = later[:, 0:UNITS * 256]
        qpT = later[:, 4096:5120].rearrange("p (j s) -> p j s", j=4)
        half_mix = big[:, 2048:2560]
        vmem = sb("vmem", [P, C, NW])
        kxT = sb("kxT", [P, X_H, S])
        keysT = sb("keysT", [P, 2, NKEYS])
        ident = sb("ident", [P, P])
        causal = sb("causal", [P, 2 * P])
        cm_add = sb("cm_add", [P, C, N_CMP])
        cm_mul = sb("cm_mul", [P, C, N_CMP])
        gn = sb("gn", [P, C, NG_COLS])
        gnT = sb("gnT", [NG_COLS, S])
        posT = sb("posT", [P, CMP_LEN])
        w2 = sb("w2", [P, 2, N_DK])
        hid = sb("hid", [P, 2, N_G * N_CMP])
        kcT = sb("kcT", [64, N_G * N_CMP])
        vc = sb("vc", [N_CMP, N_G * N_DK])
        lamb = sb("lamb", [P, 8])
        subg = sb("subg", [P, DA_DV])
        pos_i = sb("pos_i", [P, C], I32)
        rope = sb("rope", [P, 6, C, ROPE_HALF])
        inv = sb("inv", [P, ROPE_HALF])
        ssq = sb("ssq", [P, 12])
        ssq_b = sb("ssq_b", [P, 8])
        msq = sb("msq", [P, 12])
        rstd = sb("rstd", [P, 12])
        nhalf = sb("nhalf", [P, 16])
        ms2 = sb("ms2", [P, 3, 2])
        mx = sb("mx", [P, 2, 2])
        nmx = sb("nmx", [P, 2, 2])
        sums = sb("sums", [P, 6, 4])
        rec = sb("rec", [P, 8])
        coef = sb("coef", [P, 4])
        tmp3 = sb("tmp3", [P, 3 * N_DK])
        cs = sb("cs", [P, C, 2, N_CMP])
        cmx = sb("cmx", [P, 4])
        csum = sb("csum", [P, 4])
        vmem_flat = vmem[:, :, :].rearrange("p c n -> p (c n)")
        kxT_flat = kxT[:, :, :].rearrange("p h s -> p (h s)")
        wk = vmem_flat[:, 0:256].rearrange("p (t n) -> p t n", t=2)
        wk2 = vmem_flat[:, 256:512]
        top = sb("top", [P, 2, PK])
        topi = sb("topi", [P, 2, PK], U32)
        topf = sb("topf", [P, 2, PK])
        cand = vmem_flat[:, 512:768].rearrange("p (a b) -> p a b", a=PK)
        sc16 = sb("sc16", [P, PK])
        ci = sb("ci", [P, PK], U32)
        ab = sb("ab", [P, 2, PK], U32)
        abf = sb("abf", [P, 2, PK])
        onehot = kxT_flat[:, 0:512].rearrange("p (t k a) -> p t k a", t=2, k=PK)
        e12 = sb("e12", [P, 2, PK])
        iota16 = sb("iota16", [P, PK])
        idx_u = [sb(f"idx_u{i}", [P, PK], U32) for i in range(2)]
        idx_v = [sb(f"idx_v{i}", [P, PK], U32) for i in range(2)]
        nsc = sb("nsc", [P, 1])
        ex = sb("ex", [P, PK])
        exs = sb("exs", [P, 2])
        gw = sb("gw", [P, 2, PK])
        dots = sb("dots", [P, 2, PK])
        act_u = sb("act_u", [P, PK])
        ga = sb("ga", [P, 2, PK])
        diag = kxT_flat[:, 512:1024].rearrange("p (r q) -> p r q", r=RING)

        psum = ctx.enter_context(nc.psum_tensor("banks", [P, 8 * NW], F32))
        B = [psum[:, n * NW:(n + 1) * NW] for n in range(8)]
        vacc = psum[:, 4 * NW:8 * NW]

        mem_landed = [sem(f"mem_landed{c}") for c in range(C)]
        x_landed, small_landed, w1_landed, gmem_landed, gmix_landed, gx_landed, h_landed = map(sem, (
            "x_landed", "small_landed", "w1_landed", "gmem_landed", "gmix_landed", "gx_landed", "h_landed"))
        grow_landed, gfin_landed, out_landed = map(sem, ("grow_landed", "gfin_landed", "out_landed"))
        w_landed = [sem(f"w_landed{r}") for r in range(WR)]
        w_hi, w_split, w_used = sem("w_hi"), sem("w_split"), sem("w_used")
        hi_done = sem("hi_done")
        acc0_ready = sem("acc0_ready")
        nacc0_ready = sem("nacc0_ready")
        acc_free = [sem(f"acc_free{c}") for c in range(C)]
        nacc_free = [sem(f"nacc_free{c}") for c in range(C)]
        tp_ready = [sem(f"tp_ready{b}") for b in range(2)]
        tp_free = [sem(f"tp_free{b}") for b in range(2)]
        consts_ready, sq_done, ms_done, rstd_done, xn_done = map(sem, ("consts_ready", "sq_done", "ms_done", "rstd_done", "xn_done"))
        dve_steps, act_steps, pool_steps = map(sem, ("dve_steps", "act_steps", "pool_steps"))
        angle_ready, sin_done, rope_done = map(sem, ("angle_ready", "sin_done", "rope_done"))
        lam_in, lam_exp = sem("lam_in"), sem("lam_exp")
        cmp_staged, blk_ready, hid_ready, hid_done, cmp_ready, cmp_done = map(sem, ("cmp_staged", "blk_ready", "hid_ready", "hid_done", "cmp_ready", "cmp_done"))
        staged, sc_ready, sc_free, nm_ready, exp_done = map(sem, ("staged", "sc_ready", "sc_free", "nm_ready", "exp_done"))
        da_ready, pt_ready, at_ready, pv_ready, ev_done = map(sem, ("da_ready", "pt_ready", "at_ready", "pv_ready", "ev_done"))
        map0_done = sem("map0_done")
        cm_ready, cexp_done, cp_ready = map(sem, ("cm_ready", "cexp_done", "cp_ready"))
        subln_sq, subln_ms, subln_rstd, subln_done, mix_ready, h_done = map(sem, ("subln_sq", "subln_ms", "subln_rstd", "subln_done", "mix_ready", "h_done"))
        idx_ready, idx_v_ready = map(sem, ("idx_ready", "idx_v_ready"))
        pool_turns, pe_turns, dve_turns = map(sem, ("pool_turns", "pe_turns", "dve_turns"))
        u_landed = [sem(f"u_landed{r}") for r in range(RING)]
        v_landed = [sem(f"v_landed{r}") for r in range(RING)]
        dot_done, v_used, route_scores, route_exp, gelu_done, ga_ready, diag_ready, vacc_free, y_done = map(
            sem, ("dot_done", "v_used", "route_scores", "route_exp", "gelu_done", "ga_ready", "diag_ready", "vacc_free", "y_done"))

        x_v = x[0].rearrange("(c p) d -> p c d", p=P)
        mem_v = mem[0].rearrange("(c p) d -> p c d", p=P)
        out_v = out[0].rearrange("(c p) d -> p c d", p=P)
        N_SMALL = 13

        def head_wide(piece):
            return piece.rearrange("p k n -> p (k n)").rearrange("p (k n) -> p k n", k=HK)

        def pieces_of(m):
            return m.rearrange("(s k p) n -> s p k n", k=KS, p=P)

        def norm_count(n, c):
            return min(2 * n, 8) + (n == 5) + c + 1

        block = ctx.enter_context(nc.Block())

        @block.sync
        def _(sp):
            for c in range(C):
                sp.dma_start(mn[:, c, :], mem_v[:, c, :]).then_inc(mem_landed[c], 16)
            sp.dma_start(gmem, norm_mem_g[0].partition_broadcast(P)).then_inc(gmem_landed, 16)

            def load(n, tile, src, cols=NW):
                sp.wait_ge(w_split, tile * PIECES + (n + 1))
                sp.dma_start(wraw[:, n % WR, :, 0:cols], src).then_inc(w_landed[n % WR], 16)

            kv, wi = pieces_of(w_xkv[0]), pieces_of(w_in[0])
            for t in range(2):
                for n in range(PIECES):
                    load(n, T_KV + t, kv[n][:, :, t * NW:(t + 1) * NW])
                    if t == 0 and n == WR - 1:
                        sp.dma_start(xn, x_v).then_inc(x_landed, 16)
                        sp.dma_start(gmix, norm_mix_g[0].partition_broadcast(P)).then_inc(gmix_landed, 16)
            with sp.Fori(0, T_CMP + 1 - T_QKV) as i:
                for n in range(PIECES):
                    load(n, i + T_QKV, wi[n][:, :, bass.ds(i * NW, NW)])
            for b in range(2):
                sp.wait_ge(tp_ready[b], (G_CMP - 2 + b) // 2 + 1)
            for t, m in enumerate((ck1, cv1)):
                sp.dma_start(w1[:, t, :, :], m[0].rearrange("(l p) h -> p l h", p=P)).then_inc(w1_landed, 16)
            with sp.Fori(T_CMP + 1 - T_QKV, N_QKV) as i:
                for n in range(PIECES):
                    load(n, i + T_QKV, wi[n][:, :, bass.ds(i * NW, NW)])
            for n in range(PIECES):
                load(n, T_NG, wi[n][:, :, QKV_COLS:BG], NG_COLS)
            with sp.Fori(0, N_BG) as i:
                for n in range(PIECES):
                    load(n, i + T_BG, wi[n][:, :, bass.ds(i * NW + BG, NW)])
            br = (pieces_of(w_bda[0]), pieces_of(w_bnsa[0]))
            with sp.Fori(0, N_BR) as i:
                for n in range(PIECES):
                    load(n, i + T_BR, br[n // 4][n % 4][:, :, bass.ds(i * NW, NW)])
            wo = pieces_of(w_out[0])
            for n in range(WR):
                load(n, T_WO, wo[n][:, :, 0:NW])
            sp.wait_ge(w_used, T_WO * PIECES + WR)
            sp.dma_start(h[:, :, :], x_v).then_inc(h_landed, 16)
            for n in range(WR, PIECES):
                load(n, T_WO, wo[n][:, :, 0:NW])
            with sp.Fori(1, N_WO) as i:
                for n in range(PIECES):
                    load(n, i + T_WO, wo[n][:, :, bass.ds(i * NW, NW)])
            for b in range(2):
                sp.wait_ge(tp_ready[b], (G_X2 - 2 + b) // 2 + 1)
            sp.dma_start(gx, norm_x_g[0].partition_broadcast(P)).then_inc(gx_landed, 16)
            sp.dma_start(grow, norm_ffn_g[0].partition_broadcast(P)).then_inc(grow_landed, 16)
            xq, xo = pieces_of(w_xq[0]), pieces_of(w_xo[0])
            for n in range(PIECES):
                load(n, T_XQ, xq[n])
            for n in range(PIECES):
                load(n, T_XO, xo[n % 2][:, :, n // 2 * NW:(n // 2 + 1) * NW])
            pq = pieces_of(peer_wq[0])
            pq_heads = peer_wq[0].rearrange("(s k p) n -> s p k n", k=HK, p=P)
            for n in range(PIECES):
                sp.wait_ge(w_split, T_PQ * PIECES + n + 1)
                sp.dma_start(head_wide(wraw[:, n % WR, :, :]), pq_heads[n % HP][:, :, n // HP * HW:(n // HP + 1) * HW]).then_inc(w_landed[n % WR], 16)
            with sp.Fori(1, N_PQ) as i:
                for n in range(PIECES):
                    load(n, i + T_PQ, pq[n][:, :, bass.ds(i * NW, NW)])
            sp.wait_ge(w_split, N_TILES * PIECES + WR)
            sp.dma_start(gfin[:, :], norm_final_g.partition_broadcast(P)).then_inc(gfin_landed, 16)
            for c in range(C):
                sp.wait_ge(y_done, c + 1)
                sp.dma_start(out_v[:, c, :], xn3[:, c, :]).then_inc(out_landed, 16)
            sp.wait_ge(out_landed, 16 * C)

        @block.gpsimd
        def _(pool):
            link = Chain(pool, pool_steps)
            link(nc.gpsimd.memset(ident[:, :], 0.0))
            nc.gpsimd.affine_select(out=ident[:, :], in_=ident[:, :], compare_op=ALU.not_equal, fill=1.0, base=0,
                                    pattern=[[-1, P]], channel_multiplier=1).then_inc(consts_ready, 1)
            nc.gpsimd.memset(nhalf[:, :], -0.5).then_inc(consts_ready, 1)
            link(nc.gpsimd.memset(causal[:, :], 0.0))
            nc.gpsimd.affine_select(out=causal[:, :], in_=causal[:, :], compare_op=ALU.is_ge, fill=NEG, base=P,
                                    pattern=[[-1, 2 * P]], channel_multiplier=1).then_inc(consts_ready, 1)
            link(nc.gpsimd.memset(cm_add[:, :, :], 0.0))
            link(nc.gpsimd.memset(cm_mul[:, :, :], 1.0))
            for m, fill in ((cm_add, NEG), (cm_mul, 0.0)):
                nc.gpsimd.affine_select(out=m[:, :, :], in_=m[:, :, :], compare_op=ALU.is_ge, fill=fill,
                                        base=-(CMP_LEN - 1), pattern=[[P, C], [-CMP_STRIDE, N_CMP]],
                                        channel_multiplier=1).then_inc(consts_ready, 1)
            nc.gpsimd.iota(iota16[:, :], pattern=[[1, PK]], base=0, channel_multiplier=0,
                           allow_small_or_imprecise_dtypes=True).then_inc(consts_ready, 1)

            def rsqrt(n, c):
                pool.wait_ge(ms_done, norm_count(n, c))
                nc.gpsimd.tensor_tensor(rstd[:, 2 * n + c:2 * n + c + 1], msq[:, 2 * n + c:2 * n + c + 1], nhalf[:, 0:1],
                                        ALU.pow).then_inc(rstd_done, 1)

            pool.wait_ge(consts_ready, 6)
            for n in range(2):
                for c in range(C):
                    rsqrt(n, c)
            pool.wait_ge(rope_done, 1)
            for t, base in enumerate((K_CMP, V_CMP)):
                for c in range(C):
                    for half in range(2):
                        last = nc.gpsimd.tensor_copy(twice[:, t, c, :, half, :], z[:, c, base:base + 256].rearrange("p (g d) -> p g d", g=N_G))
            last.then_inc(cmp_staged, 1)
            pool.wait_ge(rope_done, 2)
            pool.wait_ge(cmp_done, 1)
            with pool.Fori(0, N_G) as g:
                for j in range(2):
                    last_q = G_ATT // 2 + (-1, 2)[j]
                    pool.wait_ge(tp_ready[0], g * 5 + last_q - (1 if j else 0))
                    pool.sem_inc(pool_turns, 1)
                    nc.gpsimd.tensor_copy(dqk[:, :, 0, :], z[:, :, bass.ds(g * 256 + (ZQ + 128 * j), 128)])
                    nc.gpsimd.tensor_copy(dqk[:, :, 1, :], z[:, :, bass.ds(g * 256 + (ZK + 128 * j), 128)]).then_inc(staged, 1)
                    pool.wait_ge(tp_ready[1], g * 5 + last_q - (1 if j else 0))
                    pool.sem_inc(pool_turns, 1)
                    nc.gpsimd.tensor_copy(nqs[:, :, :], z[:, :, bass.ds(g * 256 + (NQ + 128 * j), 128)]).then_inc(staged, 1)
                    if j == 0:
                        nc.gpsimd.tensor_copy(kks[:, 0, :, :], z[:, :, bass.ds(g * 64 + K_SEL, 64)])
                        nc.gpsimd.tensor_copy(kks[:, 1, :, :], z[:, :, bass.ds(g * 64 + K_WIN, 64)]).then_inc(staged, 1)
                    pool.wait_ge(subln_ms, g * 2 + j + 1)
                    nc.gpsimd.tensor_tensor(ms2[:, 2, :], ms2[:, 1, :], nhalf[:, 0:C], ALU.pow).then_inc(subln_rstd, 1)
            for n in range(2, 4):
                for c in range(C):
                    rsqrt(n, c)

            def step(par, has_u, has_v, u):
                if has_v:
                    if not (isinstance(u, int) and u == 1):
                        pool.wait_ge(v_used, u * 16 + (RING - 32))
                        pool.sem_inc(pool_turns, 1)
                    nc.gpsimd.tensor_copy(idx_v[1 - par][:, :], idx_u[1 - par][:, :]).then_inc(idx_v_ready, 1)
                    pool.wait_ge(idx_v_ready, u)
                    pool.sem_inc(pool_turns, 1)
                if has_u:
                    pool.wait_ge(idx_ready, u + 1)
                    pool.sem_inc(pool_turns, 1)
                for j in range(PK):
                    r = j % RING
                    if has_u:
                        pool.wait_ge(dot_done, u * 16 + (j + 1))
                        pool.sem_inc(pool_turns, 1)
                        nc.gpsimd.indirect_dma_start(u_ring[:, r, :], None, peer_u[0],
                                                     bass.IndirectOffsetOnAxis(ap=idx_u[par][:, j:j + 1], axis=0)).then_inc(u_landed[r], 16)
                    if has_v:
                        pool.wait_ge(v_used, u * 16 + (j + 1 - 16))
                        pool.sem_inc(pool_turns, 1)
                        nc.gpsimd.indirect_dma_start(v_ring[:, r, :], None, peer_v[0],
                                                     bass.IndirectOffsetOnAxis(ap=idx_v[1 - par][:, j:j + 1], axis=0)).then_inc(v_landed[r], 16)

            step(0, True, False, 0)
            pool.wait_ge(w_used, N_TILES * PIECES + WR)
            step(1, True, True, 1)
            with pool.Fori(0, PH - 1) as i:
                step(0, True, True, i * 2 + 2)
                step(1, True, True, i * 2 + 3)
            step(0, False, True, UNITS)
            rsqrt(4, 0)
            rsqrt(5, 0)

        @block.tensor
        def _(pe):
            def tp_begin(n, g=None):
                if g is None:
                    pe.wait_ge(tp_free[n % 2], n // 2 + 1)
                else:
                    pe.wait_ge(tp_free[n % 2], g * (ATT_GROUPS // 2) + (G_ATT // 2 + n // 2 + 1))
                return B[2 + n % 2]

            def evacuated(n, g=None):
                if g is None:
                    pe.wait_ge(tp_free[n % 2], n // 2 + 2)
                else:
                    pe.wait_ge(tp_free[n % 2], g * (ATT_GROUPS // 2) + (G_ATT // 2 + n // 2 + 2))

            def transposes(n, tiles, g=None):
                bank = tp_begin(n, g)
                pe.sem_inc(pe_turns, 1)
                for src, col in tiles:
                    p, m = src.shape
                    last = nc.tensor.transpose(bank[0:m, col:col + p], src, ident[0:p, 0:p])
                last.then_inc(tp_ready[n % 2], 1)

            def part(tile, acc, n, lhs, bank=0, first=0, final=PIECES - 1, cols=NW):
                pe.wait_ge(w_split, tile * PIECES + (n + 1 + WR))
                for c in range(C):
                    if n == first:
                        pe.wait_ge((acc_free if bank == 0 else nacc_free)[c], acc + 1)
                    for k in range(KS):
                        hi, lo = (lhs[:, t, (n - first) * KS + k, c * P:(c + 1) * P] for t in range(2))
                        w_h, w_l = (ws[:, n % WR, t, k, 0:cols] for t in range(2))
                        dst = B[bank + c][:, 0:cols]
                        nc.tensor.matmul(dst, hi, w_h, start=(n == first and k == 0), stop=False)
                        nc.tensor.matmul(dst, hi, w_l, start=False, stop=False)
                        last = nc.tensor.matmul(dst, lo, w_h, start=False, stop=(n == final and k == KS - 1))
                    if c == C - 1:
                        last.then_inc(w_used, 1)
                    elif n == final:
                        last.then_inc(acc0_ready if bank == 0 else nacc0_ready, 1)

            def whole(tile, lhs, acc=None, cols=NW, groups=None):
                for n in range(PIECES):
                    if groups is not None and n % 2 == 0:
                        evacuated(groups + 4 + n // 2)
                    part(tile, tile if acc is None else acc, n, lhs, cols=cols)

            def norm_groups(base, src, norm):
                for c in range(C):
                    for q in range(4):
                        pe.wait_ge(xn_done, 8 * norm + 4 * c + q + 1)
                        transposes(base + 4 * c + q, [(src[:, c, (4 * q + t) * P:(4 * q + t + 1) * P], t * P) for t in range(4)])

            pe.wait_ge(consts_ready, 1)
            norm_groups(G_MEM, mn, 0)
            pe.wait_ge(small_landed, 16 * N_SMALL)
            transposes(G_POS, [(raw[0:CMP_LEN, 1, :], 0)])
            transposes(G_KEYS, [(raw[:, 2, :], 0), (raw[:, 3, :], P)])
            for n in range(2):
                whole(T_KV + n, orr, groups=G_MEM)
            pe.wait_ge(act_steps, 2)
            for c in range(C):
                transposes(G_MK + c, [(stage_a[:, c, t * P:(t + 1) * P], t * P) for t in range(X_H)])
            norm_groups(G_X, xn, 1)
            with pe.Fori(0, T_CMP + 2 - T_QKV) as i:
                whole(i + T_QKV, xr, groups=G_X)
            pe.wait_ge(cmp_staged, 1)
            for t in range(2):
                for c in range(C):
                    transposes(G_CMP + 2 * t + c, [(twice[:, t, c, g, :, :].rearrange("p h d -> p (h d)"), g * P) for g in range(N_G)])
            for tile in range(T_CMP + 2, T_NG):
                whole(tile, xr)
            for n in range(PIECES):
                pe.wait_ge(w_split, T_NG * PIECES + n + 1 + WR)
                if n == 0:
                    pe.wait_ge(acc_free[0], T_NG + 1)
                for k in range(KS):
                    kk = n * KS + k
                    w_h, w_l = (ws[:, n % WR, t, k, 0:NG_COLS] for t in range(2))
                    dst = B[0][0:NG_COLS, 0:S]
                    nc.tensor.matmul(dst, w_h, xr[:, 0, kk, :], start=(kk == 0), stop=False)
                    before = nc.tensor.matmul(dst, w_h, xr[:, 1, kk, :], start=False, stop=False)
                    last = nc.tensor.matmul(dst, w_l, xr[:, 0, kk, :], start=False, stop=(kk == KT - 1))
                if n == PIECES - 1:
                    before.then_inc(acc0_ready, 1)
                last.then_inc(w_used, 1)
            pe.wait_ge(w1_landed, 32)
            for t in range(2):
                pe.wait_ge(blk_ready, t + 1)
                for l in range(CMP_LEN // 2):
                    last = nc.tensor.matmul(B[5 + t][:, 0:60], w1[:, t, l, :], blk[:, t, l, :, :].rearrange("p g n -> p (g n)"),
                                            start=(l == 0), stop=(l == CMP_LEN // 2 - 1))
                last.then_inc(hid_ready, 1)
            pe.wait_ge(act_steps, 3)
            for c in range(C):
                transposes(G_NG + c, [(gnT[:, c * P:(c + 1) * P], 0)])
            pe.wait_ge(hid_done, 2)
            nc.tensor.matmul(B[7][0:64, 0:60], w2[:, 0, :], hid[:, 0, :], start=True, stop=True)
            for g in range(N_G):
                last = nc.tensor.matmul(B[7][0:N_CMP, 64 + g * 64:128 + g * 64], hid[:, 1, g * N_CMP:(g + 1) * N_CMP],
                                        w2[:, 1, :], start=True, stop=True)
            last.then_inc(cmp_ready, 1)

            pe.wait_ge(cmp_done, 2)
            pe.wait_ge(rope_done, 2)

            def score(U, u, c, pairs, apart=None):
                pe.wait_ge(sc_free, U + 1)
                nk = pairs[0][1].shape[-1]
                for m, (q, k) in enumerate(pairs):
                    last = nc.tensor.matmul(B[4 + u % 2][:, m * nk:(m + 1) * nk], q, k, start=True, stop=True)
                    if apart is not None and m == 0:
                        last.then_inc(map0_done, 1)
                        pe.wait_ge(map0_done, apart)
                last.then_inc(sc_ready, 1)

            def probs_T(U, u, nt, wait, value, x=0):
                pe.wait_ge(wait, value)
                pe.wait_ge(at_ready, U + 1)
                for t in range(nt):
                    last = nc.tensor.transpose(B[6][:, t * P:(t + 1) * P], Pr[x][:, u % 2, t * P:(t + 1) * P], ident[:, :])
                last.then_inc(pt_ready, 1)

            def values(U, products):
                pe.wait_ge(at_ready, U + 2)
                pe.wait_ge(ev_done, U + 1)
                pe.sem_inc(pe_turns, 1)
                for dst, terms in products:
                    for n, (a, v) in enumerate(terms):
                        last = nc.tensor.matmul(dst, a, v, start=(n == 0), stop=(n == len(terms) - 1))
                last.then_inc(pv_ready, 1)

            with pe.Fori(0, N_G) as g:
                for j in range(2):
                    T1, T2, CS, TC = ((0, 1, 4, 5), (6, 7, 8, 9))[j]
                    step = g * 2 + j
                    U = [g * 12 + (6 * j + u) for u in range(6)]

                    def fill(n):
                        part(step + T_BG, step + T_BG, n, xr)

                    def S_(u):
                        c = u % 2
                        nk = (c + 1) * P
                        if u < 2:
                            score(U[u], u, c, [(dT[64 * m:64 * m + 64, 0, c * P:(c + 1) * P], dT[64 * m:64 * m + 64, 1, 0:nk]) for m in range(2)],
                                  step * 2 + (c + 1))
                        else:
                            score(U[u], u, c, [(nqT[:, u // 2 - 1, c * P:(c + 1) * P], kT[:, m, 0:nk]) for m in range(2)])

                    def TP(u):
                        c = u % 2
                        if u < 2:
                            probs_T(U[u], u, c + 1, da_ready, step * 2 + (c + 1))
                        else:
                            probs_T(U[u], u, 2 * (c + 1), exp_done, U[u] + 1 + LAG)

                    def PV(u):
                        c = u % 2
                        a = at[0][:, u % 2, :]
                        kcs = range(c + 1)
                        if u < 2:
                            values(U[u], [(B[7][:, 0:P], [(a[:, kc * P:(kc + 1) * P], z[:, kc, bass.ds(g * 256 + (ZV + 128 * j), 128)]) for kc in kcs])])
                        else:
                            if u == 2:
                                evacuated(TC, g)
                            values(U[u], [
                                (B[7][:, 0:64], [(pcT[:, u // 2 - 1, c * P:(c + 1) * P], vc[:, bass.ds(g * 64, 64)])]),
                                (B[7][:, 64:128], [(a[:, kc * P:(kc + 1) * P], z[:, kc, bass.ds(g * 64 + V_SEL, 64)]) for kc in kcs]),
                                (B[7][:, 128:192], [(a[:, (c + 1 + kc) * P:(c + 2 + kc) * P], z[:, kc, bass.ds(g * 64 + V_WIN, 64)]) for kc in kcs])])

                    pe.wait_ge(staged, g * 5 + (1, 4)[j])
                    transposes(T1, [(dqk[:, c, t, :], (2 * t + c) * P) for t in range(2) for c in range(C)], g)
                    pe.wait_ge(staged, g * 5 + (2, 5)[j])
                    transposes(T2, [(nqs[:, c, t * 64:(t + 1) * 64], (2 * t + c) * P) for t in range(2) for c in range(C)], g)
                    if j == 0:
                        pe.wait_ge(staged, g * 5 + 3)
                        for t in range(2):
                            transposes(2 + t, [(kks[:, t, c, :], c * P) for c in range(C)], g)
                    fill(0)
                    evacuated(T1, g)
                    S_(0), S_(1)
                    evacuated(T2, g)
                    if j == 0:
                        evacuated(2, g)
                        evacuated(3, g)
                    bank = tp_begin(CS, g)
                    pe.sem_inc(pe_turns, 1)
                    for c in range(C):
                        for t in range(2):
                            last = nc.tensor.matmul(bank[:, (2 * c + t) * N_CMP:(2 * c + t + 1) * N_CMP],
                                                    nqT[:, t, c * P:(c + 1) * P], kcT[:, bass.ds(g * N_CMP, N_CMP)],
                                                    start=True, stop=True)
                    last.then_inc(tp_ready[CS % 2], 1)
                    fill(1)
                    TP(0), S_(2)
                    fill(2)
                    PV(0), TP(1), S_(3)
                    fill(3)
                    PV(1), TP(2), S_(4)
                    fill(4)
                    pe.wait_ge(cp_ready, step + 1)
                    transposes(TC, [(cs[:, c, t, :], (2 * t + c) * P) for t in range(2) for c in range(C)], g)
                    TP(3), S_(5), PV(2)
                    fill(5)
                    PV(3), TP(4)
                    fill(6)
                    PV(4), TP(5)
                    fill(7)
                    PV(5)

            pe.wait_ge(ev_done, 48 + 1)
            pe.wait_ge(sc_free, 48 + LAG)
            for n in range(4):
                c, hf = n // 2, n % 2
                transposes(G_OT + n, [(z[:, c, NQ + (4 * hf + t) * P:NQ + (4 * hf + t + 1) * P], t * P) for t in range(4)])
            for n in range(4):
                c, hf = n // 2, n % 2
                if n == 0:
                    pe.wait_ge(subln_done, C * DA_H)
                transposes(G_OT + 4 + n, [(z[:, c, ZQ + (4 * hf + t) * P:ZQ + (4 * hf + t + 1) * P], t * P) for t in range(4)])

            def branch_part(i, n):
                if n < 4:
                    part(i + T_BR, i + T_BR, n, orr[:, :, 0:8, :], final=3)
                else:
                    part(i + T_BR, i, n, orr[:, :, 8:16, :], bank=4, first=4)

            def mix_transposes(i):
                for c in range(C):
                    pe.wait_ge(mix_ready, i * 2 + (c + 1))
                    pe.wait_ge(tp_free[c], i + (G_MIX // 2 + 1))
                    for t in range(4):
                        last = nc.tensor.transpose(B[2 + c][:, t * P:(t + 1) * P], stage_a[:, c, t * P:(t + 1) * P], ident[:, :])
                    last.then_inc(tp_ready[c], 1)

            for n in range(PIECES):
                if n in (0, 2):
                    evacuated(G_OT + 6 + n // 2)
                branch_part(0, n)
            with pe.Fori(1, N_BR) as i:
                for n in range(PIECES):
                    if n == MIX_AFTER:
                        mix_transposes(i - 1)
                    branch_part(i, n)
            for n in range(PIECES):
                if n == MIX_AFTER:
                    mix_transposes(N_BR - 1)
                if n == PIECES - KS:
                    for b in range(2):
                        evacuated(G_X2 - 2 + b)
                part(T_WO, T_WO, n, xr)
            with pe.Fori(1, N_WO) as i:
                whole(i + T_WO, xr)

            norm_groups(G_X2, xn2, 2)
            whole(T_XQ, xr, groups=G_X2)
            pe.wait_ge(act_steps, 7)
            for c in range(C):
                transposes(G_QX + c, [(stage_b[:, c, t * P:(t + 1) * P], t * P) for t in range(X_H)])
            for c in range(C):
                evacuated(G_QX + c)
                pe.wait_ge(nacc_free[c], 1 + N_BR)

            def XS(v):
                c, hp = v // 2, v % 2
                score(48 + v, v, c, [(qxT[:, 2 * hp + m, c * P:(c + 1) * P], kxT[:, 2 * hp + m, :]) for m in range(2)])

            def XT(v):
                probs_T(48 + v, v, 4, exp_done, 48 + v + 1 + LAG, 1)

            def XV(v):
                hp, a = v % 2, at[1][:, v % 2, :]
                values(48 + v, [(B[7][:, m * P:(m + 1) * P],
                                 [(a[:, (2 * m + kc) * P:(2 * m + kc + 1) * P], vmem[:, kc, (2 * hp + m) * P:(2 * hp + m + 1) * P]) for kc in range(2)])
                                for m in range(2)])

            XS(0), XS(1), XT(0), XS(2), XT(1), XV(0), XS(3), XT(2), XV(1), XT(3), XV(2), XV(3)
            for c in range(C):
                pe.wait_ge(ev_done, 48 + 2 * c + 2 + 1)
                transposes(G_OX + c, [(ox[:, c, t * P:(t + 1) * P], t * P) for t in range(X_H)])
            for c in range(C):
                evacuated(G_OX + c)
            for n in range(PIECES):
                part(T_XO, T_XO + n // 2, n, oxr, first=n // 2 * 2, final=n // 2 * 2 + 1)

            norm_groups(G_X3, xn3, 3)
            def head_piece(n):
                hh = n // HP
                pe.wait_ge(w_split, T_PQ * PIECES + n + 1 + WR)
                for c in range(C):
                    if n == 0:
                        pe.wait_ge(acc_free[c], A_PQ + 1)
                    for k in range(HK):
                        kk = n % HP * HK + k
                        x_h, x_l = (xr[:, t, kk, c * P:(c + 1) * P] for t in range(2))
                        w_h, w_l = (head_wide(ws[:, n % WR, t, :, :])[:, k, :] for t in range(2))
                        dst = B[4 * hh + c][:, 0:HW]
                        nc.tensor.matmul(dst, x_h, w_h, start=(kk == 0), stop=False)
                        nc.tensor.matmul(dst, x_h, w_l, start=False, stop=False)
                        last = nc.tensor.matmul(dst, x_l, w_h, start=False, stop=(kk == KT - 1))
                    if c == C - 1:
                        last.then_inc(w_used, 1)
                    elif n == PIECES - 1:
                        last.then_inc(acc0_ready, 1)

            def head_transposes(hh):
                pe.wait_ge(act_steps, 8 + hh)
                transposes(G_PQ + 2 * hh, [(stage_b[:, c, hh * HW + t * P:hh * HW + (t + 1) * P], (2 * t + c) * P) for t in range(2) for c in range(C)])

            def head_scores(hh):
                evacuated(G_PQ + 2 * hh)
                pe.wait_ge(tp_free[1], G_PQ // 2 + hh + 1)
                for c in range(C):
                    for half in range(2):
                        last = nc.tensor.matmul(B[3][:, (2 * c + half) * P:(2 * c + half + 1) * P],
                                                qpT[:, 2 * hh + half, c * P:(c + 1) * P], keysT[:, half, :],
                                                start=True, stop=True)
                last.then_inc(tp_ready[1], 1)

            for n in range(HP + 1):
                if n < HP:
                    evacuated(G_X3 + 4 + n)
                head_piece(n)
            head_transposes(0)
            head_piece(HP + 1)
            head_scores(0)
            for n in range(HP + 2, PIECES):
                head_piece(n)
            head_transposes(1)
            head_scores(1)
            with pe.Fori(1, N_PQ) as i:
                whole(i + T_PQ, xr, i + A_PQ)
                for c in range(C):
                    pe.wait_ge(act_steps, i * 2 + (7 + c + 1))
                    pe.wait_ge(tp_free[c], i * 2 + (G_PQ // 2 + 1))
                    for t in range(4):
                        last = nc.tensor.transpose(B[2 + c][:, t * P:(t + 1) * P], stage_b[:, c, t * P:(t + 1) * P], ident[:, :])
                    last.then_inc(tp_ready[c], 1)
                for c in range(C):
                    pe.wait_ge(tp_free[c], i * 2 + (G_PQ // 2 + 2))
                for hh in range(2):
                    for c in range(C):
                        for half in range(2):
                            last = nc.tensor.matmul(B[2 + hh][:, (2 * c + half) * P:(2 * c + half + 1) * P],
                                                    qpT[:, 2 * hh + half, c * P:(c + 1) * P], keysT[:, half, :],
                                                    start=True, stop=True)
                    last.then_inc(tp_ready[hh], 1)

            def v_step(u):
                pe.wait_ge(vacc_free, u + 1)
                for j in range(PK):
                    r = j % RING
                    pe.wait_ge(v_landed[r], u * 64 + 16 * (j // RING + 1))
                    pe.wait_ge(diag_ready, u * 16 + (j + 1))
                    for n in range(4):
                        last = nc.tensor.matmul(B[4 + n], diag[:, r, :], v_ring[:, r, n * NW:(n + 1) * NW],
                                                start=(j == 0), stop=(j == PK - 1))
                    last.then_inc(v_used, 1)

            with pe.Fori(0, UNITS) as i:
                v_step(i)

        @block.scalar
        def _(act):
            A = nc.scalar.activation
            for q in (tp_free[0], tp_free[1], acc_free[0], acc_free[1], at_ready):
                act.sem_inc(q, 1)
            act.sem_inc(exp_done, LAG)
            act.sem_inc(w_split, WR)
            act.sem_inc(w_used, WR)

            smalls = [(raw[0:CMP_LEN, 1, 0:64], cmp_pos[0]), (raw[0:CMP_LEN, 1, 64:128], cmp_pos[0]),
                      (raw[:, 2, :], keys1[0]), (raw[:, 3, :], keys2[0]),
                      (w2[:, 0, :], ck2[0]), (w2[:, 1, :], cv2[0]),
                      (lam4[:, 0, :], lq1[0].partition_broadcast(P)), (lam4[:, 1, :], lk1[0].partition_broadcast(P)),
                      (lam4[:, 2, :], lq2[0].partition_broadcast(P)), (lam4[:, 3, :], lk2[0].partition_broadcast(P)),
                      (subg[:, :], subln_g[0].partition_broadcast(P)),
                      (pos_i[:, 0:1], positions[0, 0:P].rearrange("(p o) -> p o", o=1)),
                      (pos_i[:, 1:2], positions[0, P:S].rearrange("(p o) -> p o", o=1))]
            assert len(smalls) == N_SMALL
            for dst, src in smalls:
                act.dma_start(dst, src).then_inc(small_landed, 16)

            def squares(count, dst, src, junk):
                if count:
                    act.wait_ge(sq_done, count)
                A(junk, src, ACT.Square, accum_out=dst).then_inc(sq_done, 1)

            def squares_h(n, c, last):
                squares(4 + 4 * (n - 2) + 2 * last + c, (ssq_b if last else ssq)[:, 2 * n + c:2 * n + c + 1],
                        h[:, c, D - NW:D] if last else h[:, c, 0:D - NW], square_b[:, 0:NW] if last else square_b[:, 0:D - NW])

            def hi(n, tile, cols=NW):
                q = n + AHEAD
                act.wait_ge(w_landed[q % WR], tile * (16 * PIECES // WR) + 16 * (q // WR + 1))
                act.wait_ge(w_used, tile * PIECES + (q + 1))
                A(ws[:, q % WR, 0, :, 0:cols], wraw[:, q % WR, :, 0:cols], ACT.Copy).then_inc(w_hi, 1)

            def next_cols(n, cols, following):
                return cols if n + AHEAD < PIECES else following

            for c in range(C):
                act.wait_ge(mem_landed[c], 16)
                squares(c, ssq[:, c:c + 1], mn[:, c, :], square_a)
            for n in range(-AHEAD, 0):
                hi(n, 0)

            def evac_hi(n, number, dst):
                act.wait_ge(tp_ready[n % 2], n // 2 + 1)
                A(dst, four(n), ACT.Copy).then_inc(hi_done, 1)

            def four(n):
                return B[2 + n % 2].rearrange("p (t s) -> p t s", t=4)

            for c in range(C):
                for q in range(4):
                    evac_hi(G_MEM + 4 * c + q, H_MEM + 4 * c + q, orr[:, 0, 4 * q:4 * q + 4, c * P:(c + 1) * P])
            act.wait_ge(x_landed, 16)
            for c in range(C):
                squares(2 + c, ssq[:, 2 + c:3 + c], xn[:, c, :], square_a)
            act.wait_ge(angle_ready, 1)
            A(rope[:, 4, :, :], rope[:, 2, :, :], ACT.Sin)
            A(rope[:, 5, :, :], rope[:, 3, :, :], ACT.Sin).then_inc(sin_done, 1)

            def acc_wait(c, tile, acc):
                if c == 0:
                    act.wait_ge(acc0_ready, acc + 1)
                else:
                    act.wait_ge(w_used, tile * PIECES + (PIECES + WR))

            def copy_acc(c, tile, acc, dst):
                acc_wait(c, tile, acc)
                A(dst, B[c], ACT.Copy).then_inc(acc_free[c], 1)

            def evac(n, dst, src, g=None):
                act.wait_ge(tp_ready[n % 2], n // 2 + 1 if g is None else g * (ATT_GROUPS // 2) + (G_ATT // 2 + n // 2 + 1))
                A(dst, src, ACT.Copy).then_inc(tp_free[n % 2], 1)

            for n, dst in enumerate((stage_a, vmem)):
                for k in range(PIECES):
                    hi(k, T_KV + n)
                for c in range(C):
                    copy_acc(c, T_KV + n, T_KV + n, dst[:, c, :])
                if n == 0:
                    for c in range(C):
                        act.wait_ge(acc_free[c], 2)
                        act.sem_inc(act_steps, 1)
            for c in range(C):
                evac(G_MK + c, kxT[:, :, c * P:(c + 1) * P], four(G_MK + c))
            for c in range(C):
                for q in range(4):
                    evac_hi(G_X + 4 * c + q, H_X + 4 * c + q, xr[:, 0, 4 * q:4 * q + 4, c * P:(c + 1) * P])
            def qkv_tile(i):
                for n in range(PIECES):
                    hi(n, i + T_QKV)
                for c in range(C):
                    copy_acc(c, i + T_QKV, i + T_QKV, z[:, c, bass.ds(i * NW, NW)])

            with act.Fori(0, T_CMP + 2 - T_QKV) as i:
                qkv_tile(i)
            for t in range(2):
                for c in range(C):
                    n = G_CMP + 2 * t + c
                    evac(n, xsT[:, t, :, c * P:(c + 1) * P], four(n))
            for last in range(T_CMP + 2 - T_QKV, N_QKV):
                for n in range(PIECES):
                    hi(n, T_QKV + last, next_cols(n, NW, NG_COLS) if last == N_QKV - 1 else NW)
                for c in range(C):
                    copy_acc(c, T_QKV + last, T_QKV + last, z[:, c, last * NW:(last + 1) * NW])
            for n in range(PIECES):
                hi(n, T_NG, next_cols(n, NG_COLS, NW))
            acc_wait(1, T_NG, T_NG)
            A(gnT[:, :], B[0][0:NG_COLS, 0:S], ACT.Tanh, scale=0.5).then_inc(acc_free[0], 1)
            act.sem_inc(acc_free[1], 1)
            act.wait_ge(acc_free[0], T_NG + 2)
            act.sem_inc(act_steps, 1)
            act.wait_ge(lam_in, 1)
            A(lamb[:, 2:4], lamb[:, 0:2], ACT.Exp).then_inc(lam_exp, 1)
            for t in range(2):
                act.wait_ge(hid_ready, t + 1)
                A(hid[:, t, :], B[5 + t][:, 0:60], ACT.Gelu).then_inc(hid_done, 1)
            act.wait_ge(cmp_ready, 1)
            A(kcT[:, :], B[7][0:64, 0:60], ACT.Copy).then_inc(cmp_done, 1)
            A(vc[:, :], B[7][0:N_CMP, 64:320], ACT.Copy).then_inc(cmp_done, 1)

            def exps(U, u, nk, x=0):
                act.wait_ge(nm_ready, U + 1)
                act.wait_ge(pt_ready, U + 1)
                for m in range(2):
                    last = A(Pr[x][:, u % 2, m * nk:(m + 1) * nk], Sc[x][:, u % 2, m * nk:(m + 1) * nk], ACT.Exp,
                             bias=nmx[:, u % 2, m:m + 1], accum_out=sums[:, u, 1 + m:2 + m])
                last.then_inc(exp_done, 1)

            def copy_pt(U, u, nt, x=0):
                act.wait_ge(pt_ready, U + 1 + LAG)
                act.wait_ge(pv_ready, U + 1)
                A(at[x][:, u % 2, 0:nt * P], B[6][:, 0:nt * P], ACT.Copy).then_inc(at_ready, 1)

            with act.Fori(0, N_G) as g:
                for j in range(2):
                    T1, T2, CS, TC = ((0, 1, 4, 5), (6, 7, 8, 9))[j]
                    step = g * 2 + j
                    U = [g * 12 + (6 * j + u) for u in range(6)]
                    act.wait_ge(sc_ready, U[0] + LAG)
                    evac(T1, dT, B[2 + T1 % 2].rearrange("p (t s) -> p t s", t=2), g)
                    evac(T2, nqT, B[2 + T2 % 2][0:64].rearrange("p (t s) -> p t s", t=2), g)
                    if j == 0:
                        for t in range(2):
                            evac(2 + t, kT[:, t, :], B[2 + t][0:64, 0:S], g)
                    nt = [1, 2, 2, 4, 2, 4]
                    nks = [P, 2 * P] * 3
                    tile = step + T_BG
                    exps(U[0], 0, nks[0])
                    exps(U[1], 1, nks[1])
                    hi(0, tile)
                    copy_pt(U[0], 0, nt[0])
                    hi(1, tile)
                    exps(U[2], 2, nks[2])
                    copy_pt(U[1], 1, nt[1])
                    act.wait_ge(cm_ready, step + 1)
                    A(cs[:, :, :, :].rearrange("p c t n -> p (c t n)"), cs[:, :, :, :].rearrange("p c t n -> p (c t n)"), ACT.Exp).then_inc(cexp_done, 1)
                    hi(2, tile)
                    exps(U[3], 3, nks[3])
                    copy_pt(U[2], 2, nt[2])
                    hi(3, tile)
                    evac(TC, pcT, B[2 + TC % 2][0:N_CMP].rearrange("p (t s) -> p t s", t=2), g)
                    exps(U[4], 4, nks[4])
                    copy_pt(U[3], 3, nt[3])
                    hi(4, tile)
                    exps(U[5], 5, nks[5])
                    copy_pt(U[4], 4, nt[4])
                    hi(5, tile)
                    copy_pt(U[5], 5, nt[5])
                    hi(6, tile)
                    hi(7, tile)
                    for c in range(C):
                        acc_wait(c, step + T_BG, step + T_BG)
                        A(gates[:, c, bass.ds(g * 1024 + 512 * j, NW)], B[c], ACT.Tanh, scale=0.5).then_inc(acc_free[c], 1)

            for n in range(8):
                c, hf, first = (n % 4) // 2, n % 2, 8 if n < 4 else 0
                evac_hi(G_OT + n, H_OT + n, orr[:, 0, first + 4 * hf:first + 4 * hf + 4, c * P:(c + 1) * P])

            def mix_hi(i):
                for c in range(C):
                    act.wait_ge(tp_ready[c], i + (G_MIX // 2 + 1))
                    A(xr[:, 0, bass.ds(i * 4, 4), c * P:(c + 1) * P], four(c), ACT.Copy).then_inc(hi_done, 1)

            for n in range(PIECES):
                hi(n, T_BR)
            with act.Fori(1, N_BR) as i:
                for n in range(PIECES):
                    if n == MIX_AFTER:
                        mix_hi(i - 1)
                    hi(n, i + T_BR)
            for n in range(PIECES):
                if n == MIX_AFTER:
                    mix_hi(N_BR - 1)
                hi(n, T_WO)
            with act.Fori(1, N_WO - 1) as i:
                for n in range(PIECES):
                    hi(n, i + T_WO)
            for n in range(PIECES):
                hi(n, T_WO + N_WO - 1)
                if n in (3, 5):
                    act.wait_ge(h_done, 2 * N_WO - 2)
                    squares_h(2, n // 4, False)
            for c in range(C):
                act.wait_ge(h_done, 2 * N_WO - 1 + c)
                squares_h(2, c, True)
            for c in range(C):
                for q in range(4):
                    evac_hi(G_X2 + 4 * c + q, H_X2 + 4 * c + q, xr[:, 0, 4 * q:4 * q + 4, c * P:(c + 1) * P])
            for n in range(PIECES):
                hi(n, T_XQ)
            for c in range(C):
                copy_acc(c, T_XQ, T_XQ, stage_b[:, c, :])
            for c in range(C):
                act.wait_ge(acc_free[c], T_XQ + 2)
                act.sem_inc(act_steps, 2)
            for c in range(C):
                evac(G_QX + c, qxT[:, :, c * P:(c + 1) * P], four(c))
            for kind, v in (("e", 0), ("e", 1), ("t", 0), ("e", 2), ("t", 1), ("e", 3), ("t", 2), ("t", 3)):
                if kind == "e":
                    exps(48 + v, v, 2 * P, 1)
                else:
                    copy_pt(48 + v, v, 4, 1)
            for c in range(C):
                evac_hi(G_OX + c, H_OX + c, oxr[:, 0, :, c * P:(c + 1) * P])
            for n in range(PIECES):
                hi(n, T_XO)
                if n in (5, 6):
                    act.wait_ge(h_done, 2 * N_WO + 2 * X_H - 2)
                    squares_h(3, n - 5, False)
            for c in range(C):
                act.wait_ge(h_done, 2 * N_WO + 2 * X_H - 1 + c)
                squares_h(3, c, True)
            for c in range(C):
                for q in range(4):
                    evac_hi(G_X3 + 4 * c + q, H_X3 + 4 * c + q, xr[:, 0, 4 * q:4 * q + 4, c * P:(c + 1) * P])

            def query_tile(i, pieces=PIECES):
                for n in range(pieces):
                    hi(n, i + T_PQ)
                for c in range(C):
                    if c == 0:
                        act.wait_ge(acc0_ready, i + (A_PQ + 1))
                    else:
                        act.wait_ge(w_used, i * PIECES + ((T_PQ + 1) * PIECES + WR))
                    A(stage_b[:, c, :], B[c], ACT.Copy).then_inc(acc_free[c], 1)
                    act.wait_ge(acc_free[c], i + (A_PQ + 2))
                    act.sem_inc(act_steps, 1)
                for c in range(C):
                    act.wait_ge(tp_ready[c], i * 2 + (G_PQ // 2 + 1))
                    A(qpT[:, :, c * P:(c + 1) * P], four(c), ACT.Copy).then_inc(tp_free[c], 1)
                for hh in range(2):
                    act.wait_ge(tp_ready[hh], i * 2 + (G_PQ // 2 + 2))
                    A(scores[:, bass.ds(i * 1024 + 512 * hh, 512)] if not isinstance(i, int) else scores[:, i * 1024 + 512 * hh:i * 1024 + 512 * hh + 512],
                      B[2 + hh], ACT.Copy).then_inc(tp_free[hh], 1)

            def route_softmax(u):
                act.wait_ge(route_scores, u + 1)
                A(ex[:, :], sc16[:, :], ACT.Exp, bias=nsc[:, :], accum_out=exs[:, 0:1]).then_inc(route_exp, 1)

            def head_queries(hh):
                act.wait_ge(w_used, T_PQ * PIECES + (hh + 1) * HP + WR)
                for c in range(C):
                    last = A(stage_b[:, c, hh * HW:(hh + 1) * HW], B[4 * hh + c][:, 0:HW], ACT.Copy)
                    if hh == 1:
                        last.then_inc(acc_free[c], 1)
                    elif c == 1:
                        last.then_inc(act_steps, 1)
                if hh == 1:
                    for c in range(C):
                        act.wait_ge(acc_free[c], A_PQ + 2)
                    act.sem_inc(act_steps, 1)

            def head_evac(hh):
                evac(G_PQ + 2 * hh, qpT[:, 2 * hh:2 * hh + 2, :], B[2].rearrange("p (t s) -> p t s", t=2))

            def head_scores(hh):
                evac(G_PQ + 2 * hh + 1, scores[:, 2 * hh * HW:2 * (hh + 1) * HW], B[3])

            for n in range(HP + 1):
                hi(n, T_PQ)
            head_queries(0)
            head_evac(0)
            hi(HP + 1, T_PQ)
            head_scores(0)
            for n in range(HP + 2, PIECES):
                hi(n, T_PQ)
            head_queries(1)
            head_evac(1)
            head_scores(1)
            route_softmax(0)
            route_softmax(1)
            with act.Fori(1, N_PQ - 1) as i:
                query_tile(i)
            query_tile(N_PQ - 1, PIECES - AHEAD)

            def gelu(par, u):
                act.wait_ge(dot_done, u * 16 + (16 + RING))
                A(act_u[:, :], dots[:, par, :], ACT.Gelu).then_inc(gelu_done, 1)

            def diagonals(par, u, js):
                for j in js:
                    act.wait_ge(v_used, u * 16 + (j + 1))
                    A(diag[:, j % RING, :], ident[:, :], ACT.Copy, scale=ga[:, par, j:j + 1]).then_inc(diag_ready, 1)

            gelu(0, 0)
            with act.Fori(0, PH - 1) as i:
                for par, u in ((0, i * 2), (1, i * 2 + 1)):
                    act.wait_ge(ga_ready, u + 1)
                    diagonals(par, u, range(0, 5))
                    route_softmax(u + 2)
                    diagonals(par, u, range(5, PK))
                    gelu(1 - par, u + 1)
            act.wait_ge(ga_ready, UNITS - 1)
            diagonals(0, UNITS - 2, range(PK))
            gelu(1, UNITS - 1)
            act.wait_ge(ga_ready, UNITS)
            diagonals(1, UNITS - 1, range(0, 4))
            act.wait_ge(vacc_free, UNITS)
            squares(12, ssq[:, 8:9], h[:, 0, :], u_ring[:, 0, :])
            diagonals(1, UNITS - 1, range(4, PK))
            act.wait_ge(vacc_free, UNITS + 1)
            squares(13, ssq[:, 10:11], h[:, 1, :], u_ring[:, 0, :])

        @block.vector
        def _(dve):
            V = nc.vector
            link = Chain(dve, dve_steps)
            dve.sem_inc(sc_free, LAG)
            dve.sem_inc(sc_ready, LAG)
            dve.sem_inc(pt_ready, LAG)
            dve.sem_inc(pv_ready, LAG)
            dve.sem_inc(ev_done, 1)
            dve.sem_inc(vacc_free, 1)
            dve.sem_inc(nacc_free[0], 1)
            dve.sem_inc(nacc_free[1], 1)
            dve.sem_inc(dot_done, RING)
            dve.sem_inc(v_used, RING)

            for i in range(ROPE_HALF):
                V.memset(inv[:, i:i + 1], ROPE_INV[i])
            link(V.memset(lamb[:, :], 0.0))

            def mean_square(n, c, count):
                dve.wait_ge(sq_done, count)
                k = 2 * n + c
                V.tensor_scalar(msq[:, k:k + 1], ssq[:, k:k + 1], 1.0 / D, EPS, ALU.mult, ALU.add).then_inc(ms_done, 1)

            def mean_squares_h(n):
                first = 4 + 4 * (n - 2)
                dve.wait_ge(sq_done, first + 2)
                link(V.tensor_scalar(msq[:, 2 * n:2 * n + 2], ssq[:, 2 * n:2 * n + 2], 1.0 / D, EPS, ALU.mult, ALU.add))
                for c in range(C):
                    dve.wait_ge(sq_done, first + 3 + c)
                    k = 2 * n + c
                    V.scalar_tensor_tensor(out=msq[:, k:k + 1], in0=ssq_b[:, k:k + 1], scalar=1.0 / D, in1=msq[:, k:k + 1],
                                           op0=ALU.mult, op1=ALU.add).then_inc(ms_done, 1)

            def scale_rows(n, src, dst, gain):
                for c in range(C):
                    dve.wait_ge(rstd_done, norm_count(n, c))
                    for q in range(4):
                        cols = slice(q * NW, (q + 1) * NW)
                        V.scalar_tensor_tensor(out=dst[:, c, cols], in0=src[:, c, cols], scalar=rstd[:, 2 * n + c:2 * n + c + 1],
                                               in1=gain[:, cols], op0=ALU.mult, op1=ALU.mult).then_inc(xn_done, 1)

            def lo(n, tile, cols=NW):
                q = n + AHEAD
                dve.wait_ge(w_hi, tile * PIECES + (q + 1))
                V.tensor_tensor(ws[:, q % WR, 1, :, 0:cols], wraw[:, q % WR, :, 0:cols], ws[:, q % WR, 0, :, 0:cols].bitcast(F32),
                                ALU.subtract).then_inc(w_split, 1)

            def next_cols(n, cols, following):
                return cols if n + AHEAD < PIECES else following

            def evac_lo(n, number, pair):
                dve.wait_ge(hi_done, number + 1)
                V.tensor_tensor(pair[1], B[2 + n % 2].rearrange("p (t s) -> p t s", t=4), pair[0].bitcast(F32),
                                ALU.subtract).then_inc(tp_free[n % 2], 1)

            def norm_lo(base, number, dst):
                for c in range(C):
                    for q in range(4):
                        evac_lo(base + 4 * c + q, number + 4 * c + q, [dst[:, t, 4 * q:4 * q + 4, c * P:(c + 1) * P] for t in range(2)])

            for c in range(C):
                mean_square(0, c, 1 + c)
            dve.wait_ge(gmem_landed, 16)
            scale_rows(0, mn, mn, gmem)
            for n in range(-AHEAD, 0):
                lo(n, 0)
            norm_lo(G_MEM, H_MEM, orr)
            dve.wait_ge(tp_ready[0], G_POS // 2 + 1)
            V.tensor_copy(posT[:, :], B[2][:, 0:CMP_LEN]).then_inc(tp_free[0], 1)
            dve.wait_ge(tp_ready[1], G_KEYS // 2 + 1)
            V.tensor_copy(keysT[:, :, :].rearrange("p t n -> p (t n)"), B[3][:, 0:2 * P]).then_inc(tp_free[1], 1)
            for c in range(C):
                mean_square(1, c, 3 + c)
            dve.wait_ge(gmix_landed, 16)
            scale_rows(1, xn, xn, gmix)

            dve.wait_ge(small_landed, 16 * N_SMALL)
            link(V.tensor_copy(rope[:, 0, :, 0], pos_i[:, :]))
            link(V.tensor_tensor(rope[:, 1, :, :], rope[:, 0, :, 0:1].broadcast_to([P, C, ROPE_HALF]),
                                 inv[:, :].unsqueeze(1).broadcast_to([P, C, ROPE_HALF]), ALU.mult))
            link(V.tensor_scalar(rope[:, 0, :, :], rope[:, 1, :, :], 1.0 / (2 * math.pi), MAGIC, ALU.mult, ALU.add))
            link(V.tensor_scalar(rope[:, 0, :, :], rope[:, 0, :, :], -MAGIC, None, ALU.add))
            for part_ in (TWO_PI_A, TWO_PI_B, TWO_PI_C):
                link(V.scalar_tensor_tensor(out=rope[:, 1, :, :], in0=rope[:, 0, :, :], scalar=-part_, in1=rope[:, 1, :, :],
                                            op0=ALU.mult, op1=ALU.add))
            link(V.tensor_scalar(rope[:, 2, :, :], rope[:, 1, :, :], PI_IN, -PI_IN, ALU.min, ALU.max))
            link(V.tensor_scalar(rope[:, 0, :, :], rope[:, 2, :, :], -1.0, None, ALU.mult))
            link(V.tensor_tensor(rope[:, 1, :, :], rope[:, 0, :, :], rope[:, 2, :, :], ALU.min))
            V.tensor_scalar(rope[:, 3, :, :], rope[:, 1, :, :], math.pi / 2, None, ALU.add).then_inc(angle_ready, 1)
            link(V.tensor_tensor(lamp[:, 0:64], lam4[:, 0, :], lam4[:, 1, :], ALU.mult))
            link(V.tensor_tensor(lamp[:, 64:128], lam4[:, 2, :], lam4[:, 3, :], ALU.mult))
            V.reduce_sum(lamb[:, 0:2], lamp.rearrange("p (t d) -> p t d", t=2), axis=AX.X).then_inc(lam_in, 1)
            link(V.tensor_scalar(subg[:, :], subg[:, :], 1.0 - LAMBDA_INIT, None, ALU.mult))
            for t in range(2):
                for n in range(PIECES):
                    lo(n, T_KV + t)
            norm_lo(G_X, H_X, xr)

            sin, cos = rope[:, 4, :, :], rope[:, 5, :, :]

            def rotate(c, first, n, room):
                v = z[:, c, first:first + 64 * n].rearrange("p (n d) -> p n d", d=64)
                x1, x2 = v[:, :, 0:ROPE_HALF], v[:, :, ROPE_HALF:2 * ROPE_HALF]
                t = [room[:, k, 0:8 * n].rearrange("p (n d) -> p n d", d=8) for k in range(4)]
                cc = cos[:, c, :].unsqueeze(1).broadcast_to([P, n, ROPE_HALF])
                ss = sin[:, c, :].unsqueeze(1).broadcast_to([P, n, ROPE_HALF])
                V.tensor_tensor(t[0], x1, cc, ALU.mult)
                V.tensor_tensor(t[1], x2, ss, ALU.mult)
                V.tensor_tensor(t[2], x2, cc, ALU.mult)
                link(V.tensor_tensor(t[3], x1, ss, ALU.mult))
                V.tensor_tensor(x1, t[0], t[1], ALU.subtract)
                link(V.tensor_tensor(x2, t[2], t[3], ALU.add))

            dve.wait_ge(sin_done, 1)
            done = 0
            for tiles, parts, room in ((4, [(ZQ, 32)], rot), (8, [(NQ, 16)], rot), (9, [(K_CMP, 4)], rot), (11, [(K_SEL, 4), (K_WIN, 4)], rot_b)):
                with dve.Fori(0, tiles - done - (tiles == N_QKV)) as i:
                    for n in range(PIECES):
                        lo(n, i + (T_QKV + done))
                if tiles == N_QKV:
                    for n in range(PIECES):
                        lo(n, T_QKV + N_QKV - 1, next_cols(n, NW, NG_COLS))
                        if n in (1, 4):
                            t = n // 4
                            for c in range(C):
                                dve.wait_ge(tp_free[c], (G_CMP + 2 * t + c) // 2 + 2)
                            for odd in range(2):
                                rows = slice(64 * odd, 64 * odd + 64)
                                for lh in range(2):
                                    seen = xsT[rows, t, :, 16 * lh:16 * lh + 240].rearrange("p g (n l o) -> p o l g n", o=2, l=8)[:, odd]
                                    place = posT[rows, 16 * lh:16 * lh + 16].rearrange("p (l o) -> p o l", o=2)[:, odd]
                                    last = V.tensor_tensor(blk[rows, t, 8 * lh:8 * lh + 8, :, :], seen,
                                                           place.unsqueeze(2).unsqueeze(3).broadcast_to([64, 8, N_G, N_CMP]), ALU.add)
                            last.then_inc(blk_ready, 1)
                done = tiles
                for c in range(C):
                    dve.wait_ge(acc_free[c], T_QKV + tiles + 1)
                for c in range(C):
                    for first, n in parts:
                        rotate(c, first, n, room)
                if K_CMP // NW < tiles:
                    dve.sem_inc(rope_done, 1)
                if tiles == N_QKV:
                    for n in range(PIECES):
                        lo(n, T_NG, next_cols(n, NG_COLS, NW))
            for c in range(C):
                dve.wait_ge(tp_ready[c], G_NG // 2 + 1)
                V.tensor_scalar(gn[:, c, :], B[2 + c][:, 0:NG_COLS], 0.5, 0.5, ALU.mult, ALU.add).then_inc(tp_free[c], 1)
            for c in range(C):
                dve.wait_ge(tp_free[c], G_NG // 2 + 2)
            dve.wait_ge(lam_exp, 1)
            link(V.tensor_tensor(lamb[:, 4:5], lamb[:, 3:4], lamb[:, 2:3], ALU.subtract))
            link(V.tensor_scalar(lamb[:, 5:6], lamb[:, 4:5], -LAMBDA_INIT, None, ALU.add))
            neg_lam = lamb[:, 5:6]

            def softmax_in(U, u, nk, mask, x=0):
                dve.wait_ge(sc_ready, U + 1 + LAG)
                dve.wait_ge(exp_done, U + 1)
                b = u % 2
                sv = Sc[x][:, b, 0:2 * nk].rearrange("p (m n) -> p m n", m=2)
                pv = B[4 + b][:, 0:2 * nk].rearrange("p (m n) -> p m n", m=2)
                if mask is None:
                    V.tensor_scalar(sv, pv, X_SCALE, None, ALU.mult).then_inc(sc_free, 1)
                else:
                    V.scalar_tensor_tensor(out=sv, in0=pv, scalar=ATT_SCALE, in1=mask.unsqueeze(1).broadcast_to([P, 2, nk]),
                                           op0=ALU.mult, op1=ALU.add).then_inc(sc_free, 1)
                dve.wait_ge(sc_free, U + 1 + LAG)
                link(V.reduce_max(mx[:, b, :], sv, axis=AX.X))
                V.tensor_scalar(nmx[:, b, :], mx[:, b, :], -1.0, None, ALU.mult).then_inc(nm_ready, 1)

            with dve.Fori(0, N_G) as g:
                link.loop(g, ATT_STEPS)
                for j in range(2):
                    CS, TC = ((4, 5), (8, 9))[j]
                    step = g * 2 + j
                    U = [g * 12 + (6 * j + u) for u in range(6)]

                    def SM(u):
                        c = u % 2
                        softmax_in(U[u], u, (c + 1) * P, causal[:, P:2 * P] if c == 0 else causal[:, :])

                    def difference(u):
                        dve.wait_ge(exp_done, U[u] + 1 + LAG)
                        nk = (u + 1) * P
                        p0, p1 = Pr[0][:, u, 0:nk], Pr[0][:, u, nk:2 * nk]
                        link(V.reciprocal(rec[:, 0:2], sums[:, u, 1:3]))
                        V.tensor_scalar(coef[:, 0:1], rec[:, 1:2], neg_lam, None, ALU.mult)
                        link(V.tensor_scalar(p0, p0, rec[:, 0:1], None, ALU.mult))
                        V.scalar_tensor_tensor(out=p0, in0=p1, scalar=coef[:, 0:1], in1=p0, op0=ALU.mult, op1=ALU.add).then_inc(da_ready, 1)

                    def EV(u):
                        c = u % 2
                        dve.wait_ge(pv_ready, U[u] + 1 + LAG)
                        if u < 2:
                            out_u = z[:, c, bass.ds(g * 256 + (ZQ + 128 * j), 128)]
                            V.tensor_copy(out_u, B[7][:, 0:P]).then_inc(ev_done, 1)
                            dve.wait_ge(ev_done, U[u] + 2)
                            V.scalar_tensor_tensor(out=tmp3[:, 0:P], in0=out_u, scalar=1.0, in1=out_u, op0=ALU.mult, op1=ALU.mult,
                                                   accum_out=ms2[:, 0, c:c + 1]).then_inc(subln_sq, 1)
                            if c == 1:
                                dve.wait_ge(subln_sq, step * 2 + 2)
                                V.tensor_scalar(ms2[:, 1, :], ms2[:, 0, :], 1.0 / DA_DV, EPS, ALU.mult, ALU.add).then_inc(subln_ms, 1)
                            return
                        t = u // 2 - 1
                        link(V.tensor_copy(sums[:, u, 0:1], csum[:, 2 * c + t:2 * c + t + 1]))
                        link(V.reciprocal(rec[:, 2:5], sums[:, u, 0:3]))
                        link(V.tensor_tensor(coef[:, 1:4], rec[:, 2:5], gn[:, c, bass.ds(g * 12 + (6 * j + 3 * t), 3)], ALU.mult))
                        tv = tmp3[:, :].rearrange("p (b d) -> p b d", b=3)
                        link(V.tensor_tensor(tv, B[7][:, 0:3 * N_DK].rearrange("p (b d) -> p b d", b=3),
                                             coef[:, 1:4].unsqueeze(2).broadcast_to([P, 3, N_DK]), ALU.mult))
                        V.reduce_sum(z[:, c, bass.ds(g * 256 + (NQ + 128 * j + 64 * t), 64)],
                                     tmp3[:, :].rearrange("p (b d) -> p d b", b=3), axis=AX.X).then_inc(ev_done, 1)

                    def head_norm():
                        dve.wait_ge(subln_rstd, step + 1)
                        for c in range(C):
                            out_u = z[:, c, bass.ds(g * 256 + (ZQ + 128 * j), 128)]
                            V.scalar_tensor_tensor(out=out_u, in0=out_u, scalar=ms2[:, 2, c:c + 1], in1=subg[:, :],
                                                   op0=ALU.mult, op1=ALU.mult).then_inc(subln_done, 1)

                    def compressed_in():
                        dve.wait_ge(tp_ready[CS % 2], g * 5 + (G_ATT // 2 + CS // 2 + 1))
                        dve.wait_ge(tp_ready[1], g * 5 + (G_ATT // 2 + (0, 3)[j]))
                        for c in range(C):
                            last = V.scalar_tensor_tensor(out=cs[:, c, :, :], in0=B[2 + CS % 2][:, 30 * c:30 * c + 30].rearrange("p (t n) -> p t n", t=2),
                                                          scalar=ATT_SCALE, in1=cm_add[:, c, :].unsqueeze(1).broadcast_to([P, 2, N_CMP]),
                                                          op0=ALU.mult, op1=ALU.add)
                        last.then_inc(tp_free[CS % 2], 1)
                        dve.wait_ge(tp_free[CS % 2], g * 5 + (G_ATT // 2 + CS // 2 + 2))
                        flat = cs[:, :, :, :].rearrange("p c t n -> p (c t) n")
                        link(V.reduce_max(cmx[:, :], flat, axis=AX.X))
                        V.tensor_tensor(flat, flat, cmx[:, :].unsqueeze(2).broadcast_to([P, 4, N_CMP]), ALU.subtract).then_inc(cm_ready, 1)

                    def compressed_out():
                        dve.wait_ge(cexp_done, step + 1)
                        flat = cs[:, :, :, :].rearrange("p c t n -> p (c t) n")
                        link(V.reduce_sum(csum[:, :], flat, axis=AX.X))
                        for c in range(C):
                            last = V.tensor_tensor(cs[:, c, :, :], cs[:, c, :, :], cm_mul[:, c, :].unsqueeze(1).broadcast_to([P, 2, N_CMP]), ALU.mult)
                        last.then_inc(cp_ready, 1)

                    tile = step + T_BG
                    SM(0), SM(1), difference(0), difference(1), lo(0, tile), SM(2), lo(1, tile)
                    EV(0), compressed_in(), SM(3), lo(2, tile), EV(1), compressed_out(), SM(4), lo(3, tile)
                    SM(5), EV(2), lo(4, tile), EV(3), lo(5, tile), head_norm(), EV(4), lo(6, tile), EV(5), lo(7, tile)
                link.end(N_G)

            for n in range(8):
                c, hf, first = (n % 4) // 2, n % 2, 8 if n < 4 else 0
                evac_lo(G_OT + n, H_OT + n, [orr[:, t, first + 4 * hf:first + 4 * hf + 4, c * P:(c + 1) * P] for t in range(2)])

            def branch_tile(i):
                for c in range(C):
                    for n in range(2 * c, 2 * c + 2):
                        if n == MIX_AFTER and not isinstance(i, int):
                            mix_lo(i - 1)
                        lo(n, i + T_BR)
                for c in range(C):
                    if c == 0:
                        dve.wait_ge(acc0_ready, i + (T_BR + 1))
                    else:
                        dve.wait_ge(w_used, i * PIECES + (T_BR * PIECES + 4 + WR))
                    dve.wait_ge(tp_ready[c], i + G_MIX // 2)
                    V.scalar_tensor_tensor(out=stage_a[:, c, :], in0=gates[:, c, bass.ds(i * NW, NW)], scalar=1.0, in1=B[c],
                                           op0=ALU.add, op1=ALU.mult).then_inc(acc_free[c], 1)
                    lo(4 + c, i + T_BR)
                for n in range(6, PIECES):
                    lo(n, i + T_BR)
                for c in range(C):
                    if c == 0:
                        dve.wait_ge(nacc0_ready, i + 1)
                    else:
                        dve.wait_ge(w_used, i * PIECES + ((T_BR + 1) * PIECES + WR))
                        dve.wait_ge(mix_ready, i * 2 + 1)
                    V.scalar_tensor_tensor(out=half_mix, in0=gates[:, c, bass.ds(i * NW + D, NW)], scalar=1.0, in1=B[4 + c],
                                           op0=ALU.add, op1=ALU.mult).then_inc(nacc_free[c], 1)
                    dve.wait_ge(nacc_free[c], i + 2)
                    dve.wait_ge(acc_free[c], i + (T_BR + 2))
                    V.tensor_tensor(stage_a[:, c, :], stage_a[:, c, :], half_mix, ALU.add).then_inc(mix_ready, 1)

            def mix_lo(i):
                for c in range(C):
                    dve.wait_ge(hi_done, i * 2 + (H_MIX + c + 1))
                    V.tensor_tensor(xr[:, 1, bass.ds(i * 4, 4), c * P:(c + 1) * P], B[2 + c].rearrange("p (t s) -> p t s", t=4),
                                    xr[:, 0, bass.ds(i * 4, 4), c * P:(c + 1) * P].bitcast(F32), ALU.subtract).then_inc(tp_free[c], 1)

            def residual(i):
                for c in range(C):
                    if c == 0:
                        dve.wait_ge(acc0_ready, i + (T_WO + 1))
                    else:
                        dve.wait_ge(w_used, i * PIECES + ((T_WO + 1) * PIECES + WR))
                    hv = h[:, c, bass.ds(i * NW, NW)]
                    V.scalar_tensor_tensor(out=hv, in0=B[c], scalar=0.5, in1=hv, op0=ALU.mult, op1=ALU.add).then_inc(acc_free[c], 1)
                    dve.wait_ge(acc_free[c], i + (T_WO + 2))
                    dve.sem_inc(h_done, 1)

            branch_tile(0)
            with dve.Fori(1, N_BR) as i:
                branch_tile(i)
            for n in range(PIECES):
                if n == MIX_AFTER:
                    mix_lo(N_BR - 1)
                lo(n, T_WO)
            dve.wait_ge(h_landed, 16)
            residual(0)
            with dve.Fori(1, N_WO) as i:
                for n in range(PIECES):
                    lo(n, i + T_WO)
                residual(i)
            mean_squares_h(2)
            dve.wait_ge(gx_landed, 16)
            scale_rows(2, h, xn2, gx)
            norm_lo(G_X2, H_X2, xr)
            for n in range(PIECES):
                lo(n, T_XQ)

            def XEV(v):
                c, hp = v // 2, v % 2
                dve.wait_ge(pv_ready, 48 + v + 1 + LAG)
                link(V.reciprocal(rec[:, 0:2], sums[:, v, 1:3]))
                V.tensor_tensor(ox[:, c, 256 * hp:256 * hp + 256].rearrange("p (m d) -> p m d", m=2), B[7][:, 0:256].rearrange("p (m d) -> p m d", m=2),
                                rec[:, 0:2].unsqueeze(2).broadcast_to([P, 2, P]), ALU.mult).then_inc(ev_done, 1)

            for kind, v in (("s", 0), ("s", 1), ("s", 2), ("e", 0), ("s", 3), ("e", 1), ("e", 2), ("e", 3)):
                if kind == "s":
                    softmax_in(48 + v, v, 2 * P, None, 1)
                else:
                    XEV(v)
            for c in range(C):
                evac_lo(G_OX + c, H_OX + c, [oxr[:, t, :, c * P:(c + 1) * P] for t in range(2)])
            for n in range(X_H):
                lo(2 * n, T_XO)
                lo(2 * n + 1, T_XO)
                for c in range(C):
                    if c == 0:
                        dve.wait_ge(acc0_ready, T_XO + n + 1)
                    else:
                        dve.wait_ge(w_used, T_XO * PIECES + 2 * n + 2 + WR)
                    hv = h[:, c, n * NW:(n + 1) * NW]
                    V.tensor_tensor(hv, B[c], hv, ALU.add).then_inc(acc_free[c], 1)
                    dve.wait_ge(acc_free[c], T_XO + n + 2)
                    dve.sem_inc(h_done, 1)
            mean_squares_h(3)
            dve.wait_ge(grow_landed, 16)
            scale_rows(3, h, xn3, grow)
            norm_lo(G_X3, H_X3, xr)
            for n in range(HP + 1):
                lo(n, T_PQ)

            def top16(src, scratch, vals, ids):
                dve.sem_inc(dve_turns, 1)
                link(V.max(vals[:, 0:8], src))
                dve.sem_inc(dve_turns, 1)
                V.max_index(ids[:, 0:8], vals[:, 0:8], src)
                link(V.match_replace(scratch, vals[:, 0:8], src, -3.0e38))
                dve.sem_inc(dve_turns, 1)
                link(V.max(vals[:, 8:16], scratch))
                dve.sem_inc(dve_turns, 1)
                link(V.max_index(ids[:, 8:16], vals[:, 8:16], scratch))

            def route(u, src, par):
                link(V.tensor_copy(wk[:, :, :].rearrange("p t n -> p (t n)"), src))
                for t in range(2):
                    top16(wk[:, t, :], wk2[:, t * P:(t + 1) * P], top[:, t, :], topi[:, t, :])
                V.tensor_copy(topf[:, :, :], topi[:, :, :])
                link(V.tensor_tensor(cand[:, :, :], top[:, 0, :].unsqueeze(2).broadcast_to([P, PK, PK]),
                                     top[:, 1, :].unsqueeze(1).broadcast_to([P, PK, PK]), ALU.add))
                if not (isinstance(u, int) and u == 0):
                    dve.wait_ge(route_exp, u)
                top16(cand[:, :, :].rearrange("p a b -> p (a b)"), wk2[:, :], sc16, ci)
                V.tensor_scalar(nsc[:, :], sc16[:, 0:1], -1.0, None, ALU.mult).then_inc(route_scores, 1)
                V.tensor_scalar(ab[:, 0, :], ci[:, :], 4, None, ALU.logical_shift_right)
                link(V.tensor_scalar(ab[:, 1, :], ci[:, :], PK - 1, None, ALU.bitwise_and))
                link(V.tensor_copy(abf[:, :, :], ab[:, :, :]))
                for t in range(2):
                    last = V.tensor_tensor(onehot[:, t, :, :], abf[:, t, :].unsqueeze(2).broadcast_to([P, PK, PK]),
                                           iota16[:, :].unsqueeze(1).broadcast_to([P, PK, PK]), ALU.is_equal)
                link(last)
                for t in range(2):
                    last = V.tensor_tensor(onehot[:, t, :, :], onehot[:, t, :, :],
                                           topf[:, t, :].unsqueeze(1).broadcast_to([P, PK, PK]), ALU.mult)
                link(last)
                link(V.reduce_sum(e12[:, :, :].rearrange("p t k -> p (t k)"), onehot[:, :, :, :].rearrange("p t k a -> p (t k) a"), axis=AX.X))
                if not (isinstance(u, int) and u < 2):
                    dve.wait_ge(idx_v_ready, u - 1)
                V.scalar_tensor_tensor(out=idx_u[par][:, :], in0=e12[:, 0, :], scalar=float(NKEYS), in1=e12[:, 1, :],
                                       op0=ALU.mult, op1=ALU.add).then_inc(idx_ready, 1)

            def route_weights(u, par):
                dve.wait_ge(route_exp, u + 1)
                link(V.reciprocal(exs[:, 1:2], exs[:, 0:1]))
                link(V.tensor_scalar(gw[:, par, :], ex[:, :], exs[:, 1:2], None, ALU.mult))

            def dot(u, par, j):
                r = j % RING
                dve.wait_ge(u_landed[r], u * 64 + 16 * (j // RING + 1))
                dve.wait_ge(dot_done, u * 16 + (j + RING))
                V.scalar_tensor_tensor(out=product, in0=u_ring[:, r, :], scalar=1.0, in1=xn3[:, par, :], op0=ALU.mult, op1=ALU.mult,
                                       accum_out=dots[:, par, j:j + 1]).then_inc(dot_done, 1)

            def weigh(u, par):
                dve.wait_ge(gelu_done, u + 1)
                V.tensor_tensor(ga[:, par, :], act_u[:, :], gw[:, par, :], ALU.mult).then_inc(ga_ready, 1)

            def add_out(u, par):
                dve.wait_ge(v_used, u * 16 + (16 + RING))
                V.tensor_tensor(h[:, par, :], vacc, h[:, par, :], ALU.add).then_inc(vacc_free, 1)

            dve.wait_ge(tp_free[1], G_PQ // 2 + 2)
            route(0, scores[:, 0:256], 0)
            for n in range(HP + 1, PIECES):
                lo(n, T_PQ)
            route_weights(0, 0)
            route(1, scores[:, 256:512], 1)
            route_weights(1, 1)
            for n in range(3):
                lo(n, T_PQ + 1)
            pieces = [(T_PQ + 1 + n // PIECES, n % PIECES) for n in range(3, 3 * PIECES - AHEAD)]
            for j in range(PK):
                dot(0, 0, j)
                for tile, n in pieces[2 * j:2 * j + 2]:
                    lo(n, tile)
            weigh(0, 0)
            for hh in range(2):
                dve.wait_ge(tp_free[hh], (G_PQ + 14) // 2 + 2)

            def step(u, par, add, route_next):
                if add:
                    add_out(u - 2, par)
                for j in range(PK):
                    dot(u, par, j)
                    if route_next and j == 3:
                        route(u + 1, scores[:, bass.ds(u * 256 + 256, 256)], 1 - par)
                    if route_next and j == 8:
                        route_weights(u + 1, 1 - par)
                weigh(u, par)

            for par, u in ((1, 1),):
                for j in range(PK):
                    dot(u, par, j)
                    if j == 3:
                        route(2, scores[:, 512:768], 0)
                    if j == 8:
                        route_weights(2, 0)
                weigh(u, par)
            with dve.Fori(0, PH - 2) as i:
                link.loop(i, 2 * ROUTE_STEPS)
                step(i * 2 + 2, 0, True, True)
                step(i * 2 + 3, 1, True, True)
                link.end(PH - 2)
            add_out(UNITS - 4, 0)
            for j in range(PK):
                dot(UNITS - 2, 0, j)
                if j == 3:
                    route(UNITS - 1, scores[:, (UNITS - 1) * 256:UNITS * 256], 1)
                if j == 8:
                    route_weights(UNITS - 1, 1)
            weigh(UNITS - 2, 0)
            add_out(UNITS - 3, 1)
            for j in range(PK):
                dot(UNITS - 1, 1, j)
            weigh(UNITS - 1, 1)

            dve.wait_ge(gfin_landed, 16)
            for c in range(C):
                add_out(UNITS - 2 + c, c)
                n = 4 + c
                mean_square(n, 0, 13 + c)
                dve.wait_ge(rstd_done, norm_count(n, 0))
                V.scalar_tensor_tensor(out=xn3[:, c, :], in0=h[:, c, :], scalar=rstd[:, 2 * n:2 * n + 1], in1=gfin[:, :],
                                       op0=ALU.mult, op1=ALU.mult).then_inc(y_done, 1)


_INS = ['x', 'mem', 'positions', 'norm_mix_g', 'w_in', 'da_lambda_q1', 'da_lambda_k1', 'da_lambda_q2', 'da_lambda_k2',
        'da_subln_g', 'nsa_cmp_pos', 'nsa_cmpk_w1', 'nsa_cmpk_w2', 'nsa_cmpv_w1', 'nsa_cmpv_w2', 'w_branch_da',
        'w_branch_nsa', 'w_out', 'norm_x_g', 'norm_mem_g', 'w_xq', 'w_xkv', 'w_xo', 'norm_ffn_g', 'peer_wq',
        'peer_keys1', 'peer_keys2', 'peer_u', 'peer_v', 'norm_final_g']


def kernel(**inputs):
    import numpy as _np
    import concourse.bacc as _bacc
    from concourse import mybir as _mybir
    from concourse.bass_utils import run_bass_kernel_spmd as _run

    nc = _bacc.Bacc("TRN2", target_bir_lowering=False, num_devices=1)
    arrays, args = {}, []
    for name in _INS:
        a = _np.ascontiguousarray(inputs[name])
        arrays[f"in_{name}_dram"] = a
        args.append(nc.dram_tensor(f"in_{name}_dram", a.shape, _mybir.dt.from_np(a.dtype), kind="ExternalInput").ap())
    args.append(nc.dram_tensor("out_dram", (1, S, D), _mybir.dt.float32, kind="ExternalOutput").ap())
    block_program(nc, *args)
    r = _run(nc, [arrays], core_ids=[0])
    return r.results[0]["out_dram"]
```
